# Optimizing a Trainium2 kernel written in Bass

```python
import jax, jax.numpy as jnp
from jax import lax
import numpy as np

D_MODEL = 1024
BATCH = 1
SEQ = 1024
DEPTH = 1

N_BRANCH = 4
BW = 256
EPS = 1e-6
RWKV_HEADS = 4
RWKV_HEAD = BW // RWKV_HEADS
RWKV_DECAY_LORA = 64
RWKV_A_LORA = 64
RWKV_SHIFT_WIDTH = 3 * BW + RWKV_DECAY_LORA + RWKV_A_LORA
RWKV_LN_EPS = 64e-5
HGRN_HEADS = 4
HGRN_EXPAND = BW // HGRN_HEADS
HGRN_VHEAD = BW // HGRN_HEADS
HGRN_CHUNK = 64
RET_HEADS = 4
RET_VHEAD = BW // RET_HEADS
RET_QKHEAD = RET_VHEAD // 2
RET_QK = RET_HEADS * RET_QKHEAD
RET_CHUNK = 128
ROPE_BASE = 10000.0
LRU_BLOCKS = 4
LRU_BLOCK = BW // LRU_BLOCKS
CONV_WIDTH = 4
LRU_C = 8.0

IN_SPLITS = (
    BW, BW, BW, RWKV_DECAY_LORA, RWKV_A_LORA, BW,
    BW, BW, BW, BW,
    RET_QK, RET_QK, BW, BW,
    BW, BW,
    N_BRANCH * D_MODEL,
)
IN_WIDTH = sum(IN_SPLITS)

kernel_name = "hybrid_rwkv7_hgrn2_retnet_rglru_trunk"

def _rmsnorm(x, g):
    xf = x.astype(jnp.float32)
    y = xf * lax.rsqrt(jnp.mean(xf * xf, axis=-1, keepdims=True) + EPS)
    return y * g.astype(jnp.float32)

def _head_rms(o):
    return o * lax.rsqrt(jnp.mean(o * o, axis=-1, keepdims=True) + EPS)

def _token_shift(u):
    return jnp.pad(u, ((0, 0), (1, 0), (0, 0)))[:, :-1]

def _rwkv7(r, k, v, w_lo, a_lo, mu, w0, w2, a0, a2, k_k, k_a, r_k, ln_g, ln_b):
    B, T, _ = r.shape
    H, N = RWKV_HEADS, RWKV_HEAD
    feats = jnp.concatenate([r, k, v, w_lo, a_lo], -1).astype(jnp.float32)
    feats = feats + mu * (_token_shift(feats) - feats)
    r, k, v, w_lo, a_lo = jnp.split(feats, [BW, 2 * BW, 3 * BW, 3 * BW + RWKV_DECAY_LORA], -1)
    w = -jax.nn.softplus(-(w0 + jnp.tanh(w_lo) @ w2)) - 0.5
    decay = jnp.exp(-jnp.exp(w))
    a = jax.nn.sigmoid(a0 + a_lo @ a2)
    kk = k * k_k
    k = k * (1.0 + (a - 1.0) * k_a)
    hd = lambda t: t.reshape(B, T, H, N)
    r, k, v, kk, a, decay = hd(r), hd(k), hd(v), hd(kk), hd(a), hd(decay)
    kk = kk / jnp.maximum(jnp.sqrt(jnp.sum(kk * kk, -1, keepdims=True)), 1e-12)

    def step(S, inp):
        r_t, w_t, k_t, v_t, kk_t, a_t = inp
        sa = jnp.einsum('bhvk,bhk->bhv', S, -kk_t)
        S = (S * w_t[:, :, None, :] + sa[..., None] * (kk_t * a_t)[:, :, None, :]
             + v_t[..., None] * k_t[:, :, None, :])
        return S, jnp.einsum('bhvk,bhk->bhv', S, r_t)

    tm = lambda t: jnp.moveaxis(t, 1, 0)
    S0 = jnp.zeros((B, H, N, N), jnp.float32)
    _, y = lax.scan(step, S0, (tm(r), tm(decay), tm(k), tm(v), tm(kk), tm(a)))
    y = jnp.moveaxis(y, 0, 1)
    mean = jnp.mean(y, -1, keepdims=True)
    var = jnp.mean(jnp.square(y - mean), -1, keepdims=True)
    y = ((y - mean) * lax.rsqrt(var + RWKV_LN_EPS)).reshape(B, T, BW) * ln_g + ln_b
    bonus = jnp.sum(r * k * r_k.reshape(H, N), -1, keepdims=True) * v
    return y + bonus.reshape(B, T, BW)

def _hgrn2(q, f_pre, i, lb, norm_g):
    B, T, _ = q.shape
    H, K, V, C = HGRN_HEADS, HGRN_EXPAND, HGRN_VHEAD, HGRN_CHUNK
    n = T // C
    f_pre = f_pre.astype(jnp.float32)
    lb = lb.astype(jnp.float32)
    k = (1.0 - lb) * jax.nn.sigmoid(-f_pre)
    log_f = jnp.log1p(-k)
    chunks = lambda t, d: t.astype(jnp.float32).reshape(B, n, C, H, d).transpose(1, 0, 3, 2, 4)
    causal = jnp.tril(jnp.ones((C, C), bool))[:, :, None]

    def step(S, inp):
        q_c, k_c, v_c, lf_c = inp
        b = jnp.cumsum(lf_c, axis=2)
        rel = jnp.where(causal, b[:, :, :, None, :] - b[:, :, None, :, :], -jnp.inf)
        scores = jnp.sum(q_c[:, :, :, None, :] * k_c[:, :, None, :, :] * jnp.exp(rel), -1)
        o = (jnp.einsum('bhts,bhsv->bhtv', scores, v_c)
             + jnp.einsum('bhtk,bhkv->bhtv', q_c * jnp.exp(b), S))
        b_end = b[:, :, -1:, :]
        S = (jnp.exp(b_end)[:, :, 0, :, None] * S
             + jnp.einsum('bhsk,bhsv->bhkv', k_c * jnp.exp(b_end - b), v_c))
        return S, o

    S0 = jnp.zeros((B, H, K, V), jnp.float32)
    _, o = lax.scan(step, S0, (chunks(q, K), chunks(k, K), chunks(i, V), chunks(log_f, K)))
    o = o.transpose(1, 0, 3, 2, 4).reshape(B, T, H, V)
    return _head_rms(o).reshape(B, T, BW) * norm_g

def _rope(t, cos, sin):
    t1, t2 = jnp.split(t, 2, -1)
    return jnp.concatenate([t1 * cos - t2 * sin, t1 * sin + t2 * cos], -1)

def _retention(q, k, v, norm_g):
    B, T, _ = q.shape
    H, Dk, Dv, C = RET_HEADS, RET_QKHEAD, RET_VHEAD, RET_CHUNK
    n = T // C
    pos = jnp.arange(T, dtype=jnp.float32)
    inv_freq = 1.0 / (ROPE_BASE ** jnp.linspace(0.0, 1.0, Dk // 2, dtype=jnp.float32))
    ang = pos[:, None] * inv_freq[None, :]
    cos, sin = jnp.cos(ang)[None, :, None, :], jnp.sin(ang)[None, :, None, :]
    q = _rope(q.astype(jnp.float32).reshape(B, T, H, Dk), cos, sin)
    k = _rope(k.astype(jnp.float32).reshape(B, T, H, Dk), cos, sin) * (Dk ** -0.5)
    v = v.astype(jnp.float32).reshape(B, T, H, Dv)
    chunk = lambda t: t.reshape(B, n, C, H, t.shape[-1]).transpose(0, 3, 1, 2, 4)
    q, k, v = chunk(q), chunk(k), chunk(v)
    log_gamma = jnp.log1p(-jnp.exp2(-5.0 - jnp.arange(H, dtype=jnp.float32)))
    idx = jnp.arange(C, dtype=jnp.float32)
    rel = idx[:, None] - idx[None, :]
    decay = jnp.where(rel >= 0, jnp.exp(log_gamma[:, None, None] * jnp.maximum(rel, 0.0)), 0.0)
    scores = jnp.einsum('bhntd,bhnsd->bhnts', q, k) * decay[:, None]
    o = jnp.einsum('bhnts,bhnse->bhnte', scores, v)
    zeta = jnp.exp(log_gamma[:, None] * (C - 1 - idx))
    xi = jnp.exp(log_gamma[:, None] * (idx + 1.0))
    kv = jnp.einsum('bhnsd,hs,bhnse->bhnde', k, zeta, v)
    gamma_c = jnp.exp(log_gamma * C)[None, :, None, None]

    def step(R, kv_n):
        return gamma_c * R + kv_n, R

    _, R_prev = lax.scan(step, jnp.zeros((B, H, Dk, Dv), jnp.float32), jnp.moveaxis(kv, 2, 0))
    R_prev = jnp.moveaxis(R_prev, 0, 2)
    o = o + jnp.einsum('bhntd,bhnde->bhnte', q * xi[:, None, :, None], R_prev)
    o = o.transpose(0, 2, 3, 1, 4).reshape(B, T, H, Dv)
    return _head_rms(o).reshape(B, T, BW) * norm_g

def _rglru(x, conv_w, conv_b, w_a, b_a, w_x, b_x, lam):
    B, T, _ = x.shape
    x = x.astype(jnp.float32)
    xp = jnp.pad(x, ((0, 0), (CONV_WIDTH - 1, 0), (0, 0)))
    y = conv_b + sum(conv_w[j] * xp[:, j:j + T] for j in range(CONV_WIDTH))
    yb = y.reshape(B, T, LRU_BLOCKS, LRU_BLOCK)
    r = jax.nn.sigmoid(jnp.einsum('btgi,gij->btgj', yb, w_a).reshape(B, T, BW) + b_a)
    i = jax.nn.sigmoid(jnp.einsum('btgi,gij->btgj', yb, w_x).reshape(B, T, BW) + b_x)
    log_a = -LRU_C * r * jax.nn.softplus(-lam)
    mult = jnp.sqrt(-jnp.expm1(2.0 * log_a))
    mult = jnp.where(jnp.arange(T)[None, :, None] == 0, 1.0, mult)
    u = mult * (i * y)

    def combine(left, right):
        a1, b1 = left
        a2, b2 = right
        return a1 * a2, a2 * b1 + b2

    _, h = lax.associative_scan(combine, (jnp.exp(log_a), u), axis=1)
    return h

def setup_inputs(seed: int = 0) -> dict:
    key = jax.random.key(seed)
    ks = jax.random.split(key, 29)
    f32 = jnp.float32
    nrm = lambda i, shape, s: s * jax.random.normal(ks[i], shape, f32)
    a_c = jax.random.uniform(ks[25], (DEPTH, BW), f32, 0.9, 0.999)
    a_base = a_c ** (1.0 / LRU_C)
    return {
        "x": nrm(0, (BATCH, SEQ, D_MODEL), 1.0),
        "c": nrm(1, (BATCH, D_MODEL), 1.0),
        "norm_g": 1.0 + nrm(2, (DEPTH, D_MODEL), 0.05),
        "w_mod": nrm(3, (DEPTH, D_MODEL, 3 * D_MODEL), 0.5 * D_MODEL ** -0.5),
        "b_mod": nrm(4, (DEPTH, 3 * D_MODEL), 0.02),
        "w_in": nrm(5, (DEPTH, D_MODEL, IN_WIDTH), D_MODEL ** -0.5),
        "rwkv_mu": jax.random.uniform(ks[6], (DEPTH, RWKV_SHIFT_WIDTH), f32),
        "rwkv_w0": jax.random.uniform(ks[7], (DEPTH, BW), f32, -6.0, -1.0),
        "rwkv_w2": nrm(8, (DEPTH, RWKV_DECAY_LORA, BW), 0.1 * RWKV_DECAY_LORA ** -0.5),
        "rwkv_a0": nrm(9, (DEPTH, BW), 0.1),
        "rwkv_a2": nrm(10, (DEPTH, RWKV_A_LORA, BW), 0.5 * RWKV_A_LORA ** -0.5),
        "rwkv_kk": 0.85 + nrm(11, (DEPTH, BW), 0.05),
        "rwkv_ka": 1.0 + nrm(12, (DEPTH, BW), 0.05),
        "rwkv_rk": nrm(13, (DEPTH, BW), 0.1),
        "rwkv_ln_g": 1.0 + nrm(14, (DEPTH, BW), 0.05),
        "rwkv_ln_b": nrm(15, (DEPTH, BW), 0.02),
        "hgrn_lb": nrm(16, (DEPTH, BW), 1.0),
        "hgrn_norm_g": 1.0 + nrm(17, (DEPTH, BW), 0.05),
        "ret_norm_g": 1.0 + nrm(18, (DEPTH, BW), 0.05),
        "lru_conv_w": nrm(19, (DEPTH, CONV_WIDTH, BW), CONV_WIDTH ** -0.5),
        "lru_conv_b": nrm(20, (DEPTH, BW), 0.02),
        "lru_wa": nrm(21, (DEPTH, LRU_BLOCKS, LRU_BLOCK, LRU_BLOCK), LRU_BLOCK ** -0.5),
        "lru_ba": nrm(22, (DEPTH, BW), 0.02),
        "lru_wx": nrm(23, (DEPTH, LRU_BLOCKS, LRU_BLOCK, LRU_BLOCK), LRU_BLOCK ** -0.5),
        "lru_bx": nrm(24, (DEPTH, BW), 0.02),
        "lru_lam": jnp.log(a_base) - jnp.log1p(-a_base),
        "w_branch": nrm(26, (DEPTH, N_BRANCH, BW, D_MODEL), BW ** -0.5),
        "w_out": nrm(27, (DEPTH, D_MODEL, D_MODEL), D_MODEL ** -0.5),
        "final_g": 1.0 + nrm(28, (D_MODEL,), 0.05),
    }

def reference(x, c, norm_g, w_mod, b_mod, w_in, rwkv_mu, rwkv_w0, rwkv_w2, rwkv_a0, rwkv_a2,
              rwkv_kk, rwkv_ka, rwkv_rk, rwkv_ln_g, rwkv_ln_b, hgrn_lb, hgrn_norm_g, ret_norm_g,
              lru_conv_w, lru_conv_b, lru_wa, lru_ba, lru_wx, lru_bx, lru_lam, w_branch, w_out,
              final_g):
    B, T, _ = x.shape
    split_at = np.cumsum(IN_SPLITS)[:-1].tolist()
    lb_p = jax.nn.softmax(hgrn_lb.astype(jnp.float32), axis=0)
    lb_all = jnp.cumsum(lb_p, axis=0) - lb_p[0]
    cond = jax.nn.silu(c.astype(jnp.float32))
    h = x
    for l in range(DEPTH):
        mod = cond @ w_mod[l] + b_mod[l]
        shift, scale, gate = jnp.split(mod, 3, -1)
        hn = _rmsnorm(h, norm_g[l]) * (1.0 + scale[:, None, :]) + shift[:, None, :]
        u = hn @ w_in[l]
        (ar, ak, av, aw, aa, ag, bq, bf, bi, bg, cq, ck, cv, cg, dx, dg, mg) = jnp.split(u, split_at, -1)
        ya = _rwkv7(ar, ak, av, aw, aa, rwkv_mu[l], rwkv_w0[l], rwkv_w2[l], rwkv_a0[l], rwkv_a2[l],
                    rwkv_kk[l], rwkv_ka[l], rwkv_rk[l], rwkv_ln_g[l], rwkv_ln_b[l]) * jax.nn.silu(ag)
        yb = _hgrn2(bq, bf, bi, lb_all[l], hgrn_norm_g[l]) * jax.nn.silu(bg)
        yc = _retention(cq, ck, cv, ret_norm_g[l]) * jax.nn.silu(cg)
        yd = _rglru(dx, lru_conv_w[l], lru_conv_b[l], lru_wa[l], lru_ba[l], lru_wx[l], lru_bx[l],
                    lru_lam[l]) * jax.nn.silu(dg)
        merge_gates = jax.nn.sigmoid(mg.astype(jnp.float32).reshape(B, T, N_BRANCH, D_MODEL))
        branches = (ya, yb, yc, yd)
        merged = sum(merge_gates[:, :, b_i] * (branches[b_i] @ w_branch[l, b_i]) for b_i in range(N_BRANCH))
        h = h + gate[:, None, :] * (merged @ w_out[l])
    return _rmsnorm(h, final_g)


_drawn_inputs = setup_inputs


def setup_inputs(seed=0):
    import zlib

    import numpy as np

    out = dict(_drawn_inputs(seed))
    spreads = {}
    factors = {'rwkv_w2': 8.0,
     'rwkv_a0': 8.0,
     'rwkv_kk': 5.899,
     'rwkv_ka': 6.637,
     'rwkv_ln_g': 8.0,
     'rwkv_ln_b': 51.039,
     'hgrn_norm_g': 8.0,
     'ret_norm_g': 8.0,
     'lru_conv_b': 5.307,
     'lru_ba': 200.0,
     'lru_bx': 64.0,
     'lru_wa': 4.205}
    for name, (base, spread) in spreads.items():
        noise = np.random.default_rng([zlib.crc32(name.encode()), seed]).standard_normal(out[name].shape)
        drawn = base * np.exp(spread * noise) if base else spread * noise
        out[name] = __import__('jax').numpy.asarray(drawn.astype(out[name].dtype))
    for name, factor in factors.items():
        out[name] = (out[name] * factor).astype(out[name].dtype)
    return out
```

```python
from contextlib import ExitStack

import numpy as np

import concourse.bass as bass
from concourse import mybir

F32 = mybir.dt.float32
F32R = mybir.dt.float32r
ACT = mybir.ActivationFunctionType
ALU = mybir.AluOpType

P = 128
T = 1024
D = 1024
BW = 256
KT = D // P
HALF = 512
NT = T // P
C = 64
RET_SCALE = 32 ** -0.5
EPS = 1e-6
RWKV_LN_EPS = 64e-5
LEVELS = (64, 32, 16, 8, 4, 2, 1)
NLOW = 6

AR, AK, AV, AWA, AG = 0, 2, 4, 6, 7
BQ, BF, BI, BG = 9, 11, 13, 15
CQ, CK, CV, CG = 17, 18, 19, 21
DX, DG = 23, 25
MG = 27

PARAMS = (("c", 8), ("norm_g", 8), ("b_mod", 16), ("mu", 7), ("w0", 2), ("a0", 2), ("kk", 2), ("ka", 2),
          ("rk", 2), ("ln_g", 2), ("ln_b", 2), ("lb", 2), ("hgrn_g", 2), ("ret_g", 2), ("conv_w", 8),
          ("conv_b", 2), ("ba", 2), ("bx", 2), ("lam", 2), ("eps", 1), ("ln_eps", 1), ("gamma_c", 1))
TABLES = (("ident", 128), ("blockones", 128), ("perm", 128), ("xi", 128), ("zeta", 128), ("decay", 512),
          ("low", NLOW * 32), ("m_rwkv", 128), ("lev", 6 * 64), ("up1", 64), ("eye64", 64), ("ret_head", 4))


def columns(fields):
    at, n = {}, 0
    for name, k in fields:
        at[name] = (n, n + k)
        n += k
    return at, n


PCOL, NPAR = columns(PARAMS)
TCOL, NTAB = columns(TABLES)

PROJ = {DX: 0, DX + 1: 1, DG: 2, DG + 1: 3, AR: 8, AR + 1: 9, AK: 10, AK + 1: 11, AV: 12, AV + 1: 13, AWA: 16,
        CQ: 20, CK: 21, CG: 6, CG + 1: 7, BQ: 0, BQ + 1: 1, BF: 4, BF + 1: 5, AG: 2, AG + 1: 3, BG: 10, BG + 1: 11}
TIME_MAJOR = {CV: (22, 0), CV + 1: (22, 1), BI: (8, 0), BI + 1: (8, 1)}
GATED = (DG, DG + 1, CG, CG + 1, AG, AG + 1, BG, BG + 1)
BULK_D = [DX, DX + 1, DG, DG + 1]
BULK_A = [AR, AR + 1, AK, AK + 1, AV, AV + 1, AWA]
BULK_C = [CQ, CK, CV, CV + 1, CG, CG + 1]
BULK_B1 = [BQ, BQ + 1, AG, AG + 1]
BULK_B2 = [BF, BF + 1, BI, BI + 1, BG, BG + 1]
MERGE_BRANCHES = (3, 2, 0, 1)
MERGE_TILES = [(b, m) for b in MERGE_BRANCHES for m in range(D // P)]
BULK = (BULK_D + BULK_A + BULK_C + [MG + 8 * b + m for b, m in MERGE_TILES[:16]] + BULK_B1 + BULK_B2
        + [MG + 8 * b + m for b, m in MERGE_TILES[16:]])
BULK_AT = {ct: n for n, ct in enumerate(BULK)}
Y_SLOT = {3: 2, 2: 6, 0: 2, 1: 10}
MERGED = 16


def build(nc, ins, out_d):
    x_d, w_mod_d, w_in_d, w_branch_d, w_out_d = (ins[n] for n in ("x", "w_mod", "w_in", "w_branch", "w_out"))
    with ExitStack() as ctx:
        def sb(name, shape, dt=F32):
            return ctx.enter_context(nc.sbuf_tensor(name, shape, dt))

        def sem(name):
            return ctx.enter_context(nc.semaphore(name))

        counts = {}

        def after(s):
            counts[s.name] = counts.get(s.name, 0) + 1
            return counts[s.name]

        s_params_landed = sem("params_landed")
        s_x_landed = [sem(f"x_landed{i}") for i in range(8)]
        s_mod_acc = sem("mod_acc")
        s_w_mod_landed = [sem(f"w_mod_landed{i}") for i in range(4)]
        s_w_lo_ready = sem("w_lo_ready")
        s_w_landed = [sem(f"w_landed{i}") for i in range(2)]
        s_br_done = sem("br_done")
        s_w_branch_landed = [sem(f"w_branch_landed{i}") for i in range(2)]
        s_lru_w_zero = sem("lru_w_zero")
        s_w_first_used = sem("w_first_used")
        s_proj_done = sem("proj_done")
        s_w_hi_ready = sem("w_hi_ready")
        s_merged = sem("merged")
        s_evac = sem("evac")
        s_hn_lo_ready = sem("hn_lo_ready")
        s_y_ready = [sem(f"y_ready{i}") for i in range(4)]
        s_tables_landed = sem("tables_landed")
        s_hn_f32_ready = sem("hn_f32_ready")
        s_xn_ready = sem("xn_ready")
        s_xn_turned = sem("xn_turned")
        s_ones_ready = sem("ones_ready")
        s_mod_done = sem("mod_done")
        s_mod_read = sem("mod_read")
        s_lru_w_landed = sem("lru_w_landed")
        s_conv_ready = sem("conv_ready")
        s_gates_ready = sem("gates_ready")
        s_gates_done = sem("gates_done")
        s_a_tanh = sem("a_tanh")
        s_squares = sem("squares")
        s_head_sums = sem("head_sums")
        s_roots = sem("roots")
        s_rot_done = sem("rot_done")
        s_kz_ready = sem("kz_ready")
        s_kz_turned = sem("kz_turned")
        s_kz_tm_ready = sem("kz_tm_ready")
        s_ret_r_ready = sem("ret_r_ready")
        s_ret_q_ready = sem("ret_q_ready")
        s_ret_p_ready = sem("ret_p_ready")
        s_ret_s_done = sem("ret_s_done")
        s_ret_kv_done = sem("ret_kv_done")
        s_ret_o_ready = sem("ret_o_ready")
        s_ret_o_done = sem("ret_o_done")
        s_a_y_ready = sem("a_y_ready")
        s_a_g_ready = sem("a_g_ready")
        s_a_ends_ready = sem("a_ends_ready")
        s_a_tm1_done = sem("a_tm1_done")
        s_a_tm2_done = sem("a_tm2_done")
        s_a_m_done = sem("a_m_done")
        s_a_tm_ready = sem("a_tm_ready")
        s_a_a_done = sem("a_a_done")
        s_a_x_ready = sem("a_x_ready")
        s_a_v_done = sem("a_v_done")
        s_a_v_ready = sem("a_v_ready")
        s_a_dx_done = sem("a_dx_done")
        s_a_p_done = sem("a_p_done")
        s_a_w_done = sem("a_w_done")
        s_a_p_ready = sem("a_p_ready")
        s_a_u_done = sem("a_u_done")
        s_a_w_ready = sem("a_w_ready")
        s_a_u_ready = sem("a_u_ready")
        s_a_g_zero = sem("a_g_zero")
        s_a_wg_done = sem("a_wg_done")
        s_a_y_done = sem("a_y_done")
        s_a_sa_ready = sem("a_sa_ready")
        s_a_gnew_done = sem("a_gnew_done")
        s_a_mean_done = sem("a_mean_done")
        s_a_rk_ready = sem("a_rk_ready")
        s_a_bonus_done = sem("a_bonus_done")
        s_a_bonus_read = sem("a_bonus_read")
        s_b_z_ready = sem("b_z_ready")
        s_b_o_ready = sem("b_o_ready")
        s_b_s_ready = sem("b_s_ready")
        s_b_p_ready = sem("b_p_ready")
        s_b_scores_done = sem("b_scores_done")
        s_b_o_done = sem("b_o_done")
        s_b_ke_ready = sem("b_ke_ready")
        s_b_snew_done = sem("b_snew_done")
        s_gate_acc = sem("gate_acc")
        s_ones2_ready = sem("ones2_ready")
        s_gate_done = sem("gate_done")
        s_gate_read = sem("gate_read")
        s_out_read = sem("out_read")
        s_out_done = sem("out_done")
        s_cond_ready = sem("cond_ready")
        s_x_squares = sem("x_squares")
        s_x_rms = sem("x_rms")
        s_rs_ready = sem("rs_ready")
        s_hn_hi_ready = sem("hn_hi_ready")
        s_lam_abs = sem("lam_abs")
        s_lam_exp = sem("lam_exp")
        s_lb_shifted = sem("lb_shifted")
        s_lb_exp = sem("lb_exp")
        s_lru_y8_ready = sem("lru_y8_ready")
        s_lru_t = sem("lru_t")
        s_lru_a = sem("lru_a")
        s_lru_q_ready = sem("lru_q_ready")
        s_lru_mult = sem("lru_mult")
        s_a_mixed = sem("a_mixed")
        s_a_kk_ready = sem("a_kk_ready")
        s_a_b_ready = sem("a_b_ready")
        s_cos_landed = sem("cos_landed")
        s_a_norms_used = sem("a_norms_used")
        s_sin_landed = sem("sin_landed")
        s_c_out_ready = sem("c_out_ready")
        s_a_e_ready = sem("a_e_ready")
        s_a_y_part = sem("a_y_part")
        s_a_centred = sem("a_centred")
        s_lb_ready = sem("lb_ready")
        s_b_k_sig = sem("b_k_sig")
        s_b_f_sig = sem("b_f_sig")
        s_b_f_ready = sem("b_f_ready")
        s_b_lnf = sem("b_lnf")
        s_reset128_landed = sem("reset128_landed")
        s_b_d_ready = sem("b_d_ready")
        s_b_e_ready = sem("b_e_ready")
        s_b_gate_landed = sem("b_gate_landed")
        s_final_g_landed = sem("final_g_landed")
        s_xr_landed = [sem(f"xr_landed{i}") for i in range(4)]
        s_h_ready = sem("h_ready")
        s_h_squares = sem("h_squares")
        s_h_rms = sem("h_rms")
        s_out_ready = sem("out_ready")
        s_stored = [sem(f"stored{i}") for i in range(4)]
        s_vector_step = sem("vector_step")

        hn_hi = sb("hn_hi", [P, KT, T], F32R)
        hn_lo = sb("hn_lo", [P, KT, T], F32R)
        w_raw = [sb(f"w_raw{i}", [P, 4, P]) for i in range(2)]
        w_hi = [sb(f"w_hi{i}", [P, 4, P], F32R) for i in range(2)]
        w_lo = [sb(f"w_lo{i}", [P, 4, P], F32R) for i in range(2)]
        w_branch = [sb(f"w_branch{i}", [P, 2, P]) for i in range(2)]
        slots = sb("slots", [P, 24, T])
        stage = sb("stage", [P, 5508])
        par = sb("par", [P, NPAR])
        tab = sb("tab", [P, NTAB])
        wa2 = sb("wa2", [P, BW])
        lru_w = sb("lru_w", [P, 4, P])
        small = sb("small", [P, 80])
        bank = [ctx.enter_context(nc.psum_tensor(f"bank{i}", [P, HALF], F32)) for i in range(8)]

        def slot(i):
            return slots[:, i, :]

        def pair(i):
            return slots[:, i:i + 2, :]

        def pc(name, j=0):
            a = PCOL[name][0] + j
            return par[:, a:a + 1]

        def pcs(name):
            a, b = PCOL[name]
            return par[:, a:b]

        def tb(name):
            a, b = TCOL[name]
            return tab[:, a:b]

        def st(a, n):
            return stage[:, a:a + n]

        ident, blockones = tb("ident"), tb("blockones")
        cond, ssq, rs, gs, sh = (small[:, a:a + 8] for a in (0, 8, 16, 24, 32))
        sp8, omlb, lball = small[:, 40:42], small[:, 42:44], small[:, 44:46]
        sc1, sc2, sc3, sc4 = (small[:, a:a + 2] for a in (46, 48, 50, 52))
        ssq2, rs2 = small[:, 54:62], small[:, 62:70]
        ones = small[:, 70:71]
        e_last = small[:, 72:74]

        acc = slots[:, 0:2, :].rearrange("p a t -> p (a t)")
        w_mod = [slots[:, 2 + 2 * i:4 + 2 * i, :].rearrange("p a t -> p (a t)") for i in range(4)]
        hn_f32 = [st(HALF * i, HALF) for i in range(4)]
        scratch = st(2048, T)
        reset = st(3200, T)
        kz_tm = st(0, T).rearrange("p (i c) -> p i c", c=P)
        rope_tmp = [st(1024, HALF), st(1536, HALF)]
        ret_p = [st(2048 + 512 * i, 512).rearrange("p (h t) -> p h t", h=4) for i in range(2)]
        ret_r = st(4224, 256)
        ret_q = [st(4480, 512).rearrange("p (h t) -> p h t", h=4), st(3072, 512).rearrange("p (h t) -> p h t", h=4)]
        ret_kv = st(3584, 256)
        Ep = st(0, 260).rearrange("p (g t) -> p g t", t=65)
        a_r = st(260, 512).rearrange("p (a g t) -> p g a t", a=2, t=C)
        b_hat = st(772, 256).rearrange("p (g t) -> p g t", t=C)
        k_hat = st(1028, 256).rearrange("p (g t) -> p g t", t=C)
        b_end = st(1284, 256).rearrange("p (g t) -> p g t", t=C)
        k_end = st(1540, 256).rearrange("p (g t) -> p g t", t=C)
        tm1 = st(1796, 512)
        tm2 = st(2308, 512)
        m_all = st(2820, 1024).rearrange("p (o a j t) -> p o a j t", o=2, a=2, j=2)
        Em = st(2820, 256).rearrange("p (g t) -> p g t", t=C)

        def m13(h):
            return m_all[:, h % 2, 0, h // 2, :]

        def m24(h):
            return m_all[:, h % 2, 1, h // 2, :]
        xx = st(3844, 512).rearrange("p (a h t) -> p a h t", a=2, h=4)
        G = st(4356, 128)
        v_lev = b_hat.rearrange("p g t -> p (g t)").rearrange("p (h t) -> p h t", h=4)
        w_t = k_hat.rearrange("p g t -> p (g t)")
        p_sb = b_end.rearrange("p g t -> p (g t)")
        u_sb = k_end.rearrange("p g t -> p (g t)")
        sig = [st(4484 + 512 * n, 512) for n in range(2)]
        dz = st(0, 9 * 256).rearrange("p (l j t) -> p l j t", l=9, j=2)
        ke_tm = st(2304, 256)
        h_diag = st(2560, 128).rearrange("p (h t) -> p h t", h=4)
        h_p = st(2688, 512).rearrange("p (h t) -> p h t", h=4)
        h_prod = st(3200, 384).rearrange("p (j l t) -> p j l t", j=2, l=NLOW)
        h_s = st(3584, 128)
        h_qe = st(3712, 256).rearrange("p (j t) -> p j t", j=2)
        final_g = st(0, T)
        fin_tmp = st(1024, T)
        OUT_W = (12, 13, 14, 15, 8, 9, 0, 1)
        XR = (4, 5, 6, 7)

        block = ctx.enter_context(nc.Block())

        @block.sync
        def _(sp):
            sp.dma_start(par[:, :], ins["params"]).then_inc(s_params_landed, 16)
            for i in range(NT):
                sp.dma_start(slot(MERGED + i), x_d[0, i * P:(i + 1) * P, :]).then_inc(s_x_landed[i], 16)
            for k in range(KT):
                if k >= 4:
                    sp.wait_ge(s_mod_acc, k - 3)
                sp.dma_start(w_mod[k % 4], w_mod_d[0, k * P:(k + 1) * P, 0:2 * D]).then_inc(
                    s_w_mod_landed[k % 4], 16)
            merge = 0
            for bi, ct in enumerate(BULK):
                for p in range(2):
                    if bi >= 1:
                        sp.wait_ge(s_w_lo_ready, 2 * bi + p - 1)
                    src = w_in_d[0, p * 512:(p + 1) * 512, ct * P:(ct + 1) * P]
                    sp.dma_start(w_raw[p][:, :, :], src.rearrange("(k p) c -> p k c", p=P)).then_inc(
                        s_w_landed[p], 16)
                if ct >= MG:
                    b, m = MERGE_TILES[merge]
                    if merge >= 2:
                        sp.wait_ge(s_br_done, 2 * (merge - 1))
                    src = w_branch_d[0, b, :, m * P:(m + 1) * P]
                    sp.dma_start(w_branch[merge % 2][:, :, :], src.rearrange("(k p) c -> p k c", p=P)).then_inc(
                        s_w_branch_landed[merge % 2], 16)
                    merge += 1

        @block.gpsimd
        def _(pool):
            nc.gpsimd.memset(lru_w[:, :, :], 0.0).then_inc(s_lru_w_zero, 1)
            for bi in range(len(BULK)):
                for p in range(2):
                    pool.wait_ge(s_w_landed[p], 16 * (bi + 1))
                    if bi >= 1:
                        if p == 0:
                            pool.wait_ge(s_w_first_used, bi)
                        else:
                            pool.wait_ge(s_proj_done, 2 * bi)
                    nc.gpsimd.tensor_copy(w_hi[p][:, :, :], w_raw[p][:, :, :]).then_inc(s_w_hi_ready, 1)
                    pool.wait_ge(s_w_hi_ready, after(s_w_hi_ready))
                    nc.gpsimd.tensor_tensor(w_lo[p][:, :, :], w_raw[p][:, :, :],
                                            w_hi[p][:, :, :].bitcast(F32), ALU.subtract).then_inc(s_w_lo_ready, 1)

        @block.tensor
        def _(pe):
            mm = pe.matmul
            state = {"bi": 0, "merge": 0, "after_merge": False}


            def project(count):
                for _ in range(count):
                    bi = state["bi"]
                    ct = BULK[bi]
                    banks = (0, 1) if bi % 2 == 0 else (2, 3)
                    if state["after_merge"]:
                        pe.wait_ge(s_merged, 2 * state["merge"])
                        pe.wait_ge(s_evac, 2 * bi)
                        state["after_merge"] = False
                    elif bi >= 2:
                        pe.wait_ge(s_evac, 2 * bi - 2)
                    stream(bi, ct, banks)

            def stream(bi, ct, banks, parts=(0, 1, 2, 3)):
                for p in range(2):
                    for n in range(2):
                        if 2 * p + n not in parts:
                            continue
                        if n == 0:
                            pe.wait_ge(s_w_lo_ready, 2 * bi + p + 1)
                        if bi == 0:
                            pe.wait_ge(s_hn_lo_ready, 8 * n + 4 * (p + 1))
                        if ct in TIME_MAJOR:
                            for i4 in range(4):
                                o = bank[banks[n]][:, i4 * P:(i4 + 1) * P]
                                t0 = (4 * n + i4) * P
                                for k4 in range(4):
                                    k = 4 * p + k4
                                    for q, (h, w) in enumerate(((hn_hi, w_hi), (hn_lo, w_hi), (hn_hi, w_lo))):
                                        last = mm(o, h[:, k, t0:t0 + P], w[p][:, k4, :],
                                                  start=(p == 0 and i4 == 0 and k4 == 0 and q == 0),
                                                  stop=(p == 1 and k4 == 3 and q == 2), skip_group_check=True)
                        else:
                            o = bank[banks[n]][:, :]
                            for k4 in range(4):
                                k = 4 * p + k4
                                for q, (h, w) in enumerate(((hn_hi, w_hi), (hn_lo, w_hi), (hn_hi, w_lo))):
                                    last = mm(o, w[p][:, k4, :], h[:, k, n * HALF:(n + 1) * HALF],
                                              start=(p == 0 and k4 == 0 and q == 0),
                                              stop=(p == 1 and k4 == 3 and q == 2))
                        if p == 1:
                            last.then_inc(s_proj_done, 1)
                        elif n == 1:
                            last.then_inc(s_w_first_used, 1)
                if 3 in parts:
                    state["bi"] += 1

            def project_part(part):
                bi = state["bi"]
                if part == 0:
                    pe.wait_ge(s_evac, 2 * bi - 2)
                stream(bi, BULK[bi], (0, 1) if bi % 2 == 0 else (2, 3), (part,))

            def merge_part(part):
                bi, mi = state["bi"], state["merge"]
                if part < 4:
                    if part == 0:
                        pe.wait_ge(s_evac, 2 * bi)
                    stream(bi, BULK[bi], (0, 1), (part,))
                    return
                b, m = MERGE_TILES[mi]
                n, y = part - 4, Y_SLOT[b]
                if n == 0:
                    pe.wait_ge(s_w_branch_landed[mi % 2], 16 * (mi // 2 + 1))
                    pe.wait_ge(s_y_ready[b], 2)
                if mi:
                    pe.wait_ge(s_merged, 2 * mi - 1 + n)
                for k in range(2):
                    last = mm(bank[2 + n][:, :], w_branch[mi % 2][:, k, :], slot(y + k)[:, n * HALF:(n + 1) * HALF],
                              start=(k == 0), stop=(k == 1))
                last.then_inc(s_br_done, 1)
                if n == 1:
                    state["merge"] += 1
                    state["after_merge"] = True

            pe.wait_ge(s_tables_landed, TAB_DMAS)
            for u in range(16):
                n, k = u // 8, u % 8
                if u >= 4:
                    pe.wait_ge(s_hn_f32_ready, u - 3)
                if k == 0:
                    pe.wait_ge(s_xn_ready, 4 * (n + 1))
                for i4 in range(4):
                    last = pe.transpose(bank[4 + u % 4][:, i4 * P:(i4 + 1) * P],
                                        slot(MERGED + 4 * n + i4)[:, k * P:(k + 1) * P], ident)
                last.then_inc(s_xn_turned, 1)
                if u == 3:
                    pe.wait_ge(s_mod_acc, 8)
                    pe.wait_ge(s_ones_ready, 1)
                    for m in range(16):
                        last = mm(bank[0][:, m:m + 1], acc[:, m * P:(m + 1) * P], ones, start=True, stop=True)
                    last.then_inc(s_mod_done, 1)
            pe.wait_ge(s_mod_read, 2)
            project(4)
            pe.wait_ge(s_lru_w_landed, 128)
            for j in range(2):
                pe.wait_ge(s_conv_ready, j + 1)
                for g in range(2):
                    for n in range(2):
                        q = 4 + 2 * g + n
                        pe.wait_ge(s_hn_f32_ready, 16)
                        if j:
                            pe.wait_ge(s_gates_ready, 2 * g + n + 1)
                        mm(bank[q][:, :], lru_w[:, 2 * g + j, :], slot(4 + j)[:, n * HALF:(n + 1) * HALF],
                           start=True, stop=True).then_inc(s_gates_done, 1)
            project(7)
            pe.wait_ge(s_a_tanh, 1)
            for j in range(2):
                for g in range(2):
                    for n in range(2):
                        if j == 0:
                            pe.wait_ge(s_gates_ready, 4 + 2 * g + n + 1)
                        else:
                            pe.wait_ge(s_gates_ready, 8 + 2 * g + n + 1)
                        r = slice(64 * g, 64 * g + 64)
                        mm(bank[4 + 2 * g + n][:, :], wa2[r, j * P:(j + 1) * P],
                           slot(16)[r, n * HALF:(n + 1) * HALF], start=True, stop=True).then_inc(s_gates_done, 1)
            project(2)

            def head_sums(src, turn):
                for j in range(2):
                    pe.wait_ge(s_squares, 2 * turn + j + 1)
                    for n in range(2):
                        mm(bank[4 + 2 * j + n][:, :], blockones,
                           slot(src + j)[:, n * HALF:(n + 1) * HALF], start=True, stop=True).then_inc(s_head_sums, 1)

            pe.wait_ge(s_gates_ready, 16)
            head_sums(18, 0)
            project(2)
            pe.wait_ge(s_roots, 4)
            for q in range(2):
                for n in range(2):
                    pe.wait_ge(s_evac, 2 * (BULK_AT[CK] + 1))
                    mm(bank[4 + 2 * q + n][:, :], tb("perm"), slot(20 + q)[:, n * HALF:(n + 1) * HALF],
                       start=True, stop=True).then_inc(s_rot_done, 1)
            pe.wait_ge(s_kz_ready, 1)
            for n in range(2):
                for i4 in range(4):
                    i = 4 * n + i4
                    last = pe.transpose(bank[4 + n][:, i4 * P:(i4 + 1) * P], slot(17)[:, i * P:(i + 1) * P], ident)
                last.then_inc(s_kz_turned, 1)
            v_c = pair(22).rearrange("p a t -> p (a t)").rearrange("p (i c) -> p i c", i=NT)
            pe.wait_ge(s_kz_tm_ready, 2)
            pe.wait_ge(s_ret_r_ready, 1)
            def ret_scores(i):
                pe.wait_ge(s_ret_q_ready, i + 1)
                if i >= 2:
                    pe.wait_ge(s_ret_p_ready, i - 1)
                mm(bank[5 + i % 2][:, :], slot(21)[:, i * P:(i + 1) * P], ret_q[i % 2], start=True, stop=True).then_inc(s_ret_s_done, 1)

            ret_scores(0)
            for i in range(NT):
                ts = slice(i * P, (i + 1) * P)
                if i + 1 < NT:
                    ret_scores(i + 1)
                mm(bank[4][:, 0:256], kz_tm[:, i, :], v_c[:, i, :], start=True, stop=True).then_inc(s_ret_kv_done, 1)
                project_part(i % 4)
                pe.wait_ge(s_ret_p_ready, i + 1)
                if i:
                    pe.wait_ge(s_ret_o_ready, i)
                for j in range(2):
                    mm(bank[7][:, j * P:(j + 1) * P], ret_r[:, j * P:(j + 1) * P], slot(16)[:, ts], start=True,
                       stop=False, skip_group_check=True)
                    for h in (2 * j, 2 * j + 1):
                        last = mm(bank[7][64 * (h % 2):64 * (h % 2) + 64, j * P:(j + 1) * P],
                                  v_c[:, i, 64 * h:64 * h + 64], ret_p[i % 2][:, h, :], start=False, stop=True,
                                  skip_group_check=True)
                last.then_inc(s_ret_o_done, 1)
                if i + 1 < NT:
                    pe.wait_ge(s_ret_r_ready, i + 2)
            head_sums(16, 1)

            pe.wait_ge(s_roots, 8)

            def turn(o, src):
                return pe.transpose(o, src, ident)

            def rwkv_products(i):
                ts = slice(i * P, (i + 1) * P)
                if i:
                    pe.wait_ge(s_a_y_ready, 2 * i)
                    pe.wait_ge(s_a_g_ready, 4 * i)
                pe.wait_ge(s_a_ends_ready, i + 1)
                turn(bank[4][:, 0:128], slot(12)[:, ts])
                turn(bank[4][:, 128:256], slot(13)[:, ts])
                for j in range(2):
                    turn(bank[4][:, 256 + j * P:384 + j * P], a_r[:, 2 * j:2 * j + 2, 0, :])
                turn(bank[5][:, 0:128], b_end[:, 0:2, :]).then_inc(s_a_tm1_done, 1)
                turn(bank[5][:, 128:256], b_end[:, 2:4, :])
                turn(bank[5][:, 256:384], k_end[:, 0:2, :])
                turn(bank[5][:, 384:512], k_end[:, 2:4, :]).then_inc(s_a_tm2_done, 1)
                for par in range(2):
                    r = slice(64 * par, 64 * par + 64)
                    for a, src in enumerate((b_hat, k_hat)):
                        for j in range(2):
                            for c in range(2):
                                last = mm(bank[6 + par][64 * c:64 * c + 64, (2 * a + j) * P:(2 * a + j + 1) * P],
                                          src[r, 2 * j + c, :], a_r[r, 2 * j + c, :, :], start=True, stop=True)
                    last.then_inc(s_a_m_done, 1)
                merge_part(0)
                pe.wait_ge(s_a_tm_ready, 2 * i + 2)
                for par in range(2):
                    r = slice(64 * par, 64 * par + 64)
                    for j in range(2):
                        for c in range(2):
                            last = mm(bank[4 + par][64 * c:64 * c + 64, j * C:(j + 1) * C], a_r[r, 2 * j + c, 0, :],
                                      b_hat[r, 2 * j + c, :], start=True, stop=True)
                    last.then_inc(s_a_a_done, 1)

            def each(f):
                for h in range(4):
                    for c in range(2):
                        last = f(h, slice(64 * c, 64 * c + 64), c)
                return last

            def rwkv_inverse(i):
                for l in range(1, 6):
                    pe.wait_ge(s_a_x_ready, 6 * i + l)
                    each(lambda h, r, c: mm(bank[5][r, h * C:(h + 1) * C], m13(h)[r, 0:C], xx[r, 0, h, :], start=True, stop=True)).then_inc(s_a_v_done, 1)
                    merge_part(l)
                    pe.wait_ge(s_a_v_ready, 5 * i + l)
                    if l < 5:
                        each(lambda h, r, c: mm(bank[6][r, h * C:(h + 1) * C], xx[r, 1, h, :], v_lev[r, h, :],
                                                start=True, stop=True))
                    each(lambda h, r, c: mm(bank[6][r, 256 + h * C:256 + (h + 1) * C], v_lev[r, h, :], xx[r, 1, h, :], start=True, stop=True)).then_inc(s_a_dx_done, 1)
                each(lambda h, r, c: mm(bank[4][r, h * C:(h + 1) * C], m24(h)[r, 0:C], tm1[r, h * C:(h + 1) * C], start=True, stop=True)).then_inc(s_a_p_done, 1)
                pe.wait_ge(s_a_x_ready, 6 * i + 6)
                each(lambda h, r, c: mm(bank[6 + c][64 * (h % 2):64 * (h % 2) + 64, (h // 2) * C:(h // 2 + 1) * C], tm1[r, 256 + h * C:256 + (h + 1) * C], xx[r, 1, h, :], start=True, stop=True)).then_inc(s_a_w_done, 1)
                merge_part(0)
                pe.wait_ge(s_a_p_ready, i + 1)
                each(lambda h, r, c: mm(bank[5][r, h * C:(h + 1) * C], xx[r, 1, h, :], p_sb[r, h * C:(h + 1) * C], start=True, stop=True)).then_inc(s_a_u_done, 1)

            def rwkv_chunk(i, c):
                n = 2 * i + c
                rc = slice(64 * c, 64 * c + 64)
                if c == 0:
                    merge_part(1)
                pe.wait_ge(s_a_w_ready, 2 * i + 2)
                pe.wait_ge(s_a_u_ready, i + 1)
                if n:
                    pe.wait_ge(s_a_g_ready, 2 * n)
                else:
                    pe.wait_ge(s_a_g_zero, 1)
                for h in range(4):
                    r = slice(64 * (h % 2), 64 * (h % 2) + 64)
                    last = mm(bank[6 + h % 2][rc, (h // 2) * C:(h // 2 + 1) * C],
                              w_t[r, c * P + (h // 2) * C:c * P + (h // 2 + 1) * C],
                              G[r, (h // 2) * C:(h // 2 + 1) * C], start=True, stop=True)
                last.then_inc(s_a_wg_done, 1)
                if n:
                    pe.wait_ge(s_a_y_ready, n)
                for h in range(4):
                    r = slice(64 * (h % 2), 64 * (h % 2) + 64)
                    last = mm(bank[4][r, (h // 2) * C:(h // 2 + 1) * C], G[r, (h // 2) * C:(h // 2 + 1) * C],
                              a_r[r, 2 * (h // 2) + c, 1, :], start=True, stop=True)
                last.then_inc(s_a_y_done, 1)
                merge_part(2 + 2 * c)
                pe.wait_ge(s_a_sa_ready, 2 * n + 2)
                for h in range(4):
                    r = slice(64 * (h % 2), 64 * (h % 2) + 64)
                    hc = slice(h * C, (h + 1) * C)
                    o = bank[6][r, 256 + (h // 2) * C:256 + (h // 2 + 1) * C]
                    mm(o, u_sb[rc, hc], m13(h)[rc, C:2 * C], start=True, stop=False, skip_group_check=True)
                    last = mm(o, tm1[rc, hc], m24(h)[rc, C:2 * C], start=False, stop=True, skip_group_check=True)
                last.then_inc(s_a_y_done, 1)
                for h in range(4):
                    r = slice(64 * (h % 2), 64 * (h % 2) + 64)
                    hc = slice(h * C, (h + 1) * C)
                    o = bank[5][r, (h // 2) * C:(h // 2 + 1) * C]
                    mm(o, tm2[rc, hc], u_sb[rc, hc], start=True, stop=False, skip_group_check=True)
                    last = mm(o, tm2[rc, 256 + h * C:256 + (h + 1) * C], tm1[rc, hc], start=False, stop=True,
                              skip_group_check=True)
                last.then_inc(s_a_gnew_done, 1)
                merge_part(3 + 2 * c)

            for i in range(NT):
                rwkv_products(i)
                rwkv_inverse(i)
                rwkv_chunk(i, 0)
                rwkv_chunk(i, 1)
            pe.wait_ge(s_a_y_ready, 16)
            pe.wait_ge(s_a_g_ready, 32)
            project(4)
            for j in range(2):
                for n in range(2):
                    mm(bank[4 + 2 * j + n][:, :], blockones, slot(4 + j)[:, n * HALF:(n + 1) * HALF],
                       start=True, stop=True).then_inc(s_a_mean_done, 1)
            head_sums(6, 2)
            for j in range(2):
                pe.wait_ge(s_a_rk_ready, j + 1)
                for n in range(2):
                    pe.wait_ge(s_roots, 8 + 2 * j + n + 1)
                    mm(bank[4 + 2 * j + n][:, :], blockones, slot(14 + j)[:, n * HALF:(n + 1) * HALF],
                       start=True, stop=True).then_inc(s_a_bonus_done, 1)
            project(6)

            v_b = pair(8).rearrange("p a t -> p (a t)").rearrange("p (i c) -> p i c", i=NT)
            pe.wait_ge(s_a_bonus_read, 4)
            pe.wait_ge(s_evac, 2 * state["bi"])
            for i in range(NT):
                ts = slice(i * P, (i + 1) * P)
                pe.wait_ge(s_b_z_ready, i + 1)
                if i:
                    pe.wait_ge(s_b_o_ready, i)
                    pe.wait_ge(s_b_s_ready, 2 * i + 1)
                    pe.wait_ge(s_b_p_ready, i)
                turn(bank[6][:, 0:128], dz[:, 8, 0, :])
                turn(bank[6][:, 128:256], dz[:, 8, 1, :])
                for hh in range(2):
                    r = slice(64 * hh, 64 * hh + 64)
                    for j in range(2):
                        mm(bank[4 + hh][0:64, 384 + j * 64:448 + j * 64], dz[r, 0, j, 0:64], dz[r, 0, j, 64:128],
                           start=True, stop=True)
                        for nb in (0, 2):
                            mm(bank[6 + hh][32 * nb:32 * nb + 32, 256 + j * 32:288 + j * 32],
                               dz[r, 1, j, 32 * nb:32 * nb + 32], dz[r, 1, j, 32 * nb + 32:32 * nb + 64],
                               start=True, stop=True, tile_position=(64 * hh, 32 * nb))
                        for l in range(NLOW):
                            for nb in range(4):
                                if l < 5:
                                    z = dz[r, 2 + l, j, 32 * nb:32 * nb + 32]
                                    lhs, rhs = z, z
                                else:
                                    cs = slice(i * P + 32 * nb, i * P + 32 * nb + 32)
                                    lhs, rhs = slot(12 + j)[r, cs], slot(0 + j)[r, cs]
                                c0 = j * 192 + l * 32
                                last = mm(bank[4 + hh][32 * nb:32 * nb + 32, c0:c0 + 32], lhs, rhs, start=True,
                                          stop=True, tile_position=(64 * hh, 32 * nb))
                    last.then_inc(s_b_scores_done, 1)
                merge_part(0)
                merge_part(1)
                pe.wait_ge(s_b_p_ready, i + 1)
                pe.wait_ge(s_b_s_ready, 2 * i + 1)
                for h in range(4):
                    j, r = h // 2, slice(64 * (h % 2), 64 * (h % 2) + 64)
                    hc = slice(64 * h, 64 * h + 64)

                    def o(a, b):
                        return bank[7][r, j * P + a:j * P + b]

                    mm(o(0, 128), h_s[r, j * 64:j * 64 + 64], h_qe[r, j, :], start=True, stop=False,
                       skip_group_check=True)
                    last = mm(o(0, 128), v_b[:, i, hc], h_p[:, h, :], start=False, stop=True, skip_group_check=True)
                last.then_inc(s_b_o_done, 1)
                pe.wait_ge(s_b_ke_ready, i + 1)
                for h in range(4):
                    j, r = h // 2, slice(64 * (h % 2), 64 * (h % 2) + 64)
                    hc = slice(64 * h, 64 * h + 64)
                    last = mm(bank[6][r, 384 + j * 64:448 + j * 64], ke_tm[:, hc], v_b[:, i, hc], start=True, stop=True)
                last.then_inc(s_b_snew_done, 1)
                for part in range(2, 6):
                    merge_part(part)
            pe.wait_ge(s_b_s_ready, 17)
            head_sums(12, 3)
            for _ in range(8):
                for part in range(6):
                    merge_part(part)
            pe.wait_ge(s_gate_acc, 8)
            pe.wait_ge(s_roots, 16)
            pe.wait_ge(s_ones2_ready, 1)
            for n in range(2):
                mm(bank[4 + n][:, :], st(2048, P), slot(3)[:, n * HALF:(n + 1) * HALF], start=True, stop=True).then_inc(s_gate_done, 1)
            pe.wait_ge(s_merged, 64)
            pe.wait_ge(s_gate_read, 2)
            for tt in range(NT):
                for n in range(2):
                    bk = bank[(2 * tt + n) % 8]
                    if tt >= 4:
                        pe.wait_ge(s_out_read, 2 * (tt - 4) + n + 1)
                    for k in range(KT):
                        if tt == 0 and n == 0:
                            pe.wait_ge(s_x_landed[k], 32)
                        last = mm(bk[:, :], slot(MERGED + k)[:, tt * P:(tt + 1) * P],
                                  slot(OUT_W[k])[:, n * HALF:(n + 1) * HALF], start=(k == 0), stop=(k == KT - 1))
                    last.then_inc(s_out_done, 1)

        @block.scalar
        def _(act):
            for src, dst in ((ins["tables"], tab[:, :]), (ins["wa2"], wa2[:, :]), (ins["reset64"], reset)):
                act.dma_start(dst, src).then_inc(s_tables_landed, 16)



            def halves(n):
                return slice(n * HALF, (n + 1) * HALF)

            act.wait_ge(s_lru_w_zero, 1)
            for g, name in enumerate(("lru_wa", "lru_wx")):
                for q in range(4):
                    j, r = q // 2, slice(64 * (q % 2), 64 * (q % 2) + 64)
                    act.dma_start(lru_w[r, 2 * g + j, r], ins[name][0, q, :, :]).then_inc(s_lru_w_landed, 16)
            act.wait_ge(s_params_landed, 16)
            nc.scalar.activation(cond, pcs("c"), ACT.Silu).then_inc(s_cond_ready, 1)
            act.wait_ge(s_cond_ready, after(s_cond_ready))
            for i in range(NT):
                act.wait_ge(s_x_landed[i], 16)
                nc.scalar.activation(scratch, slot(MERGED + i), ACT.Square, accum_out=ssq[:, i:i + 1])\
                    .then_inc(s_x_squares, 1)
                act.wait_ge(s_x_squares, after(s_x_squares))
            nc.scalar.activation(rs, ssq, ACT.Sqrt, scale=1.0 / D, bias=pc("eps")).then_inc(s_x_rms, 1)
            act.wait_ge(s_x_rms, after(s_x_rms))
            act.wait_ge(s_rs_ready, 1)
            for i in range(NT):
                nc.scalar.activation(slot(MERGED + i), slot(MERGED + i), ACT.Copy, scale=rs[:, i:i + 1])\
                    .then_inc(s_xn_ready, 1)
                act.wait_ge(s_xn_ready, after(s_xn_ready))
            for u in range(16):
                n, k = u // 8, u % 8
                act.wait_ge(s_hn_f32_ready, u + 1)
                nc.scalar.activation(hn_hi[:, k, halves(n)], hn_f32[u % 4], ACT.Copy).then_inc(s_hn_hi_ready, 1)
                act.wait_ge(s_hn_hi_ready, after(s_hn_hi_ready))
            act.wait_ge(s_lam_abs, 1)
            nc.scalar.activation(sc2, sc1, ACT.Exp, scale=-1.0).then_inc(s_lam_exp, 1)
            act.wait_ge(s_lam_exp, after(s_lam_exp))
            act.wait_ge(s_lb_shifted, 1)
            nc.scalar.activation(lball, sc4, ACT.Exp).then_inc(s_lb_exp, 1)
            act.wait_ge(s_lb_exp, after(s_lb_exp))

            state = {"bi": 0, "merge": 0}

            def evac(count):
                for _ in range(count):
                    bi = state["bi"]
                    ct = BULK[bi]
                    banks = (0, 1) if bi % 2 == 0 else (2, 3)
                    for n in range(2):
                        act.wait_ge(s_proj_done, 2 * bi + n + 1)
                        src = bank[banks[n]][:, :]
                        if ct in TIME_MAJOR:
                            s0, j = TIME_MAJOR[ct]
                            dst = pair(s0).rearrange("p a t -> p (a t)").rearrange("p (i c) -> p i c", i=NT)
                            nc.scalar.activation(dst[:, 4 * n:4 * n + 4, j * P:(j + 1) * P],
                                                 src.rearrange("p (i c) -> p i c", c=P), ACT.Copy).then_inc(s_evac, 1)
                            act.wait_ge(s_evac, after(s_evac))
                        else:
                            nc.scalar.activation(slot(PROJ[ct])[:, halves(n)], src,
                                                 ACT.Silu if ct in GATED else ACT.Copy).then_inc(s_evac, 1)
                            act.wait_ge(s_evac, after(s_evac))
                    state["bi"] += 1

            def merge_gate():
                bi, mi = state["bi"], state["merge"]
                for n in range(2):
                    act.wait_ge(s_proj_done, 2 * bi + n + 1)
                    if mi:
                        act.wait_ge(s_merged, 2 * (mi - 1) + n + 1)
                    nc.scalar.activation(sig[n], bank[n][:, :], ACT.Sigmoid).then_inc(s_evac, 1)
                    act.wait_ge(s_evac, after(s_evac))
                state["bi"] += 1
                state["merge"] += 1

            act.wait_ge(s_mod_read, 2)
            evac(4)
            for j in range(2):
                for g, bias in enumerate(("ba", "bx")):
                    for n in range(2):
                        act.wait_ge(s_gates_done, 4 * j + 2 * g + n + 1)
                        dst = slot(j) if g == 0 else slot(14 + j)
                        nc.scalar.activation(dst[:, halves(n)], bank[4 + 2 * g + n][:, :], ACT.Sigmoid,
                                             bias=pc(bias, j)).then_inc(s_gates_ready, 1)
                        act.wait_ge(s_gates_ready, after(s_gates_ready))
            for j in range(2):
                act.wait_ge(s_lru_y8_ready, j + 1)
                nc.scalar.activation(slot(6 + j), slot(j), ACT.Tanh).then_inc(s_lru_t, 1)
                act.wait_ge(s_lru_t, after(s_lru_t))
                nc.scalar.activation(slot(j), slot(j), ACT.Exp, scale=-1.0).then_inc(s_lru_a, 1)
                act.wait_ge(s_lru_a, after(s_lru_a))
            for j in range(2):
                act.wait_ge(s_lru_q_ready, j + 1)
                nc.scalar.activation(slot(6 + j), slot(6 + j), ACT.Sqrt, scale=2.0).then_inc(s_lru_mult, 1)
                act.wait_ge(s_lru_mult, after(s_lru_mult))
            evac(7)
            act.wait_ge(s_a_mixed, 7)
            nc.scalar.activation(slot(16)[0:64, :], slot(16)[0:64, :], ACT.Tanh).then_inc(s_a_tanh, 1)
            act.wait_ge(s_a_tanh, after(s_a_tanh))
            act.wait_ge(s_y_ready[3], 2)
            for j in range(2):
                for g, bias in enumerate(("w0", "a0")):
                    for n in range(2):
                        act.wait_ge(s_gates_done, 8 + 4 * j + 2 * g + n + 1)
                        dst = slot(j) if g == 0 else slot(14 + j)
                        nc.scalar.activation(dst[:, halves(n)], bank[4 + 2 * g + n][:, :], ACT.Sigmoid,
                                             bias=pc(bias, j)).then_inc(s_gates_ready, 1)
                        act.wait_ge(s_gates_ready, after(s_gates_ready))
            for j in range(2):
                act.wait_ge(s_a_kk_ready, j + 1)
                nc.scalar.activation(slot(18 + j), slot(4 + j), ACT.Square).then_inc(s_squares, 1)
                act.wait_ge(s_squares, after(s_squares))
            evac(2)
            for j in range(2):
                for n in range(2):
                    act.wait_ge(s_head_sums, 2 * j + n + 1)
                    nc.scalar.activation(slot(18 + j)[:, halves(n)], bank[4 + 2 * j + n][:, :], ACT.Sqrt)\
                        .then_inc(s_roots, 1)
                    act.wait_ge(s_roots, after(s_roots))
            act.wait_ge(s_a_b_ready, 2)
            evac(2)
            act.dma_start(slot(16), ins["cos"]).then_inc(s_cos_landed, 16)
            act.wait_ge(s_a_norms_used, 2)
            act.dma_start(slot(17), ins["sin"]).then_inc(s_sin_landed, 16)
            for n in range(2):
                act.wait_ge(s_kz_turned, n + 1)
                nc.scalar.activation(kz_tm[:, 4 * n:4 * n + 4, :],
                                     bank[4 + n][:, :].rearrange("p (i c) -> p i c", c=P), ACT.Copy)\
                    .then_inc(s_kz_tm_ready, 1)
                act.wait_ge(s_kz_tm_ready, after(s_kz_tm_ready))
            for i in range(NT):
                act.wait_ge(s_ret_o_done, i + 1)
                nc.scalar.activation(pair(18)[:, :, i * P:(i + 1) * P],
                                     bank[7][:, 0:256].rearrange("p (j t) -> p j t", j=2), ACT.Copy)\
                    .then_inc(s_ret_o_ready, 1)
                act.wait_ge(s_ret_o_ready, after(s_ret_o_ready))
                if i % 4 == 3:
                    evac(1)

            def square_and_root(src, tmp, turn, scale, eps):
                for j in range(2):
                    nc.scalar.activation(slot(tmp + j), slot(src + j), ACT.Square).then_inc(s_squares, 1)
                    act.wait_ge(s_squares, after(s_squares))
                for j in range(2):
                    act.wait_ge(s_head_sums, 4 * turn + 2 * j + 2)
                    for n in range(2):
                        nc.scalar.activation(slot(tmp + j)[:, halves(n)], bank[4 + 2 * j + n][:, :],
                                             ACT.Sqrt, scale=scale, bias=pc(eps)).then_inc(s_roots, 1)
                        act.wait_ge(s_roots, after(s_roots))

            square_and_root(18, 16, 1, 1.0 / 64, "eps")

            for i in range(NT):
                ts = slice(i * P, (i + 1) * P)
                b4 = pair(0)[:, :, ts].rearrange("p j (c t) -> p j c t", t=C)
                if i:
                    act.wait_ge(s_a_g_ready, 4 * i)
                else:
                    act.wait_ge(s_a_b_ready, 2)
                    act.wait_ge(s_c_out_ready, 2)
                nc.scalar.activation(Ep.rearrange("p (j c) t -> p j c t", c=2)[:, :, :, 1:65], b4, ACT.Exp)\
                    .then_inc(s_a_e_ready, 1)
                act.wait_ge(s_a_e_ready, after(s_a_e_ready))
                if i:
                    act.wait_ge(s_a_y_done, 4 * i)
                nc.scalar.activation(Em.rearrange("p (j c) t -> p j c t", c=2), b4, ACT.Exp, scale=-1.0)\
                    .then_inc(s_a_e_ready, 1)
                act.wait_ge(s_a_e_ready, after(s_a_e_ready))
                act.wait_ge(s_a_tm1_done, i + 1)
                nc.scalar.activation(tm1, bank[4][:, :], ACT.Copy).then_inc(s_a_tm_ready, 1)
                act.wait_ge(s_a_tm_ready, after(s_a_tm_ready))
                act.wait_ge(s_a_tm2_done, i + 1)
                nc.scalar.activation(tm2, bank[5][:, :], ACT.Copy).then_inc(s_a_tm_ready, 1)
                act.wait_ge(s_a_tm_ready, after(s_a_tm_ready))
                merge_gate()
                act.wait_ge(s_a_p_done, i + 1)
                nc.scalar.activation(p_sb, bank[4][:, 0:256], ACT.Copy).then_inc(s_a_p_ready, 1)
                act.wait_ge(s_a_p_ready, after(s_a_p_ready))
                act.wait_ge(s_a_w_done, i + 1)
                for c in range(2):
                    nc.scalar.activation(w_t[:, c * P:(c + 1) * P], bank[6 + c][:, 0:P], ACT.Copy)\
                        .then_inc(s_a_w_ready, 1)
                    act.wait_ge(s_a_w_ready, after(s_a_w_ready))
                act.wait_ge(s_a_u_done, i + 1)
                nc.scalar.activation(u_sb, bank[5][:, 0:256], ACT.Copy).then_inc(s_a_u_ready, 1)
                act.wait_ge(s_a_u_ready, after(s_a_u_ready))
                for c in range(2):
                    if c == 1:
                        merge_gate()
                    act.wait_ge(s_a_y_done, 4 * i + 2 * c + 1)
                    nc.scalar.activation(pair(4)[:, :, i * P + c * C:i * P + (c + 1) * C],
                                         bank[4][:, 0:P].rearrange("p (j t) -> p j t", j=2), ACT.Copy)\
                        .then_inc(s_a_y_part, 1)
                    act.wait_ge(s_a_y_part, after(s_a_y_part))
            evac(4)
            act.wait_ge(s_a_centred, 4)
            square_and_root(4, 6, 2, 1.0 / 64, "ln_eps")
            act.wait_ge(s_lb_ready, 1)
            act.wait_ge(s_y_ready[0], 2)
            evac(2)
            for j in range(2):
                nc.scalar.activation(slot(12 + j), slot(4 + j), ACT.Sigmoid, scale=-1.0).then_inc(s_b_k_sig, 1)
                act.wait_ge(s_b_k_sig, after(s_b_k_sig))
                nc.scalar.activation(slot(4 + j), slot(4 + j), ACT.Sigmoid).then_inc(s_b_f_sig, 1)
                act.wait_ge(s_b_f_sig, after(s_b_f_sig))
            for j in range(2):
                act.wait_ge(s_b_f_ready, j + 1)
                nc.scalar.activation(slot(4 + j), slot(4 + j), ACT.Ln).then_inc(s_b_lnf, 1)
                act.wait_ge(s_b_lnf, after(s_b_lnf))
            act.dma_start(reset, ins["reset128"]).then_inc(s_reset128_landed, 16)
            evac(4)
            act.wait_ge(s_b_d_ready, 1)
            nc.scalar.activation(dz[:, :, :, :], dz[:, :, :, :], ACT.Exp).then_inc(s_b_e_ready, 1)
            act.wait_ge(s_b_e_ready, after(s_b_e_ready))
            for i in range(NT):
                act.wait_ge(s_b_scores_done, 2 * i + 1)
                nc.scalar.activation(ke_tm, bank[6][:, 0:256], ACT.Copy).then_inc(s_b_ke_ready, 1)
                act.wait_ge(s_b_ke_ready, after(s_b_ke_ready))
                act.wait_ge(s_b_o_done, i + 1)
                nc.scalar.activation(pair(6)[:, :, i * P:(i + 1) * P],
                                     bank[7][:, 0:256].rearrange("p (j t) -> p j t", j=2), ACT.Copy)\
                    .then_inc(s_b_o_ready, 1)
                act.wait_ge(s_b_o_ready, after(s_b_o_ready))
                if i + 1 < NT:
                    act.wait_ge(s_b_d_ready, i + 2)
                    nc.scalar.activation(dz[:, :, :, :], dz[:, :, :, :], ACT.Exp).then_inc(s_b_e_ready, 1)
                    act.wait_ge(s_b_e_ready, after(s_b_e_ready))
                merge_gate()
            square_and_root(6, 12, 3, 1.0 / 64, "eps")
            act.wait_ge(s_y_ready[1], 2)
            act.dma_start(slot(2), ins["b_gate"].partition_broadcast(P)).then_inc(s_b_gate_landed, 16)
            act.dma_start(final_g, ins["final_g"].partition_broadcast(P)).then_inc(s_final_g_landed, 16)
            for k in range(KT):
                if k >= 4:
                    act.wait_ge(s_gate_acc, k - 3)
                act.dma_start(slot(XR[k % 4]), w_mod_d[0, k * P:(k + 1) * P, 2 * D:3 * D]).then_inc(
                    s_w_mod_landed[k % 4], 16)
                act.dma_start(slot(OUT_W[k]), w_out_d[0, k * P:(k + 1) * P, :]).then_inc(s_x_landed[k], 16)
            for _ in range(8):
                merge_gate()
            for i in range(4):
                act.wait_ge(s_gate_acc, 8)
                act.dma_start(slot(XR[i]), x_d[0, i * P:(i + 1) * P, :]).then_inc(s_xr_landed[i], 16)
            for tt in range(NT):
                act.wait_ge(s_h_ready, 2 * tt + 2)
                nc.scalar.activation(st(2176, T), slot(XR[tt % 4]), ACT.Square, accum_out=ssq2[:, tt:tt + 1])\
                    .then_inc(s_h_squares, 1)
                act.wait_ge(s_h_squares, after(s_h_squares))
                nc.scalar.activation(rs2[:, tt:tt + 1], ssq2[:, tt:tt + 1], ACT.Sqrt, scale=1.0 / D, bias=pc("eps"))\
                    .then_inc(s_h_rms, 1)
                act.wait_ge(s_h_rms, after(s_h_rms))
                act.wait_ge(s_out_ready, tt + 1)
                act.dma_start(out_d[0, tt * P:(tt + 1) * P, :], slot(XR[tt % 4])).then_inc(s_stored[tt % 4], 16)
                if tt + 4 < NT:
                    act.wait_ge(s_stored[tt % 4], 16)
                    act.dma_start(slot(XR[tt % 4]), x_d[0, (tt + 4) * P:(tt + 5) * P, :]).then_inc(
                        s_xr_landed[tt % 4], 16)
            for i in range(4):
                act.wait_ge(s_stored[i], 32)

        @block.vector
        def _(dve):





            def halves(n):
                return slice(n * HALF, (n + 1) * HALF)

            MUL, ADD, SUB, MAX = ALU.mult, ALU.add, ALU.subtract, ALU.max
            nc.vector.memset(ones, 1.0).then_inc(s_ones_ready, 1)
            dve.wait_ge(s_ones_ready, after(s_ones_ready))
            dve.wait_ge(s_params_landed, 16)
            lam = pcs("lam")
            nc.vector.tensor_scalar(sc3, lam, -1.0, None, MUL).then_inc(s_vector_step, 1)
            dve.wait_ge(s_vector_step, after(s_vector_step))
            nc.vector.tensor_tensor(sc1, lam, sc3, MAX).then_inc(s_lam_abs, 1)
            dve.wait_ge(s_lam_abs, after(s_lam_abs))
            lb = pcs("lb")
            nc.vector.tensor_tensor(sc4, lb, lb, SUB).then_inc(s_lb_shifted, 1)
            dve.wait_ge(s_lb_shifted, after(s_lb_shifted))
            dve.wait_ge(s_x_rms, 1)
            nc.vector.reciprocal(rs, rs).then_inc(s_rs_ready, 1)
            dve.wait_ge(s_rs_ready, after(s_rs_ready))
            dve.wait_ge(s_cond_ready, 1)
            for k in range(KT):
                dve.wait_ge(s_w_mod_landed[k % 4], 16 * (k // 4 + 1))
                if k == 0:
                    nc.vector.tensor_scalar(acc, w_mod[0], cond[:, 0:1], None, MUL).then_inc(s_mod_acc, 1)
                    dve.wait_ge(s_mod_acc, after(s_mod_acc))
                else:
                    nc.vector.scalar_tensor_tensor(out=acc, in0=w_mod[k % 4], scalar=cond[:, k:k + 1],
                                                   in1=acc, op0=MUL, op1=ADD).then_inc(s_mod_acc, 1)
                    dve.wait_ge(s_mod_acc, after(s_mod_acc))
            dve.wait_ge(s_mod_done, 1)
            b_mod = pcs("b_mod")
            nc.vector.tensor_tensor(sh, bank[0][:, 0:8], b_mod[:, 0:8], ADD).then_inc(s_mod_read, 1)
            dve.wait_ge(s_mod_read, after(s_mod_read))
            nc.vector.scalar_tensor_tensor(out=gs, in0=bank[0][:, 8:16], scalar=1.0, in1=b_mod[:, 8:16],
                                           op0=ADD, op1=ADD).then_inc(s_mod_read, 1)
            dve.wait_ge(s_mod_read, after(s_mod_read))
            nc.vector.tensor_tensor(gs, gs, pcs("norm_g"), MUL).then_inc(s_vector_step, 1)
            dve.wait_ge(s_vector_step, after(s_vector_step))
            for u in range(17):
                if u < 16:
                    dve.wait_ge(s_xn_turned, u + 1)
                    if u >= 4:
                        dve.wait_ge(s_hn_lo_ready, u - 3)
                    nc.vector.tensor_scalar(hn_f32[u % 4], bank[4 + u % 4][:, :], gs[:, u % 8:u % 8 + 1],
                                            sh[:, u % 8:u % 8 + 1], MUL, ADD).then_inc(s_hn_f32_ready, 1)
                    dve.wait_ge(s_hn_f32_ready, after(s_hn_f32_ready))
                if u >= 1:
                    v = u - 1
                    dve.wait_ge(s_hn_hi_ready, v + 1)
                    o = (slice(None), v % 8, halves(v // 8))
                    nc.vector.tensor_tensor(hn_lo[o], hn_f32[v % 4], hn_hi[o].bitcast(F32), SUB)\
                        .then_inc(s_hn_lo_ready, 1)
                    dve.wait_ge(s_hn_lo_ready, after(s_hn_lo_ready))
            dve.wait_ge(s_lam_exp, 1)
            nc.vector.tensor_scalar(sc1, sc2, 2.0, None, ADD).then_inc(s_vector_step, 1)
            dve.wait_ge(s_vector_step, after(s_vector_step))
            nc.vector.reciprocal(sc1, sc1).then_inc(s_vector_step, 1)
            dve.wait_ge(s_vector_step, after(s_vector_step))
            nc.vector.tensor_tensor(sc1, sc1, sc2, MUL).then_inc(s_vector_step, 1)
            dve.wait_ge(s_vector_step, after(s_vector_step))
            nc.vector.tensor_tensor(sc2, sc1, sc1, MUL).then_inc(s_vector_step, 1)
            dve.wait_ge(s_vector_step, after(s_vector_step))
            dve.wait_ge(s_lb_exp, 1)
            nc.vector.tensor_scalar(sp8, sc2, 1.0 / 17, 1.0 / 15, MUL, ADD).then_inc(s_vector_step, 1)
            dve.wait_ge(s_vector_step, after(s_vector_step))
            for q in (13, 11, 9, 7, 5, 3, 1):
                nc.vector.tensor_tensor(sp8, sp8, sc2, MUL).then_inc(s_vector_step, 1)
                dve.wait_ge(s_vector_step, after(s_vector_step))
                nc.vector.tensor_scalar(sp8, sp8, 1.0 / q, None, ADD).then_inc(s_vector_step, 1)
                dve.wait_ge(s_vector_step, after(s_vector_step))
            nc.vector.tensor_tensor(sp8, sp8, sc1, MUL).then_inc(s_vector_step, 1)
            dve.wait_ge(s_vector_step, after(s_vector_step))
            nc.vector.tensor_scalar(sc3, sc3, 0.0, None, MAX).then_inc(s_vector_step, 1)
            dve.wait_ge(s_vector_step, after(s_vector_step))
            nc.vector.scalar_tensor_tensor(out=sp8, in0=sp8, scalar=2.0, in1=sc3, op0=MUL, op1=ADD)\
                .then_inc(s_vector_step, 1)
            dve.wait_ge(s_vector_step, after(s_vector_step))
            nc.vector.tensor_scalar(sp8, sp8, 8.0, None, MUL).then_inc(s_vector_step, 1)
            dve.wait_ge(s_vector_step, after(s_vector_step))
            nc.vector.reciprocal(sc4, lball).then_inc(s_vector_step, 1)
            dve.wait_ge(s_vector_step, after(s_vector_step))
            nc.vector.tensor_tensor(lball, lball, sc4, MUL).then_inc(s_vector_step, 1)
            dve.wait_ge(s_vector_step, after(s_vector_step))
            nc.vector.tensor_tensor(lball, lball, lball, SUB).then_inc(s_vector_step, 1)
            dve.wait_ge(s_vector_step, after(s_vector_step))
            nc.vector.tensor_scalar(omlb, lball, -1.0, 1.0, MUL, ADD).then_inc(s_lb_ready, 1)
            dve.wait_ge(s_lb_ready, after(s_lb_ready))

            for j in range(2):
                dve.wait_ge(s_evac, 2 * (j + 1))
                x, y = slot(j), slot(4 + j)
                if j == 0:
                    dve.wait_ge(s_mod_done, 1)
                nc.vector.tensor_scalar(y, x, pc("conv_w", 6 + j), pc("conv_b", j), MUL, ADD).then_inc(s_vector_step, 1)
                dve.wait_ge(s_vector_step, after(s_vector_step))
                for lag in (1, 2, 3):
                    nc.vector.scalar_tensor_tensor(out=y[:, lag:], in0=x[:, :T - lag],
                                                   scalar=pc("conv_w", 2 * (3 - lag) + j), in1=y[:, lag:],
                                                   op0=MUL, op1=ADD)\
                        .then_inc(s_vector_step if lag < 3 else s_conv_ready, 1)
                    dve.wait_ge(s_vector_step if lag < 3 else s_conv_ready, after(s_vector_step if lag < 3 else s_conv_ready))
            for j in range(2):
                dve.wait_ge(s_gates_ready, 4 * j + 4)
                nc.vector.tensor_scalar(slot(j), slot(j), sp8[:, j:j + 1], None, MUL).then_inc(s_lru_y8_ready, 1)
                dve.wait_ge(s_lru_y8_ready, after(s_lru_y8_ready))
                nc.vector.tensor_tensor(slot(4 + j), slot(14 + j), slot(4 + j), MUL).then_inc(s_vector_step, 1)
                dve.wait_ge(s_vector_step, after(s_vector_step))
            for j in range(2):
                dve.wait_ge(s_lru_t, j + 1)
                nc.vector.tensor_scalar(slot(14 + j), slot(6 + j), 1.0, None, ADD).then_inc(s_vector_step, 1)
                dve.wait_ge(s_vector_step, after(s_vector_step))
                nc.vector.reciprocal(slot(14 + j), slot(14 + j)).then_inc(s_vector_step, 1)
                dve.wait_ge(s_vector_step, after(s_vector_step))
                nc.vector.tensor_tensor(slot(6 + j), slot(6 + j), slot(14 + j), MUL).then_inc(s_lru_q_ready, 1)
                dve.wait_ge(s_lru_q_ready, after(s_lru_q_ready))
            for j in range(2):
                dve.wait_ge(s_lru_mult, j + 1)
                nc.vector.memset(slot(6 + j)[:, 0:1], 1.0).then_inc(s_vector_step, 1)
                dve.wait_ge(s_vector_step, after(s_vector_step))
                nc.vector.tensor_tensor(slot(4 + j), slot(4 + j), slot(6 + j), MUL).then_inc(s_vector_step, 1)
                dve.wait_ge(s_vector_step, after(s_vector_step))
                dve.wait_ge(s_lru_a, j + 1)
                nc.vector.tensor_tensor_scan(slot(6 + j), slot(j), slot(4 + j), 0.0, MUL, ADD)\
                    .then_inc(s_vector_step, 1)
                dve.wait_ge(s_vector_step, after(s_vector_step))
                dve.wait_ge(s_evac, 2 * (BULK_AT[DG] + j + 1))
                nc.vector.tensor_tensor(slot(2 + j), slot(6 + j), slot(2 + j), MUL).then_inc(s_y_ready[3], 1)
                dve.wait_ge(s_y_ready[3], after(s_y_ready[3]))

            for q, s in enumerate((8, 9, 10, 11, 12, 13, 16)):
                dve.wait_ge(s_evac, 2 * (BULK_AT[AR] + q + 1))
                u, d = slot(s), slot(18 + q % 2)
                nc.vector.tensor_scalar(d[:, 0:1], u[:, 0:1], -1.0, None, MUL).then_inc(s_vector_step, 1)
                dve.wait_ge(s_vector_step, after(s_vector_step))
                nc.vector.tensor_tensor(d[:, 1:], u[:, :T - 1], u[:, 1:], SUB).then_inc(s_vector_step, 1)
                dve.wait_ge(s_vector_step, after(s_vector_step))
                nc.vector.scalar_tensor_tensor(out=u, in0=d, scalar=pc("mu", q), in1=u, op0=MUL, op1=ADD)\
                    .then_inc(s_a_mixed, 1)
                dve.wait_ge(s_a_mixed, after(s_a_mixed))
            for j in range(2):
                nc.vector.tensor_scalar(slot(4 + j), slot(10 + j), pc("kk", j), None, MUL).then_inc(s_a_kk_ready, 1)
                dve.wait_ge(s_a_kk_ready, after(s_a_kk_ready))
            for j in range(2):
                dve.wait_ge(s_gates_ready, 8 + 4 * (j + 1))
                a, k, ld = slot(14 + j), slot(10 + j), slot(j)
                nc.vector.tensor_scalar(slot(22 + j), a, 1.0, pc("ka", j), SUB, MUL).then_inc(s_vector_step, 1)
                dve.wait_ge(s_vector_step, after(s_vector_step))
                nc.vector.scalar_tensor_tensor(out=k, in0=slot(22 + j), scalar=1.0, in1=k, op0=ADD, op1=MUL)\
                    .then_inc(s_vector_step, 1)
                dve.wait_ge(s_vector_step, after(s_vector_step))
                nc.vector.tensor_scalar(ld, ld, float(-np.exp(-0.5)), None, MUL).then_inc(s_vector_step, 1)
                dve.wait_ge(s_vector_step, after(s_vector_step))
                dve.wait_ge(s_tables_landed, TAB_DMAS)
                nc.vector.tensor_tensor_scan(slot(22 + j), reset, ld, 0.0, MUL, ADD).then_inc(s_vector_step, 1)
                dve.wait_ge(s_vector_step, after(s_vector_step))
                nc.vector.tensor_copy(ld, slot(22 + j)).then_inc(s_a_b_ready, 1)
                dve.wait_ge(s_a_b_ready, after(s_a_b_ready))
            for j in range(2):
                dve.wait_ge(s_roots, 2 * j + 2)
                n, kk, a = slot(18 + j), slot(4 + j), slot(14 + j)
                nc.vector.tensor_scalar(n, n, 1e-12, None, MAX).then_inc(s_vector_step, 1)
                dve.wait_ge(s_vector_step, after(s_vector_step))
                nc.vector.reciprocal(n, n).then_inc(s_vector_step, 1)
                dve.wait_ge(s_vector_step, after(s_vector_step))
                nc.vector.scalar_tensor_tensor(out=kk, in0=kk, scalar=-1.0, in1=n, op0=MUL, op1=MUL)\
                    .then_inc(s_vector_step, 1)
                dve.wait_ge(s_vector_step, after(s_vector_step))
                nc.vector.scalar_tensor_tensor(out=a, in0=kk, scalar=-1.0, in1=a, op0=MUL, op1=MUL)\
                    .then_inc(s_a_norms_used, 1)
                dve.wait_ge(s_a_norms_used, after(s_a_norms_used))

            dve.wait_ge(s_cos_landed, 16)
            dve.wait_ge(s_sin_landed, 16)
            for q in range(2):
                for n in range(2):
                    dve.wait_ge(s_rot_done, 2 * q + n + 1)
                    s = slot(20 + q)[:, halves(n)]
                    nc.vector.tensor_tensor(rope_tmp[n], bank[4 + 2 * q + n][:, :], slot(17)[:, halves(n)], MUL)\
                        .then_inc(s_vector_step, 1)
                    dve.wait_ge(s_vector_step, after(s_vector_step))
                    nc.vector.tensor_tensor(s, s, slot(16)[:, halves(n)], MUL).then_inc(s_vector_step, 1)
                    dve.wait_ge(s_vector_step, after(s_vector_step))
                    nc.vector.tensor_tensor(s, s, rope_tmp[n], ADD).then_inc(s_vector_step, 1)
                    dve.wait_ge(s_vector_step, after(s_vector_step))

            def by_chunk(ap):
                return ap.rearrange("p (i t) -> p i t", t=P)

            def over_chunks(name):
                return tb(name).unsqueeze(1).to_broadcast([P, NT, P])

            nc.vector.tensor_tensor(by_chunk(slot(17)), by_chunk(slot(21)), over_chunks("zeta"), MUL)\
                .then_inc(s_kz_ready, 1)
            dve.wait_ge(s_kz_ready, after(s_kz_ready))
            nc.vector.tensor_tensor(by_chunk(slot(16)), by_chunk(slot(20)), over_chunks("xi"), MUL)\
                .then_inc(s_vector_step, 1)
            dve.wait_ge(s_vector_step, after(s_vector_step))
            nc.vector.memset(ret_r, 0.0).then_inc(s_ret_r_ready, 1)
            dve.wait_ge(s_ret_r_ready, after(s_ret_r_ready))
            heads = tb("ret_head").unsqueeze(2)

            def ret_mask_q(i):
                q_all = slot(20)[:, i * P:(i + 1) * P].unsqueeze(1).to_broadcast([P, 4, P])
                if i >= 2:
                    dve.wait_ge(s_ret_s_done, i - 1)
                nc.vector.tensor_tensor(ret_q[i % 2], q_all, heads.to_broadcast([P, 4, P]), MUL)\
                    .then_inc(s_ret_q_ready, 1)
                dve.wait_ge(s_ret_q_ready, after(s_ret_q_ready))

            ret_mask_q(0)
            for i in range(NT):
                if i + 1 < NT:
                    ret_mask_q(i + 1)
                dve.wait_ge(s_ret_kv_done, i + 1)
                nc.vector.tensor_tensor(ret_kv.rearrange("p (h v) -> p h v", h=4),
                                        bank[4][:, 0:256].rearrange("p (h v) -> p h v", h=4),
                                        heads.to_broadcast([P, 4, C]), MUL).then_inc(s_vector_step, 1)
                dve.wait_ge(s_vector_step, after(s_vector_step))
                if i >= 2:
                    dve.wait_ge(s_ret_o_done, i - 1)
                dve.wait_ge(s_ret_s_done, i + 1)
                nc.vector.tensor_tensor(ret_p[i % 2].rearrange("p h t -> p (h t)"), bank[5 + i % 2][:, :],
                                        tb("decay"), MUL).then_inc(s_ret_p_ready, 1)
                dve.wait_ge(s_ret_p_ready, after(s_ret_p_ready))
                dve.wait_ge(s_ret_o_done, i + 1)
                nc.vector.scalar_tensor_tensor(out=ret_r, in0=ret_r, scalar=pc("gamma_c"), in1=ret_kv,
                                               op0=MUL, op1=ADD).then_inc(s_ret_r_ready, 1)
                dve.wait_ge(s_ret_r_ready, after(s_ret_r_ready))

            def normed(o, tmp, turn, gain, g, final):
                for j in range(2):
                    dve.wait_ge(s_roots, 4 * turn + 2 * j + 2)
                    nc.vector.reciprocal(slot(tmp + j), slot(tmp + j)).then_inc(s_vector_step, 1)
                    dve.wait_ge(s_vector_step, after(s_vector_step))
                    nc.vector.tensor_tensor(slot(o + j), slot(o + j), slot(tmp + j), MUL).then_inc(s_vector_step, 1)
                    dve.wait_ge(s_vector_step, after(s_vector_step))
                    nc.vector.scalar_tensor_tensor(out=slot(g + j), in0=slot(o + j), scalar=pc(gain, j),
                                                   in1=slot(g + j), op0=MUL, op1=MUL).then_inc(final, 1)
                    dve.wait_ge(final, after(final))

            dve.wait_ge(s_evac, 2 * (BULK_AT[CG] + 2))
            normed(18, 16, 1, "ret_g", 6, s_y_ready[2])
            nc.vector.memset(sc1, 0.0).then_inc(s_c_out_ready, 1)
            dve.wait_ge(s_c_out_ready, after(s_c_out_ready))
            nc.vector.memset(Ep[:, :, 0:1], 1.0).then_inc(s_c_out_ready, 1)
            dve.wait_ge(s_c_out_ready, after(s_c_out_ready))

            state = {"merge": 0}

            def merge():
                mi = state["merge"]
                b, m = MERGE_TILES[mi]
                bi = BULK_AT[MG + 8 * b + m]
                for n in range(2):
                    dve.wait_ge(s_evac, 2 * bi + n + 1)
                    dve.wait_ge(s_br_done, 2 * mi + n + 1)
                    o = slot(MERGED + m)[:, halves(n)]
                    if mi < 8:
                        nc.vector.tensor_tensor(o, sig[n], bank[2 + n][:, :], MUL).then_inc(s_merged, 1)
                        dve.wait_ge(s_merged, after(s_merged))
                    else:
                        nc.vector.tensor_tensor(sig[n], sig[n], bank[2 + n][:, :], MUL).then_inc(s_vector_step, 1)
                        dve.wait_ge(s_vector_step, after(s_vector_step))
                        nc.vector.tensor_tensor(o, o, sig[n], ADD).then_inc(s_merged, 1)
                        dve.wait_ge(s_merged, after(s_merged))
                state["merge"] += 1

            nc.vector.memset(G, 0.0).then_inc(s_a_g_zero, 1)
            dve.wait_ge(s_a_g_zero, after(s_a_g_zero))
            def prep(i):
                tsl = slice(i * P, (i + 1) * P)

                def four(s):
                    return pair(s)[:, :, tsl].rearrange("p j (c t) -> p j c t", t=C)

                def jc(ap):
                    return ap.rearrange("p (j c) t -> p j c t", c=2)

                ar = a_r.rearrange("p (j c) a t -> p j c a t", c=2)
                ep = jc(Ep)
                dve.wait_ge(s_a_e_ready, 2 * i + 2)
                if i:
                    dve.wait_ge(s_a_gnew_done, 2 * i)
                nc.vector.tensor_tensor(ar[:, :, :, 0, :], four(4), ep[:, :, :, 0:64], MUL).then_inc(s_vector_step, 1)
                dve.wait_ge(s_vector_step, after(s_vector_step))
                nc.vector.tensor_tensor(ar[:, :, :, 1, :], four(8), ep[:, :, :, 1:65], MUL).then_inc(s_vector_step, 1)
                dve.wait_ge(s_vector_step, after(s_vector_step))
                nc.vector.tensor_tensor(jc(b_hat), four(14), jc(Em), MUL).then_inc(s_vector_step, 1)
                dve.wait_ge(s_vector_step, after(s_vector_step))
                nc.vector.tensor_tensor(jc(k_hat), four(10), jc(Em), MUL).then_inc(s_vector_step, 1)
                dve.wait_ge(s_vector_step, after(s_vector_step))
                e_end = Ep[:, :, 64:65].to_broadcast([P, 4, C])
                nc.vector.tensor_tensor(b_end, b_hat, e_end, MUL).then_inc(s_vector_step, 1)
                dve.wait_ge(s_vector_step, after(s_vector_step))
                nc.vector.tensor_tensor(k_end, k_hat, e_end, MUL).then_inc(s_a_ends_ready, 1)
                dve.wait_ge(s_a_ends_ready, after(s_a_ends_ready))

            prep(0)
            for i in range(NT):
                m_b = tb("m_rwkv").unsqueeze(1).to_broadcast([P, 4, P])
                for par in range(2):
                    dve.wait_ge(s_a_m_done, 2 * i + par + 1)
                    nc.vector.tensor_tensor(m_all[:, par].rearrange("p a j t -> p (a j) t"),
                                            bank[6 + par][:, :].rearrange("p (h t) -> p h t", h=4), m_b,
                                            MUL).then_inc(s_vector_step, 1)
                    dve.wait_ge(s_vector_step, after(s_vector_step))

                def heads_of(a, par):
                    return xx[:, a, :, :].rearrange("p (j o) t -> p j o t", o=2)[:, :, par, :]

                eye = tb("eye64").unsqueeze(1).to_broadcast([P, 4, C])
                for par in range(2):
                    nc.vector.tensor_tensor(heads_of(1, par), m_all[:, par, 0, :, 0:C],
                                            tb("up1").unsqueeze(1).to_broadcast([P, 2, C]), MUL)\
                        .then_inc(s_vector_step, 1)
                    dve.wait_ge(s_vector_step, after(s_vector_step))
                nc.vector.tensor_tensor(xx[:, 1, :, :], xx[:, 1, :, :], eye, ADD).then_inc(s_vector_step, 1)
                dve.wait_ge(s_vector_step, after(s_vector_step))

                def lev(l):
                    return tb("lev")[:, l * C:(l + 1) * C].unsqueeze(1).to_broadcast([P, 4, C])

                for par in range(2):
                    dve.wait_ge(s_a_a_done, 2 * i + par + 1)
                    nc.vector.tensor_tensor(heads_of(0, par),
                                            bank[4 + par][:, 0:128].rearrange("p (j t) -> p j t", j=2),
                                            tb("lev")[:, 0:C].unsqueeze(1).to_broadcast([P, 2, C]), MUL)\
                        .then_inc(s_vector_step, 1)
                    dve.wait_ge(s_vector_step, after(s_vector_step))
                nc.vector.tensor_tensor(xx[:, 0, :, :], xx[:, 0, :, :], eye, ADD).then_inc(s_a_x_ready, 1)
                dve.wait_ge(s_a_x_ready, after(s_a_x_ready))
                for l in range(1, 6):
                    dve.wait_ge(s_a_v_done, 5 * i + l)
                    nc.vector.tensor_tensor(v_lev, bank[5][:, 0:256].rearrange("p (h t) -> p h t", h=4), lev(l), MUL)\
                        .then_inc(s_a_v_ready, 1)
                    dve.wait_ge(s_a_v_ready, after(s_a_v_ready))
                    dve.wait_ge(s_a_dx_done, 5 * i + l)
                    xf = xx.rearrange("p a h t -> p (a h t)")
                    c0 = 0 if l < 5 else 256
                    nc.vector.tensor_tensor(xf[:, c0:512], xf[:, c0:512], bank[6][:, c0:512], ADD)\
                        .then_inc(s_a_x_ready, 1)
                    dve.wait_ge(s_a_x_ready, after(s_a_x_ready))
                merge()
                for c in range(2):
                    n = 2 * i + c
                    rc = slice(64 * c, 64 * c + 64)
                    dve.wait_ge(s_a_wg_done, n + 1)
                    u4 = u_sb.rearrange("p (j o v) -> p j o v", j=2, o=2)
                    for par in range(2):
                        nc.vector.tensor_tensor(u4[rc, :, par, :], u4[rc, :, par, :],
                                                bank[6 + par][rc, 0:128].rearrange("p (j v) -> p j v", j=2),
                                                ADD).then_inc(s_a_sa_ready, 1)
                        dve.wait_ge(s_a_sa_ready, after(s_a_sa_ready))
                    dve.wait_ge(s_a_y_done, 2 * n + 2)
                    dve.wait_ge(s_a_y_part, n + 1)
                    y = pair(4)[:, :, i * P + c * C:i * P + (c + 1) * C]
                    nc.vector.tensor_tensor(y, y, bank[6][:, 256:384].rearrange("p (j t) -> p j t", j=2), ADD)\
                        .then_inc(s_a_y_ready, 1)
                    dve.wait_ge(s_a_y_ready, after(s_a_y_ready))
                    dve.wait_ge(s_a_gnew_done, n + 1)
                    for j in range(2):
                        nc.vector.scalar_tensor_tensor(out=G[:, j * C:(j + 1) * C],
                                                       in0=G[:, j * C:(j + 1) * C],
                                                       scalar=Ep[:, 2 * j + c, 64:65],
                                                       in1=bank[5][:, j * C:(j + 1) * C], op0=MUL, op1=ADD)\
                            .then_inc(s_a_g_ready, 1)
                        dve.wait_ge(s_a_g_ready, after(s_a_g_ready))
                if i + 1 < NT:
                    prep(i + 1)
                merge()

            for j in range(2):
                for n in range(2):
                    dve.wait_ge(s_a_mean_done, 2 * j + n + 1)
                    y = slot(4 + j)[:, halves(n)]
                    nc.vector.scalar_tensor_tensor(out=y, in0=bank[4 + 2 * j + n][:, :], scalar=-1.0 / 64,
                                                   in1=y, op0=MUL, op1=ADD).then_inc(s_a_centred, 1)
                    dve.wait_ge(s_a_centred, after(s_a_centred))
            for j in range(2):
                nc.vector.scalar_tensor_tensor(out=slot(14 + j), in0=slot(8 + j), scalar=pc("rk", j),
                                               in1=slot(10 + j), op0=MUL, op1=MUL).then_inc(s_a_rk_ready, 1)
                dve.wait_ge(s_a_rk_ready, after(s_a_rk_ready))
            for j in range(2):
                dve.wait_ge(s_roots, 8 + 2 * j + 2)
                y, q = slot(4 + j), slot(6 + j)
                nc.vector.reciprocal(q, q).then_inc(s_vector_step, 1)
                dve.wait_ge(s_vector_step, after(s_vector_step))
                nc.vector.tensor_tensor(y, y, q, MUL).then_inc(s_vector_step, 1)
                dve.wait_ge(s_vector_step, after(s_vector_step))
                nc.vector.tensor_scalar(y, y, pc("ln_g", j), pc("ln_b", j), MUL, ADD).then_inc(s_vector_step, 1)
                dve.wait_ge(s_vector_step, after(s_vector_step))
                for n in range(2):
                    dve.wait_ge(s_a_bonus_done, 2 * j + n + 1)
                    nc.vector.tensor_tensor(q[:, halves(n)], slot(12 + j)[:, halves(n)],
                                            bank[4 + 2 * j + n][:, :], MUL).then_inc(s_a_bonus_read, 1)
                    dve.wait_ge(s_a_bonus_read, after(s_a_bonus_read))
                nc.vector.tensor_tensor(y, y, q, ADD).then_inc(s_vector_step, 1)
                dve.wait_ge(s_vector_step, after(s_vector_step))
                dve.wait_ge(s_evac, 2 * (BULK_AT[AG] + j + 1))
                nc.vector.tensor_tensor(slot(2 + j), y, slot(2 + j), MUL).then_inc(s_y_ready[0], 1)
                dve.wait_ge(s_y_ready[0], after(s_y_ready[0]))
            for j in range(2):
                dve.wait_ge(s_b_k_sig, j + 1)
                nc.vector.tensor_scalar(slot(12 + j), slot(12 + j), omlb[:, j:j + 1], None, MUL)\
                    .then_inc(s_vector_step, 1)
                dve.wait_ge(s_vector_step, after(s_vector_step))
                dve.wait_ge(s_b_f_sig, j + 1)
                nc.vector.tensor_scalar(slot(4 + j), slot(4 + j), omlb[:, j:j + 1], lball[:, j:j + 1], MUL, ADD)\
                    .then_inc(s_vector_step, 1)
                dve.wait_ge(s_vector_step, after(s_vector_step))
                nc.vector.tensor_scalar(slot(4 + j), slot(4 + j), 1e-19, None, MAX).then_inc(s_b_f_ready, 1)
                dve.wait_ge(s_b_f_ready, after(s_b_f_ready))
            dve.wait_ge(s_reset128_landed, 16)
            for j in range(2):
                dve.wait_ge(s_b_lnf, j + 1)
                nc.vector.tensor_tensor_scan(slot(14 + j), reset, slot(4 + j), 0.0, MUL, ADD).then_inc(s_vector_step, 1)
                dve.wait_ge(s_vector_step, after(s_vector_step))
            nc.vector.memset(h_p, 0.0).then_inc(s_vector_step, 1)
            dve.wait_ge(s_vector_step, after(s_vector_step))
            nc.vector.memset(h_s, 0.0).then_inc(s_b_s_ready, 1)
            dve.wait_ge(s_b_s_ready, after(s_b_s_ready))
            def exponents(i):
                b = pair(14)[:, :, i * P:(i + 1) * P]
                for li, hl in enumerate(LEVELS):
                    nb = 64 // hl
                    bb = b.rearrange("p j (n s) -> p j n s", s=2 * hl)
                    zz = dz[:, li, :, :].rearrange("p j (n s) -> p j n s", s=2 * hl)
                    mid = bb[:, :, :, hl - 1:hl].to_broadcast([P, 2, nb, hl])
                    nc.vector.tensor_tensor(zz[:, :, :, 0:hl], mid, bb[:, :, :, 0:hl], SUB).then_inc(s_vector_step, 1)
                    dve.wait_ge(s_vector_step, after(s_vector_step))
                    nc.vector.tensor_tensor(zz[:, :, :, hl:2 * hl], bb[:, :, :, hl:2 * hl], mid, SUB)\
                        .then_inc(s_vector_step, 1)
                    dve.wait_ge(s_vector_step, after(s_vector_step))
                nc.vector.tensor_copy(dz[:, 7, :, :], b).then_inc(s_vector_step, 1)
                dve.wait_ge(s_vector_step, after(s_vector_step))
                nc.vector.tensor_tensor(dz[:, 8, :, :], b[:, :, P - 1:P].to_broadcast([P, 2, P]), b, SUB)\
                    .then_inc(s_b_d_ready, 1)
                dve.wait_ge(s_b_d_ready, after(s_b_d_ready))

            def decayed(i):
                tsl = slice(i * P, (i + 1) * P)
                dve.wait_ge(s_b_e_ready, i + 1)
                if i == 0:
                    dve.wait_ge(s_evac, 2 * (BULK_AT[BG] + 2))
                q, k = pair(0)[:, :, tsl], pair(12)[:, :, tsl]
                for li, hl in enumerate(LEVELS):
                    zz = dz[:, li, :, :].rearrange("p j (n s) -> p j n s", s=2 * hl)
                    kk = k.rearrange("p j (n s) -> p j n s", s=2 * hl)
                    qq = q.rearrange("p j (n s) -> p j n s", s=2 * hl)
                    nc.vector.tensor_tensor(zz[:, :, :, 0:hl], zz[:, :, :, 0:hl], kk[:, :, :, 0:hl], MUL)\
                        .then_inc(s_vector_step, 1)
                    dve.wait_ge(s_vector_step, after(s_vector_step))
                    nc.vector.tensor_tensor(zz[:, :, :, hl:2 * hl], zz[:, :, :, hl:2 * hl],
                                            qq[:, :, :, hl:2 * hl], MUL).then_inc(s_vector_step, 1)
                    dve.wait_ge(s_vector_step, after(s_vector_step))
                nc.vector.tensor_copy(e_last, dz[:, 7, :, P - 1:P].rearrange("p j t -> p (j t)"))\
                    .then_inc(s_vector_step, 1)
                dve.wait_ge(s_vector_step, after(s_vector_step))
                nc.vector.tensor_tensor(h_qe, dz[:, 7, :, :], q, MUL).then_inc(s_vector_step, 1)
                dve.wait_ge(s_vector_step, after(s_vector_step))
                nc.vector.tensor_tensor(dz[:, 8, :, :], dz[:, 8, :, :], k, MUL).then_inc(s_b_z_ready, 1)
                dve.wait_ge(s_b_z_ready, after(s_b_z_ready))

            exponents(0)
            decayed(0)
            for i in range(NT):
                low = tb("low").rearrange("p (l t) -> p l t", l=NLOW)
                hd4 = h_diag.rearrange("p (j o) t -> p j o t", o=2)
                hp4 = h_p.rearrange("p (j o) t -> p j o t", o=2)
                for hh in range(2):
                    dve.wait_ge(s_b_scores_done, 2 * i + hh + 1)
                    for j in range(2):
                        nc.vector.tensor_tensor(h_prod[:, j],
                                                bank[4 + hh][:, j * 192:(j + 1) * 192].rearrange( "p (l t) -> p l t", l=NLOW),
                                                low, MUL).then_inc(s_vector_step, 1)
                        dve.wait_ge(s_vector_step, after(s_vector_step))
                    nc.vector.tensor_reduce(hd4[:, :, hh, :], h_prod.rearrange("p j l t -> p j t l"),
                                            mybir.AxisListType.X, ADD).then_inc(s_vector_step, 1)
                    dve.wait_ge(s_vector_step, after(s_vector_step))
                    nc.vector.tensor_copy(hp4[0:64, :, hh, 64:128],
                                          bank[4 + hh][0:64, 384:512].rearrange("p (j t) -> p j t", j=2))\
                        .then_inc(s_vector_step, 1)
                    dve.wait_ge(s_vector_step, after(s_vector_step))
                    dve.wait_ge(s_b_ke_ready, i + 1)
                    for nb in (0, 2):
                        r = slice(32 * nb, 32 * nb + 32)
                        nc.vector.tensor_copy(hp4[r, :, hh, 32 * nb + 32:32 * nb + 64],
                                              bank[6 + hh][r, 256:320].rearrange("p (j t) -> p j t", j=2))\
                            .then_inc(s_vector_step, 1)
                        dve.wait_ge(s_vector_step, after(s_vector_step))
                for nb in range(4):
                    r = slice(32 * nb, 32 * nb + 32)
                    nc.vector.tensor_copy(h_p[r, :, 32 * nb:32 * nb + 32], h_diag[r, :, :])\
                        .then_inc(s_vector_step if nb < 3 else s_b_p_ready, 1)
                    dve.wait_ge(s_vector_step if nb < 3 else s_b_p_ready, after(s_vector_step if nb < 3 else s_b_p_ready))
                if i + 1 < NT:
                    exponents(i + 1)
                dve.wait_ge(s_b_snew_done, i + 1)
                for j in range(2):
                    nc.vector.scalar_tensor_tensor(out=h_s[:, j * 64:(j + 1) * 64],
                                                   in0=h_s[:, j * 64:(j + 1) * 64],
                                                   scalar=e_last[:, j:j + 1],
                                                   in1=bank[6][:, 384 + j * 64:448 + j * 64], op0=MUL,
                                                   op1=ADD).then_inc(s_b_s_ready, 1)
                    dve.wait_ge(s_b_s_ready, after(s_b_s_ready))
                if i + 1 < NT:
                    decayed(i + 1)
                merge()
            normed(6, 12, 3, "hgrn_g", 10, s_y_ready[1])
            nc.vector.memset(st(2048, P), 1.0).then_inc(s_ones2_ready, 1)
            dve.wait_ge(s_ones2_ready, after(s_ones2_ready))
            for k in range(KT):
                dve.wait_ge(s_w_mod_landed[k % 4], 32 + 16 * (k // 4 + 1))
                if k == 0:
                    nc.vector.tensor_scalar(slot(3), slot(XR[0]), cond[:, 0:1], None, MUL).then_inc(s_gate_acc, 1)
                    dve.wait_ge(s_gate_acc, after(s_gate_acc))
                else:
                    nc.vector.scalar_tensor_tensor(out=slot(3), in0=slot(XR[k % 4]),
                                                   scalar=cond[:, k:k + 1], in1=slot(3), op0=MUL, op1=ADD)\
                        .then_inc(s_gate_acc, 1)
                    dve.wait_ge(s_gate_acc, after(s_gate_acc))
            for _ in range(8):
                merge()
            dve.wait_ge(s_b_gate_landed, 16)
            for n in range(2):
                dve.wait_ge(s_gate_done, n + 1)
                nc.vector.tensor_tensor(slot(2)[:, halves(n)], slot(2)[:, halves(n)], bank[4 + n][:, :], ADD)\
                    .then_inc(s_gate_read, 1)
                dve.wait_ge(s_gate_read, after(s_gate_read))
            dve.wait_ge(s_final_g_landed, 16)
            for i in range(NT):
                dve.wait_ge(s_xr_landed[i % 4], 16 * (i // 4 + 1))
                for n in range(2):
                    dve.wait_ge(s_out_done, 2 * i + n + 1)
                    tmp = fin_tmp[:, halves(n)]
                    nc.vector.tensor_tensor(tmp, bank[(2 * i + n) % 8][:, :], slot(2)[:, halves(n)], MUL)\
                        .then_inc(s_out_read, 1)
                    dve.wait_ge(s_out_read, after(s_out_read))
                    nc.vector.tensor_tensor(slot(XR[i % 4])[:, halves(n)], slot(XR[i % 4])[:, halves(n)], tmp, ADD)\
                        .then_inc(s_h_ready, 1)
                    dve.wait_ge(s_h_ready, after(s_h_ready))
                dve.wait_ge(s_h_rms, i + 1)
                nc.vector.reciprocal(rs2[:, i:i + 1], rs2[:, i:i + 1]).then_inc(s_vector_step, 1)
                dve.wait_ge(s_vector_step, after(s_vector_step))
                nc.vector.scalar_tensor_tensor(out=slot(XR[i % 4]), in0=slot(XR[i % 4]),
                                               scalar=rs2[:, i:i + 1], in1=final_g, op0=MUL, op1=MUL)\
                    .then_inc(s_out_ready, 1)
                dve.wait_ge(s_out_ready, after(s_out_ready))


TAB_DMAS = 48


def shape_tables():
    f = np.float32
    p = np.arange(P)
    t = {}
    t["ident"] = np.eye(P)
    t["blockones"] = (p[:, None] // 64 == p[None, :] // 64)
    perm = np.zeros((P, P))
    for m in range(P):
        if m % 32 < 16:
            perm[m + 16, m] = -1
        else:
            perm[m - 16, m] = 1
    t["perm"] = perm
    lg = np.log1p(-np.exp2(-5.0 - np.arange(4)))
    head = p // 32
    i = np.arange(P)
    t["xi"] = np.exp(lg[head][:, None] * (i[None] + 1.0))
    t["zeta"] = np.exp(lg[head][:, None] * (P - 1 - i[None])) * RET_SCALE
    rel = i[None, :] - i[:, None]
    t["decay"] = np.concatenate([np.where(rel >= 0, np.exp(lg[h] * np.maximum(rel, 0)), 0) * RET_SCALE
                                 for h in range(4)], 1)
    ks, qs = p[:, None] % 32, np.arange(32)[None]
    low = [(ks // (2 * l) == qs // (2 * l)) & (ks % (2 * l) < l) & (qs % (2 * l) >= l) for l in LEVELS[2:]]
    t["low"] = np.concatenate(low + [ks == qs], 1)
    s, q = p[:, None] % 64, np.arange(64)[None]
    t["m_rwkv"] = np.concatenate([s < q, s <= q], 1)
    t["lev"] = np.concatenate([(s // (2 * l) == q // (2 * l)) & (s % (2 * l) >= l) & (q % (2 * l) < l)
                               for l in (1, 2, 4, 8, 16, 32)], 1)
    t["up1"] = (s // 2 == q // 2) & (s < q)
    t["eye64"] = s == q
    t["ret_head"] = head[:, None] == np.arange(4)[None]
    tables = np.concatenate([np.asarray(t[n], f) for n, _ in TABLES], 1)
    inv = (f(1.0) / (f(10000.0) ** np.linspace(0.0, 1.0, 16, dtype=f))).astype(f)
    ang = (inv[p % 32 % 16][:, None] * np.arange(T, dtype=f)[None]).astype(f)
    starts = {n: np.broadcast_to((np.arange(T) % n != 0).astype(f), (P, T)) for n in (64, 128)}
    return {"tables": tables, "cos": np.cos(ang).astype(f), "sin": np.sin(ang).astype(f),
            "reset64": starts[64], "reset128": starts[128], "gamma_c": np.exp(lg[head] * P).astype(f)[:, None]}


def kernel(**inputs):
    import concourse.bacc as _bacc
    from concourse.bass_utils import run_bass_kernel_spmd as _run

    a = {k: np.ascontiguousarray(v) for k, v in inputs.items()}
    consts = shape_tables()

    def cols(v):
        return v.reshape(-1, P).T

    fields = {
        "c": cols(a["c"]), "norm_g": cols(a["norm_g"]), "b_mod": cols(a["b_mod"][0, :2 * D]), "mu": cols(a["rwkv_mu"]),
        "w0": cols(a["rwkv_w0"]), "a0": cols(a["rwkv_a0"]), "kk": cols(a["rwkv_kk"]), "ka": cols(a["rwkv_ka"]),
        "rk": cols(a["rwkv_rk"]), "ln_g": cols(a["rwkv_ln_g"]), "ln_b": cols(a["rwkv_ln_b"]), "lb": cols(a["hgrn_lb"]),
        "hgrn_g": cols(a["hgrn_norm_g"]), "ret_g": cols(a["ret_norm_g"]), "conv_w": cols(a["lru_conv_w"]),
        "conv_b": cols(a["lru_conv_b"]), "ba": cols(a["lru_ba"]), "bx": cols(a["lru_bx"]), "lam": cols(a["lru_lam"]),
        "eps": np.full((P, 1), EPS, np.float32), "ln_eps": np.full((P, 1), RWKV_LN_EPS, np.float32),
        "gamma_c": consts["gamma_c"],
    }
    arrays = {
        "x": a["x"], "w_mod": a["w_mod"], "w_in": a["w_in"], "w_branch": a["w_branch"], "w_out": a["w_out"],
        "params": np.concatenate([fields[n] for n, _ in PARAMS], 1), "wa2": np.concatenate([a["rwkv_w2"][0], a["rwkv_a2"][0]], 0),
        "lru_wa": a["lru_wa"], "lru_wx": a["lru_wx"], "b_gate": a["b_mod"][0, 2 * D:], "final_g": a["final_g"],
        "tables": consts["tables"], "cos": consts["cos"], "sin": consts["sin"],
        "reset64": consts["reset64"], "reset128": consts["reset128"],
    }
    arrays = {f"in_{n}": np.ascontiguousarray(v) for n, v in arrays.items()}
    nc = _bacc.Bacc("TRN2", target_bir_lowering=False, num_devices=1)
    ins = {n[3:]: nc.dram_tensor(n, v.shape, F32, kind="ExternalInput").ap() for n, v in arrays.items()}
    out = nc.dram_tensor("out", (1, T, D), F32, kind="ExternalOutput").ap()
    build(nc, ins, out)
    r = _run(nc, [arrays], core_ids=[0])
    return r.results[0]["out"]
```

```python
from contextlib import ExitStack

import numpy as np

import concourse.bass as bass
from concourse import mybir

F32 = mybir.dt.float32
F32R = mybir.dt.float32r
ACT = mybir.ActivationFunctionType
ALU = mybir.AluOpType

P = 128
T = 1024
D = 1024
BW = 256
KT = D // P
HALF = 512
NT = T // P
C = 64
RET_SCALE = 32 ** -0.5
EPS = 1e-6
RWKV_LN_EPS = 64e-5
LEVELS = (64, 32, 16, 8, 4, 2, 1)
NLOW = 6

AR, AK, AV, AWA, AG = 0, 2, 4, 6, 7
BQ, BF, BI, BG = 9, 11, 13, 15
CQ, CK, CV, CG = 17, 18, 19, 21
DX, DG = 23, 25
MG = 27

PARAMS = (("c", 8), ("norm_g", 8), ("b_mod", 16), ("mu", 7), ("w0", 2), ("a0", 2), ("kk", 2), ("ka", 2),
          ("rk", 2), ("ln_g", 2), ("ln_b", 2), ("lb", 2), ("hgrn_g", 2), ("ret_g", 2), ("conv_w", 8),
          ("conv_b", 2), ("ba", 2), ("bx", 2), ("lam", 2), ("eps", 1), ("ln_eps", 1), ("gamma_c", 1))
TABLES = (("ident", 128), ("blockones", 128), ("perm", 128), ("xi", 128), ("zeta", 128), ("decay", 512),
          ("low", NLOW * 32), ("m_rwkv", 128), ("lev", 6 * 64), ("up1", 64), ("eye64", 64), ("ret_head", 4))


def columns(fields):
    at, n = {}, 0
    for name, k in fields:
        at[name] = (n, n + k)
        n += k
    return at, n


PCOL, NPAR = columns(PARAMS)
TCOL, NTAB = columns(TABLES)

PROJ = {DX: 0, DX + 1: 1, DG: 2, DG + 1: 3, AR: 8, AR + 1: 9, AK: 10, AK + 1: 11, AV: 12, AV + 1: 13, AWA: 16,
        CQ: 20, CK: 21, CG: 6, CG + 1: 7, CV: 6, CV + 1: 7, BI: 10, BI + 1: 11, BQ: 0, BQ + 1: 1, AG: 2, AG + 1: 3,
        BG: 10, BG + 1: 11}
TIME_MAJOR = {CV: (22, 0), CV + 1: (22, 1), BI: (8, 0), BI + 1: (8, 1)}
GATED = (DG, DG + 1, CG, CG + 1, AG, AG + 1, BG, BG + 1)
BULK_D = [DX, DX + 1, DG, DG + 1]
BULK_A = [AR, AR + 1, AK, AK + 1, AV, AV + 1, AWA]
BULK_C = [CQ, CK, CV, CV + 1, CG, CG + 1]
BULK_B = [BF, BF + 1, AG, AG + 1, BI, BI + 1, BQ, BQ + 1, BG, BG + 1]
MERGE_BRANCHES = (3, 2, 0, 1)
MERGE_TILES = [(b, m) for b in MERGE_BRANCHES for m in (4, 5, 6, 7, 2, 3, 0, 1)]
BULK = (BULK_D + BULK_A + BULK_C + [MG + 8 * b + m for b, m in MERGE_TILES[:16]] + BULK_B
        + [MG + 8 * b + m for b, m in MERGE_TILES[16:]])
BULK_AT = {ct: n for n, ct in enumerate(BULK)}
Y_SLOT = {3: 2, 2: 6, 0: 2, 1: 10}
MERGED = 16


def build(nc, ins, out_d):
    x_d, w_mod_d, w_in_d, w_branch_d, w_out_d = (ins[n] for n in ("x", "w_mod", "w_in", "w_branch", "w_out"))
    with ExitStack() as ctx:
        def sb(name, shape, dt=F32):
            return ctx.enter_context(nc.sbuf_tensor(name, shape, dt))

        def sem(name):
            return ctx.enter_context(nc.semaphore(name))

        counts = {}

        def after(s):
            counts[s.name] = counts.get(s.name, 0) + 1
            return counts[s.name]

        s_params_landed = sem("params_landed")
        s_x_landed = [sem(f"x_landed{i}") for i in range(8)]
        s_mod_acc = sem("mod_acc")
        s_w_mod_landed = [sem(f"w_mod_landed{i}") for i in range(4)]
        s_tables_landed = sem("tables_landed")
        s_lru_w_zero = sem("lru_w_zero")
        s_lru_w_landed = sem("lru_w_landed")
        s_w_lo_ready = sem("w_lo_ready")
        s_w_landed = [sem(f"w_landed{i}") for i in range(2)]
        s_br_done = sem("br_done")
        s_w_branch_landed = [sem(f"w_branch_landed{i}") for i in range(2)]
        s_y_ready = [sem(f"y_ready{i}") for i in range(4)]
        s_gate_acc = sem("gate_acc")
        s_pool_step = sem("pool_step")
        s_out_w_ready = sem("out_w_ready")
        s_hn_hi_ready = sem("hn_hi_ready")
        s_hn_odd_ready = sem("hn_odd_ready")
        s_w_first_used = sem("w_first_used")
        s_proj_done = sem("proj_done")
        s_w_hi_ready = sem("w_hi_ready")
        s_ret_norm_ready = sem("ret_norm_ready")
        s_evac = sem("evac")
        s_merged = sem("merged")
        s_tm_ready = sem("tm_ready")
        s_tm_turned = sem("tm_turned")
        s_hn_even_ready = sem("hn_even_ready")
        s_ident_landed = sem("ident_landed")
        s_hn_f32_ready = sem("hn_f32_ready")
        s_xn_ready = sem("xn_ready")
        s_xn_turned = sem("xn_turned")
        s_ones_ready = sem("ones_ready")
        s_mod_done = sem("mod_done")
        s_mod_read = sem("mod_read")
        s_conv_ready = sem("conv_ready")
        s_gates_ready = sem("gates_ready")
        s_gates_done = sem("gates_done")
        s_a_tanh = sem("a_tanh")
        s_squares = sem("squares")
        s_head_sums = sem("head_sums")
        s_roots = sem("roots")
        s_rot_done = sem("rot_done")
        s_kz_ready = sem("kz_ready")
        s_kz_turned = sem("kz_turned")
        s_kz_tm_ready = sem("kz_tm_ready")
        s_ret_r_ready = sem("ret_r_ready")
        s_ret_q_ready = sem("ret_q_ready")
        s_ret_p_ready = sem("ret_p_ready")
        s_ret_s_done = sem("ret_s_done")
        s_ret_kv_done = sem("ret_kv_done")
        s_ret_o_ready = sem("ret_o_ready")
        s_ret_o_done = sem("ret_o_done")
        s_a_y_ready = sem("a_y_ready")
        s_a_g_ready = sem("a_g_ready")
        s_a_ends_ready = sem("a_ends_ready")
        s_a_tm1_done = sem("a_tm1_done")
        s_a_tm2_done = sem("a_tm2_done")
        s_a_m_done = sem("a_m_done")
        s_a_tm_ready = sem("a_tm_ready")
        s_a_a_done = sem("a_a_done")
        s_a_x_ready = sem("a_x_ready")
        s_a_v_done = sem("a_v_done")
        s_a_v_ready = sem("a_v_ready")
        s_a_dx_done = sem("a_dx_done")
        s_a_p_done = sem("a_p_done")
        s_a_w_done = sem("a_w_done")
        s_a_p_ready = sem("a_p_ready")
        s_a_u_done = sem("a_u_done")
        s_a_w_ready = sem("a_w_ready")
        s_a_g_zero = sem("a_g_zero")
        s_a_wg_done = sem("a_wg_done")
        s_a_y_done = sem("a_y_done")
        s_a_sa_ready = sem("a_sa_ready")
        s_a_gnew_done = sem("a_gnew_done")
        s_a_mean_done = sem("a_mean_done")
        s_a_rk_ready = sem("a_rk_ready")
        s_a_bonus_done = sem("a_bonus_done")
        s_a_bonus_read = sem("a_bonus_read")
        s_b_z_ready = sem("b_z_ready")
        s_b_o_ready = sem("b_o_ready")
        s_b_s_ready = sem("b_s_ready")
        s_b_p_ready = sem("b_p_ready")
        s_b_scores_done = sem("b_scores_done")
        s_b_o_done = sem("b_o_done")
        s_b_ke_ready = sem("b_ke_ready")
        s_b_snew_done = sem("b_snew_done")
        s_ones2_ready = sem("ones2_ready")
        s_gate_done = sem("gate_done")
        s_gate_read = sem("gate_read")
        s_out_read = sem("out_read")
        s_merged_lo_ready = sem("merged_lo_ready")
        s_out_done = sem("out_done")
        s_cond_ready = sem("cond_ready")
        s_x_squares = sem("x_squares")
        s_x_rms = sem("x_rms")
        s_rs_ready = sem("rs_ready")
        s_lam_abs = sem("lam_abs")
        s_lam_exp = sem("lam_exp")
        s_lb_shifted = sem("lb_shifted")
        s_lb_exp = sem("lb_exp")
        s_lru_y8_ready = sem("lru_y8_ready")
        s_lru_t = sem("lru_t")
        s_lru_a = sem("lru_a")
        s_lru_q_ready = sem("lru_q_ready")
        s_lru_mult = sem("lru_mult")
        s_a_mixed = sem("a_mixed")
        s_a_kk_ready = sem("a_kk_ready")
        s_cos_landed = sem("cos_landed")
        s_sin_landed = sem("sin_landed")
        s_a_b_ready = sem("a_b_ready")
        s_a_starts_ready = sem("a_starts_ready")
        s_a_e_ready = sem("a_e_ready")
        s_a_u_ready = sem("a_u_ready")
        s_a_y_part = sem("a_y_part")
        s_b_f_sig = sem("b_f_sig")
        s_reset128_landed = sem("reset128_landed")
        s_b_f_ready = sem("b_f_ready")
        s_b_lnf = sem("b_lnf")
        s_a_centred = sem("a_centred")
        s_b_d_ready = sem("b_d_ready")
        s_b_e_ready = sem("b_e_ready")
        s_b_k_sig = sem("b_k_sig")
        s_b_gate_landed = sem("b_gate_landed")
        s_xr_landed = [sem(f"xr_landed{i}") for i in range(4)]
        s_final_g_landed = sem("final_g_landed")
        s_merged_hi_ready = sem("merged_hi_ready")
        s_h_ready = sem("h_ready")
        s_h_squares = sem("h_squares")
        s_h_rms = sem("h_rms")
        s_out_ready = sem("out_ready")
        s_stored = [sem(f"stored{i}") for i in range(4)]
        s_vector_step = sem("vector_step")
        s_lb_ready = sem("lb_ready")
        s_a_norms_used = sem("a_norms_used")
        s_b_scanned = sem("b_scanned")

        hn_hi_at = -(-nc.sbuf_base // 32) * 32
        hn_hi = sb("hn_hi", [P, KT, T], F32R)
        hn_lo_at = -(-nc.sbuf_base // 32) * 32
        hn_lo = sb("hn_lo", [P, KT, T], F32R)
        w_raw = [sb(f"w_raw{i}", [P, 4, P]) for i in range(2)]
        w_hi = [sb(f"w_hi{i}", [P, 4, P], F32R) for i in range(2)]
        w_lo = [sb(f"w_lo{i}", [P, 4, P], F32R) for i in range(2)]
        w_branch = [sb(f"w_branch{i}", [P, 2, P]) for i in range(2)]
        slots_at = -(-nc.sbuf_base // 32) * 32
        slots = sb("slots", [P, 24, T])
        stage_at = -(-nc.sbuf_base // 32) * 32
        stage = sb("stage", [P, 5508])
        par = sb("par", [P, NPAR])
        tab = sb("tab", [P, NTAB])
        wa2 = sb("wa2", [P, BW])
        lru_w = sb("lru_w", [P, 4, P])
        small = sb("small", [P, 80])
        bank = [ctx.enter_context(nc.psum_tensor(f"bank{i}", [P, HALF], F32)) for i in range(8)]

        def slot(i):
            return slots[:, i, :]

        def pair(i):
            return slots[:, i:i + 2, :]

        def pc(name, j=0):
            a = PCOL[name][0] + j
            return par[:, a:a + 1]

        def pcs(name):
            a, b = PCOL[name]
            return par[:, a:b]

        def tb(name):
            a, b = TCOL[name]
            return tab[:, a:b]

        def st(a, n):
            return stage[:, a:a + n]

        ident, blockones = tb("ident"), tb("blockones")
        cond, ssq, rs, gs, sh = (small[:, a:a + 8] for a in (0, 8, 16, 24, 32))
        sp8, omlb, lball = small[:, 40:42], small[:, 42:44], small[:, 44:46]
        sc1, sc2, sc3, sc4 = (small[:, a:a + 2] for a in (46, 48, 50, 52))
        ssq2, rs2 = small[:, 54:62], small[:, 62:70]
        ones = small[:, 70:71]
        e_last = small[:, 72:74]

        acc = slots[:, 0:2, :].rearrange("p a t -> p (a t)")
        w_mod = [slots[:, 2 + 2 * i:4 + 2 * i, :].rearrange("p a t -> p (a t)") for i in range(4)]
        hn_f32 = [st(HALF * i, HALF) for i in range(4)]
        scratch = st(2048, T)
        reset = st(3200, T)
        kz_tm = st(0, T).rearrange("p (i c) -> p i c", c=P)
        rope_tmp = [st(1024, HALF), st(1536, HALF)]
        ret_p = [st(2048 + 512 * i, 512).rearrange("p (h t) -> p h t", h=4) for i in range(2)]
        ret_r = st(4224, 256)
        ret_q = [st(4480, 512).rearrange("p (h t) -> p h t", h=4), st(3072, 512).rearrange("p (h t) -> p h t", h=4)]
        ret_kv = st(3584, 256)
        Ep = st(0, 260).rearrange("p (g t) -> p g t", t=65)
        a_r = st(260, 512).rearrange("p (a g t) -> p g a t", a=2, t=C)
        b_hat = st(772, 256).rearrange("p (g t) -> p g t", t=C)
        k_hat = st(1028, 256).rearrange("p (g t) -> p g t", t=C)
        b_end = st(1284, 256).rearrange("p (g t) -> p g t", t=C)
        k_end = st(1540, 256).rearrange("p (g t) -> p g t", t=C)
        tm1 = st(1796, 512)
        tm2 = st(2308, 512)
        m_all = st(2820, 1024).rearrange("p (o a j t) -> p o a j t", o=2, a=2, j=2)
        Em = st(2820, 256).rearrange("p (g t) -> p g t", t=C)

        def m13(h):
            return m_all[:, h % 2, 0, h // 2, :]

        def m24(h):
            return m_all[:, h % 2, 1, h // 2, :]
        xx = st(3844, 512).rearrange("p (a h t) -> p a h t", a=2, h=4)
        G = st(4356, 128)
        v_lev = b_hat.rearrange("p g t -> p (g t)").rearrange("p (h t) -> p h t", h=4)
        w_t = k_hat.rearrange("p g t -> p (g t)")
        p_sb = b_end.rearrange("p g t -> p (g t)")
        u_sb = k_end.rearrange("p g t -> p (g t)")
        sig = [st(4484 + 512 * n, 512) for n in range(2)]
        dz = st(0, 9 * 256).rearrange("p (l j t) -> p l j t", l=9, j=2)
        ke_tm = st(2304, 256)
        h_diag = st(2560, 128).rearrange("p (h t) -> p h t", h=4)
        h_p = st(2688, 512).rearrange("p (h t) -> p h t", h=4)
        h_prod = st(3200, 384).rearrange("p (j l t) -> p j l t", j=2, l=NLOW)
        h_s = st(3584, 128)
        h_qe = st(3712, 256).rearrange("p (j t) -> p j t", j=2)
        b_f = [st(T * j, T) for j in range(2)]
        b_f_raw = [st(2304 + T * j, T) for j in range(2)]
        b_reset = st(4352, T)
        OUT_W = (12, 13, 14, 15, 8, 9, 0, 1)

        def over(name, at, dt=F32):
            return nc.alloc_sbuf_tensor_at(name, [P, T], dt, offset=at)[:, :]

        row = 4 * T
        out_w_raw = [slot(s) for s in OUT_W]
        out_w_lo = [over(f"out_w_lo{k}", slots_at + row * s, F32R) for k, s in enumerate(OUT_W)]
        out_w_hi = [over(f"out_w_hi{k}", (stage_at if k < 4 else slots_at) + row * k, F32R) for k in range(KT)]
        gate_w = [slot(4 + i) for i in range(4)]
        ones2 = st(4 * T, P)
        merged_hi = [hn_hi[:, i, :] for i in range(2)]
        merged_lo = [hn_lo[:, i, :] for i in range(2)]
        xr = [over(f"xr{i}", hn_hi_at + row * (2 + i)) for i in range(4)]
        final_g = over("final_gain", hn_hi_at + row * 6)
        fin_tmp = over("fin_tmp", hn_hi_at + row * 7)
        fin_squares = over("fin_squares", hn_lo_at + row * 2)

        block = ctx.enter_context(nc.Block())

        @block.sync
        def _(sp):
            sp.dma_start(par[:, :], ins["params"]).then_inc(s_params_landed, 16)
            for i in range(NT // 2):
                sp.dma_start(slot(MERGED + i), x_d[0, i * P:(i + 1) * P, :]).then_inc(s_x_landed[i], 16)
            for k in range(KT):
                if k >= 4:
                    sp.wait_ge(s_mod_acc, k - 3)
                sp.dma_start(w_mod[k % 4], w_mod_d[0, k * P:(k + 1) * P, 0:2 * D]).then_inc(
                    s_w_mod_landed[k % 4], 16)
            for i in range(NT // 2, NT):
                sp.dma_start(slot(MERGED + i), x_d[0, i * P:(i + 1) * P, :]).then_inc(s_x_landed[i], 16)
            merge = 0
            for bi, ct in enumerate(BULK):
                if bi == 1:
                    for src, dst in ((ins["tables"][:, P:], tab[:, P:]), (ins["wa2"], wa2[:, :]),
                                     (ins["reset64"], reset)):
                        sp.dma_start(dst, src).then_inc(s_tables_landed, 16)
                    sp.wait_ge(s_lru_w_zero, 1)
                    for g, name in enumerate(("lru_wa", "lru_wx")):
                        for q in range(4):
                            j, r = q // 2, slice(64 * (q % 2), 64 * (q % 2) + 64)
                            sp.dma_start(lru_w[r, 2 * g + j, r], ins[name][0, q, :, :]).then_inc(
                                s_lru_w_landed, 16)
                for p in range(2):
                    if bi >= 1:
                        sp.wait_ge(s_w_lo_ready, 2 * bi + p - 1)
                    src = w_in_d[0, p * 512:(p + 1) * 512, ct * P:(ct + 1) * P]
                    sp.dma_start(w_raw[p][:, :, :], src.rearrange("(k p) c -> p k c", p=P)).then_inc(
                        s_w_landed[p], 16)
                if ct >= MG:
                    b, m = MERGE_TILES[merge]
                    if merge >= 2:
                        sp.wait_ge(s_br_done, 2 * (merge - 1))
                    src = w_branch_d[0, b, :, m * P:(m + 1) * P]
                    sp.dma_start(w_branch[merge % 2][:, :, :], src.rearrange("(k p) c -> p k c", p=P)).then_inc(
                        s_w_branch_landed[merge % 2], 16)
                    merge += 1

        @block.gpsimd
        def _(pool):
            nc.gpsimd.memset(lru_w[:, :, :], 0.0).then_inc(s_lru_w_zero, 1)
            def split_out_w(k):
                pool.wait_ge(s_x_landed[k], 32)
                if k < 4:
                    pool.wait_ge(s_y_ready[1], 4)
                else:
                    pool.wait_ge(s_gate_acc, 8)
                nc.gpsimd.tensor_copy(out_w_hi[k], out_w_raw[k]).then_inc(s_pool_step, 1)
                pool.wait_ge(s_pool_step, after(s_pool_step))
                nc.gpsimd.tensor_tensor(out_w_lo[k], out_w_raw[k], out_w_hi[k].bitcast(F32), ALU.subtract).then_inc(s_out_w_ready, 1)

            for bi in range(len(BULK)):
                if bi == 1:
                    for u in range(1, 16, 2):
                        o = (slice(None), u % 8, slice((u // 8) * HALF, (u // 8 + 1) * HALF))
                        pool.wait_ge(s_hn_hi_ready, u + 1)
                        nc.gpsimd.tensor_tensor(hn_lo[o], hn_f32[u % 4], hn_hi[o].bitcast(F32), ALU.subtract).then_inc(s_hn_odd_ready, 1)
                for p in range(2):
                    pool.wait_ge(s_w_landed[p], 16 * (bi + 1))
                    if bi >= 1:
                        if p == 0:
                            pool.wait_ge(s_w_first_used, bi)
                        else:
                            pool.wait_ge(s_proj_done, 2 * bi)
                    nc.gpsimd.tensor_copy(w_hi[p][:, :, :], w_raw[p][:, :, :]).then_inc(s_w_hi_ready, 1)
                    pool.wait_ge(s_w_hi_ready, after(s_w_hi_ready))
                    nc.gpsimd.tensor_tensor(w_lo[p][:, :, :], w_raw[p][:, :, :],
                                            w_hi[p][:, :, :].bitcast(F32), ALU.subtract).then_inc(s_w_lo_ready, 1)

                if bi > len(BULK) - KT:
                    split_out_w(bi - (len(BULK) - KT) - 1)
                if BULK_AT[MG + 8 * 3 + 5] <= bi < BULK_AT[MG + 8 * 3 + 5] + 2:
                    j = bi - BULK_AT[MG + 8 * 3 + 5]
                    pool.wait_ge(s_ret_norm_ready, 2 * j + 2)
                    nc.gpsimd.tensor_tensor(slot(18 + j), slot(18 + j), slot(16 + j), ALU.mult).then_inc(s_pool_step, 1)
                    pool.wait_ge(s_pool_step, after(s_pool_step))
                    nc.gpsimd.tensor_scalar(slot(18 + j), slot(18 + j), pc("ret_g", j), None, ALU.mult)\
                        .then_inc(s_pool_step, 1)
                    pool.wait_ge(s_pool_step, after(s_pool_step))
                    pool.wait_ge(s_evac, 2 * (BULK_AT[CG] + j + 1))
                    nc.gpsimd.tensor_tensor(slot(6 + j), slot(18 + j), slot(6 + j), ALU.mult).then_inc(s_y_ready[2], 1)
            split_out_w(KT - 1)

        @block.tensor
        def _(pe):
            mm = pe.matmul
            state = {"bi": 0, "merge": 0, "piece": 0, "turned": 0, "after_merge": False}


            def project(count):
                for _ in range(count):
                    bi = state["bi"]
                    ct = BULK[bi]
                    banks = (0, 1) if bi % 2 == 0 else (2, 3)
                    if state["after_merge"]:
                        pe.wait_ge(s_merged, 2 * state["merge"])
                        pe.wait_ge(s_evac, 2 * bi)
                        state["after_merge"] = False
                    elif bi >= 2:
                        pe.wait_ge(s_evac, 2 * bi - 2)
                        if BULK[bi - 2] in TIME_MAJOR:
                            pe.wait_ge(s_tm_ready, 2 * state["turned"])
                    stream(bi, ct, banks)

            def turn_tile(ct):
                bi = BULK_AT[ct]
                for n in range(2):
                    pe.wait_ge(s_evac, 2 * bi + n + 1)
                    for i4 in range(4):
                        last = pe.transpose(bank[(0 if bi % 2 == 0 else 2) + n][:, i4 * P:(i4 + 1) * P],
                                            slot(PROJ[ct])[:, n * HALF + i4 * P:n * HALF + (i4 + 1) * P], ident)
                    last.then_inc(s_tm_turned, 1)
                state["turned"] += 1

            def stream(bi, ct, banks, parts=(0, 1, 2, 3), ks=(0, 1, 2, 3)):
                for p in range(2):
                    for n in range(2):
                        if 2 * p + n not in parts:
                            continue
                        if (n == 0 or bi == 0) and 0 in ks:
                            pe.wait_ge(s_w_lo_ready, 2 * bi + p + 1)
                        if bi == 0:
                            pe.wait_ge(s_hn_even_ready, 4 * n + 2 * (p + 1))
                            pe.wait_ge(s_hn_odd_ready, 4 * n + 2 * (p + 1))
                        o = bank[banks[n]][:, :]
                        for k4 in ks:
                            k = 4 * p + k4
                            for q, (h, w) in enumerate(((hn_hi, w_hi), (hn_lo, w_hi), (hn_hi, w_lo))):
                                last = mm(o, w[p][:, k4, :], h[:, k, n * HALF:(n + 1) * HALF],
                                          start=(p == 0 and k4 == 0 and q == 0), stop=(p == 1 and k4 == 3 and q == 2))
                        if 3 not in ks:
                            continue
                        if p == 1:
                            last.then_inc(s_proj_done, 1)
                        elif n == 1:
                            last.then_inc(s_w_first_used, 1)
                if 3 in parts and 3 in ks:
                    state["bi"] += 1

            def project_part(part):
                bi = state["bi"]
                if part == 0:
                    pe.wait_ge(s_evac, 2 * bi - 2)
                    if BULK[bi - 2] in TIME_MAJOR:
                        pe.wait_ge(s_tm_ready, 4)
                stream(bi, BULK[bi], (0, 1) if bi % 2 == 0 else (2, 3), (part,))

            def fill(count):
                for _ in range(count):
                    merge_piece(state["piece"] % 10)
                    state["piece"] += 1

            def merge_piece(piece):
                bi, mi = state["bi"], state["merge"]
                if piece < 8:
                    if piece == 0:
                        pe.wait_ge(s_evac, 2 * bi)
                    stream(bi, BULK[bi], (0, 1), (piece // 2,), (0, 1) if piece % 2 == 0 else (2, 3))
                    return
                b, m = MERGE_TILES[mi]
                n, y = piece - 8, Y_SLOT[b]
                if n == 0:
                    pe.wait_ge(s_w_branch_landed[mi % 2], 16 * (mi // 2 + 1))
                pe.wait_ge(s_y_ready[b], 2 * (n + 1) if b == 1 else 2)
                if mi:
                    pe.wait_ge(s_merged, 2 * mi - 1 + n)
                for k in range(2):
                    last = mm(bank[2 + n][:, :], w_branch[mi % 2][:, k, :], slot(y + k)[:, n * HALF:(n + 1) * HALF],
                              start=(k == 0), stop=(k == 1))
                last.then_inc(s_br_done, 1)
                if n == 1:
                    state["merge"] += 1
                    state["after_merge"] = True

            pe.wait_ge(s_ident_landed, 16)
            for u in range(16):
                n, k = u // 8, u % 8
                if u >= 4:
                    pe.wait_ge(s_hn_f32_ready, u - 3)
                if u == 14:
                    stream(0, BULK[0], (0, 1), (0,))
                    stream(0, BULK[0], (0, 1), (2,))
                if k == 0:
                    pe.wait_ge(s_xn_ready, 4 * (n + 1))
                for i4 in range(4):
                    last = pe.transpose(bank[4 + u % 4][:, i4 * P:(i4 + 1) * P],
                                        slot(MERGED + 4 * n + i4)[:, k * P:(k + 1) * P], ident)
                last.then_inc(s_xn_turned, 1)
                if u == 3:
                    pe.wait_ge(s_ones_ready, 1)
                    for m in range(16):
                        if m % 8 == 0:
                            pe.wait_ge(s_mod_acc, KT + m // 8)
                        last = mm(bank[0][:, m:m + 1], acc[:, m * P:(m + 1) * P], ones, start=True, stop=True)
                    last.then_inc(s_mod_done, 1)
                    pe.wait_ge(s_mod_read, 2)
            stream(0, BULK[0], (0, 1), (1,))
            stream(0, BULK[0], (0, 1), (3,))
            project(3)
            pe.wait_ge(s_tables_landed, TAB_DMAS)
            pe.wait_ge(s_lru_w_landed, 128)
            for j in range(2):
                pe.wait_ge(s_conv_ready, j + 1)
                for g in range(2):
                    for n in range(2):
                        q = 4 + 2 * g + n
                        pe.wait_ge(s_hn_f32_ready, 16)
                        if j:
                            pe.wait_ge(s_gates_ready, 2 * g + n + 1)
                        mm(bank[q][:, :], lru_w[:, 2 * g + j, :], slot(4 + j)[:, n * HALF:(n + 1) * HALF],
                           start=True, stop=True).then_inc(s_gates_done, 1)
            project(8)
            pe.wait_ge(s_a_tanh, 1)
            for j in range(2):
                for g in range(2):
                    for n in range(2):
                        if j == 0:
                            pe.wait_ge(s_gates_ready, 4 + 2 * g + n + 1)
                        else:
                            pe.wait_ge(s_gates_ready, 8 + 2 * g + n + 1)
                        r = slice(64 * g, 64 * g + 64)
                        mm(bank[4 + 2 * g + n][:, :], wa2[r, j * P:(j + 1) * P],
                           slot(16)[r, n * HALF:(n + 1) * HALF], start=True, stop=True).then_inc(s_gates_done, 1)
            project(1)

            def head_sums(src, turn):
                for j in range(2):
                    pe.wait_ge(s_squares, 2 * turn + j + 1)
                    for n in range(2):
                        mm(bank[4 + 2 * j + n][:, :], blockones,
                           slot(src + j)[:, n * HALF:(n + 1) * HALF], start=True, stop=True).then_inc(s_head_sums, 1)

            pe.wait_ge(s_gates_ready, 16)
            head_sums(18, 0)
            project(1)
            pe.wait_ge(s_roots, 4)
            for q in range(2):
                for n in range(2):
                    pe.wait_ge(s_evac, 2 * (BULK_AT[CK] + 1))
                    mm(bank[4 + 2 * q + n][:, :], tb("perm"), slot(20 + q)[:, n * HALF:(n + 1) * HALF],
                       start=True, stop=True).then_inc(s_rot_done, 1)
            project(1)
            turn_tile(CV)
            pe.wait_ge(s_kz_ready, 1)
            for n in range(2):
                for i4 in range(4):
                    i = 4 * n + i4
                    last = pe.transpose(bank[4 + n][:, i4 * P:(i4 + 1) * P], slot(17)[:, i * P:(i + 1) * P], ident)
                last.then_inc(s_kz_turned, 1)
            turn_tile(CV + 1)
            pe.wait_ge(s_tm_ready, 4)
            v_c = pair(22).rearrange("p a t -> p (a t)").rearrange("p (i c) -> p i c", i=NT)
            pe.wait_ge(s_kz_tm_ready, 2)
            pe.wait_ge(s_ret_r_ready, 1)
            def ret_scores(i):
                pe.wait_ge(s_ret_q_ready, i + 1)
                if i >= 2:
                    pe.wait_ge(s_ret_p_ready, i - 1)
                mm(bank[5 + i % 2][:, :], slot(21)[:, i * P:(i + 1) * P], ret_q[i % 2], start=True, stop=True).then_inc(s_ret_s_done, 1)

            ret_scores(0)
            for i in range(NT):
                ts = slice(i * P, (i + 1) * P)
                if i + 1 < NT:
                    ret_scores(i + 1)
                mm(bank[4][:, 0:256], kz_tm[:, i, :], v_c[:, i, :], start=True, stop=True).then_inc(s_ret_kv_done, 1)
                project_part(i % 4)
                pe.wait_ge(s_ret_p_ready, i + 1)
                if i:
                    pe.wait_ge(s_ret_o_ready, i)
                    pe.wait_ge(s_ret_r_ready, i + 1)
                for j in range(2):
                    mm(bank[7][:, j * P:(j + 1) * P], ret_r[:, j * P:(j + 1) * P], slot(16)[:, ts], start=True,
                       stop=False, skip_group_check=True)
                    for h in (2 * j, 2 * j + 1):
                        last = mm(bank[7][64 * (h % 2):64 * (h % 2) + 64, j * P:(j + 1) * P],
                                  v_c[:, i, 64 * h:64 * h + 64], ret_p[i % 2][:, h, :], start=False, stop=True,
                                  skip_group_check=True)
                last.then_inc(s_ret_o_done, 1)
            fill(2)
            head_sums(16, 1)
            fill(2)

            pe.wait_ge(s_roots, 8)

            def turn(o, src):
                return pe.transpose(o, src, ident)

            def rwkv_products(i):
                ts = slice(i * P, (i + 1) * P)
                if i:
                    pe.wait_ge(s_a_y_ready, 2 * i)
                    pe.wait_ge(s_a_g_ready, 4 * i)
                pe.wait_ge(s_a_ends_ready, i + 1)
                turn(bank[4][:, 0:128], slot(12)[:, ts])
                turn(bank[4][:, 128:256], slot(13)[:, ts])
                for j in range(2):
                    turn(bank[4][:, 256 + j * P:384 + j * P], a_r[:, 2 * j:2 * j + 2, 0, :])
                turn(bank[5][:, 0:128], b_end[:, 0:2, :]).then_inc(s_a_tm1_done, 1)
                turn(bank[5][:, 128:256], b_end[:, 2:4, :])
                turn(bank[5][:, 256:384], k_end[:, 0:2, :])
                turn(bank[5][:, 384:512], k_end[:, 2:4, :]).then_inc(s_a_tm2_done, 1)
                for par in range(2):
                    r = slice(64 * par, 64 * par + 64)
                    for a, src in enumerate((b_hat, k_hat)):
                        for j in range(2):
                            for c in range(2):
                                last = mm(bank[6 + par][64 * c:64 * c + 64, (2 * a + j) * P:(2 * a + j + 1) * P],
                                          src[r, 2 * j + c, :], a_r[r, 2 * j + c, :, :], start=True, stop=True)
                    last.then_inc(s_a_m_done, 1)
                fill(2 if i else 0)
                pe.wait_ge(s_a_tm_ready, 2 * i + 2)
                for par in range(2):
                    r = slice(64 * par, 64 * par + 64)
                    for j in range(2):
                        for c in range(2):
                            last = mm(bank[4 + par][64 * c:64 * c + 64, j * C:(j + 1) * C], a_r[r, 2 * j + c, 0, :],
                                      b_hat[r, 2 * j + c, :], start=True, stop=True)
                    last.then_inc(s_a_a_done, 1)
                fill(1)

            def each(f):
                for h in range(4):
                    for c in range(2):
                        last = f(h, slice(64 * c, 64 * c + 64), c)
                return last

            def rwkv_inverse(i):
                for l in range(1, 6):
                    pe.wait_ge(s_a_x_ready, 6 * i + l)
                    each(lambda h, r, c: mm(bank[5][r, h * C:(h + 1) * C], m13(h)[r, 0:C], xx[r, 0, h, :], start=True, stop=True)).then_inc(s_a_v_done, 1)
                    fill(1 if i or l > 1 else 0)
                    pe.wait_ge(s_a_v_ready, 5 * i + l)
                    if l < 5:
                        each(lambda h, r, c: mm(bank[6][r, h * C:(h + 1) * C], xx[r, 1, h, :], v_lev[r, h, :],
                                                start=True, stop=True))
                    each(lambda h, r, c: mm(bank[6][r, 256 + h * C:256 + (h + 1) * C], v_lev[r, h, :], xx[r, 1, h, :], start=True, stop=True)).then_inc(s_a_dx_done, 1)
                    fill(0 if l == 5 or (i == 0 and l == 1) else 1)
                each(lambda h, r, c: mm(bank[4][r, h * C:(h + 1) * C], m24(h)[r, 0:C], tm1[r, h * C:(h + 1) * C], start=True, stop=True)).then_inc(s_a_p_done, 1)
                pe.wait_ge(s_a_x_ready, 6 * i + 6)
                each(lambda h, r, c: mm(bank[6 + c][64 * (h % 2):64 * (h % 2) + 64, (h // 2) * C:(h // 2 + 1) * C], tm1[r, 256 + h * C:256 + (h + 1) * C], xx[r, 1, h, :], start=True, stop=True)).then_inc(s_a_w_done, 1)
                fill(1)
                pe.wait_ge(s_a_p_ready, i + 1)
                each(lambda h, r, c: mm(bank[5][r, h * C:(h + 1) * C], xx[r, 1, h, :], p_sb[r, h * C:(h + 1) * C], start=True, stop=True)).then_inc(s_a_u_done, 1)

            def rwkv_chunk(i, c):
                n = 2 * i + c
                rc = slice(64 * c, 64 * c + 64)
                pe.wait_ge(s_a_w_ready, 2 * i + 2)
                if n:
                    pe.wait_ge(s_a_g_ready, 2 * n)
                else:
                    pe.wait_ge(s_a_g_zero, 1)
                for h in range(4):
                    r = slice(64 * (h % 2), 64 * (h % 2) + 64)
                    last = mm(bank[6 + h % 2][rc, (h // 2) * C:(h // 2 + 1) * C],
                              w_t[r, c * P + (h // 2) * C:c * P + (h // 2 + 1) * C],
                              G[r, (h // 2) * C:(h // 2 + 1) * C], start=True, stop=True)
                last.then_inc(s_a_wg_done, 1)
                if n:
                    pe.wait_ge(s_a_y_ready, n)
                for h in range(4):
                    r = slice(64 * (h % 2), 64 * (h % 2) + 64)
                    last = mm(bank[4][r, (h // 2) * C:(h // 2 + 1) * C], G[r, (h // 2) * C:(h // 2 + 1) * C],
                              a_r[r, 2 * (h // 2) + c, 1, :], start=True, stop=True)
                last.then_inc(s_a_y_done, 1)
                fill(1)
                pe.wait_ge(s_a_sa_ready, 2 * n + 2)
                for h in range(4):
                    r = slice(64 * (h % 2), 64 * (h % 2) + 64)
                    hc = slice(h * C, (h + 1) * C)
                    o = bank[6][r, 256 + (h // 2) * C:256 + (h // 2 + 1) * C]
                    mm(o, u_sb[rc, hc], m13(h)[rc, C:2 * C], start=True, stop=False, skip_group_check=True)
                    last = mm(o, tm1[rc, hc], m24(h)[rc, C:2 * C], start=False, stop=True, skip_group_check=True)
                last.then_inc(s_a_y_done, 1)
                for h in range(4):
                    r = slice(64 * (h % 2), 64 * (h % 2) + 64)
                    hc = slice(h * C, (h + 1) * C)
                    o = bank[5][r, (h // 2) * C:(h // 2 + 1) * C]
                    mm(o, tm2[rc, hc], u_sb[rc, hc], start=True, stop=False, skip_group_check=True)
                    last = mm(o, tm2[rc, 256 + h * C:256 + (h + 1) * C], tm1[rc, hc], start=False, stop=True,
                              skip_group_check=True)
                last.then_inc(s_a_gnew_done, 1)
                fill(1 if c == 0 else 4)

            for i in range(NT):
                rwkv_products(i)
                rwkv_inverse(i)
                rwkv_chunk(i, 0)
                rwkv_chunk(i, 1)
            project(4)
            pe.wait_ge(s_a_y_ready, 16)
            pe.wait_ge(s_a_g_ready, 32)
            for j in range(2):
                for n in range(2):
                    mm(bank[4 + 2 * j + n][:, :], blockones, slot(4 + j)[:, n * HALF:(n + 1) * HALF],
                       start=True, stop=True).then_inc(s_a_mean_done, 1)
            project(1)
            head_sums(6, 2)
            project(1)
            turn_tile(BI)
            for j in range(2):
                pe.wait_ge(s_a_rk_ready, j + 1)
                for n in range(2):
                    pe.wait_ge(s_roots, 8 + 2 * j + n + 1)
                    mm(bank[4 + 2 * j + n][:, :], blockones, slot(8 + j)[:, n * HALF:(n + 1) * HALF],
                       start=True, stop=True).then_inc(s_a_bonus_done, 1)
            turn_tile(BI + 1)
            project(4)

            v_b = pair(8).rearrange("p a t -> p (a t)").rearrange("p (i c) -> p i c", i=NT)
            pe.wait_ge(s_a_bonus_read, 4)
            pe.wait_ge(s_evac, 2 * state["bi"])
            pe.wait_ge(s_tm_ready, 8)
            for i in range(NT):
                ts = slice(i * P, (i + 1) * P)
                pe.wait_ge(s_b_z_ready, i + 1)
                if i:
                    pe.wait_ge(s_b_o_ready, i)
                    pe.wait_ge(s_b_s_ready, 2 * i + 1)
                    pe.wait_ge(s_b_p_ready, i)
                turn(bank[6][:, 0:128], dz[:, 8, 0, :])
                turn(bank[6][:, 128:256], dz[:, 8, 1, :])
                for hh in range(2):
                    r = slice(64 * hh, 64 * hh + 64)
                    for j in range(2):
                        mm(bank[4 + hh][0:64, 384 + j * 64:448 + j * 64], dz[r, 0, j, 0:64], dz[r, 0, j, 64:128],
                           start=True, stop=True)
                        for nb in (0, 2):
                            mm(bank[6 + hh][32 * nb:32 * nb + 32, 256 + j * 32:288 + j * 32],
                               dz[r, 1, j, 32 * nb:32 * nb + 32], dz[r, 1, j, 32 * nb + 32:32 * nb + 64],
                               start=True, stop=True, tile_position=(64 * hh, 32 * nb))
                        for l in range(NLOW):
                            for nb in range(4):
                                if l < 5:
                                    z = dz[r, 2 + l, j, 32 * nb:32 * nb + 32]
                                    lhs, rhs = z, z
                                else:
                                    cs = slice(i * P + 32 * nb, i * P + 32 * nb + 32)
                                    lhs, rhs = slot(12 + j)[r, cs], slot(0 + j)[r, cs]
                                c0 = j * 192 + l * 32
                                last = mm(bank[4 + hh][32 * nb:32 * nb + 32, c0:c0 + 32], lhs, rhs, start=True,
                                          stop=True, tile_position=(64 * hh, 32 * nb))
                    last.then_inc(s_b_scores_done, 1)
                fill(3)
                pe.wait_ge(s_b_p_ready, i + 1)
                pe.wait_ge(s_b_s_ready, 2 * i + 1)
                for h in range(4):
                    j, r = h // 2, slice(64 * (h % 2), 64 * (h % 2) + 64)
                    hc = slice(64 * h, 64 * h + 64)

                    def o(a, b):
                        return bank[7][r, j * P + a:j * P + b]

                    mm(o(0, 128), h_s[r, j * 64:j * 64 + 64], h_qe[r, j, :], start=True, stop=False,
                       skip_group_check=True)
                    last = mm(o(0, 128), v_b[:, i, hc], h_p[:, h, :], start=False, stop=True, skip_group_check=True)
                last.then_inc(s_b_o_done, 1)
                pe.wait_ge(s_b_ke_ready, i + 1)
                for h in range(4):
                    j, r = h // 2, slice(64 * (h % 2), 64 * (h % 2) + 64)
                    hc = slice(64 * h, 64 * h + 64)
                    last = mm(bank[6][r, 384 + j * 64:448 + j * 64], ke_tm[:, hc], v_b[:, i, hc], start=True, stop=True)
                last.then_inc(s_b_snew_done, 1)
                fill(7 if i + 1 < NT else 4)
            pe.wait_ge(s_b_s_ready, 17)
            for n in range(2):
                for j in range(2):
                    pe.wait_ge(s_squares, 6 + 2 * n + j + 1)
                    mm(bank[4 + 2 * j + n][:, :], blockones, slot(12 + j)[:, n * HALF:(n + 1) * HALF],
                       start=True, stop=True).then_inc(s_head_sums, 1)
            fill(83)
            pe.wait_ge(s_gate_acc, 8)
            pe.wait_ge(s_roots, 16)
            pe.wait_ge(s_ones2_ready, 1)
            for n in range(2):
                mm(bank[4 + n][:, :], ones2, slot(3)[:, n * HALF:(n + 1) * HALF], start=True, stop=True).then_inc(s_gate_done, 1)
            pe.wait_ge(s_out_w_ready, KT)
            pe.wait_ge(s_gate_read, 2)
            for tt in range(NT):
                for n in range(2):
                    bk = bank[(2 * tt + n) % 8]
                    if tt >= 4:
                        pe.wait_ge(s_out_read, 2 * (tt - 4) + n + 1)
                    if n == 0:
                        pe.wait_ge(s_merged_lo_ready, tt + 1)
                    for k in range(KT):
                        for q, (m, w) in enumerate(((merged_hi, out_w_hi), (merged_lo, out_w_hi),
                                                    (merged_hi, out_w_lo))):
                            last = mm(bk[:, :], m[tt % 2][:, k * P:(k + 1) * P],
                                      w[k][:, n * HALF:(n + 1) * HALF], start=(k == 0 and q == 0),
                                      stop=(k == KT - 1 and q == 2))
                    last.then_inc(s_out_done, 1)

        @block.scalar
        def _(act):
            act.dma_start(ident, ins["tables"][:, 0:P]).then_inc(s_ident_landed, 16)



            def halves(n):
                return slice(n * HALF, (n + 1) * HALF)

            act.wait_ge(s_params_landed, 16)
            nc.scalar.activation(cond, pcs("c"), ACT.Silu).then_inc(s_cond_ready, 1)
            act.wait_ge(s_cond_ready, after(s_cond_ready))

            def squares_of_x(n):
                for i in range(4 * n, 4 * n + 4):
                    act.wait_ge(s_x_landed[i], 16)
                    nc.scalar.activation(scratch, slot(MERGED + i), ACT.Square, accum_out=ssq[:, i:i + 1])\
                        .then_inc(s_x_squares, 1)
                    act.wait_ge(s_x_squares, after(s_x_squares))
                half = slice(4 * n, 4 * n + 4)
                nc.scalar.activation(rs[:, half], ssq[:, half], ACT.Sqrt, scale=1.0 / D, bias=pc("eps"))\
                    .then_inc(s_x_rms, 1)
                act.wait_ge(s_x_rms, after(s_x_rms))

            def normalise_x(n):
                act.wait_ge(s_rs_ready, n + 1)
                for i in range(4 * n, 4 * n + 4):
                    nc.scalar.activation(slot(MERGED + i), slot(MERGED + i), ACT.Copy, scale=rs[:, i:i + 1])\
                        .then_inc(s_xn_ready, 1)
                    act.wait_ge(s_xn_ready, after(s_xn_ready))

            squares_of_x(0)
            normalise_x(0)
            squares_of_x(1)
            normalise_x(1)
            for u in range(16):
                n, k = u // 8, u % 8
                act.wait_ge(s_hn_f32_ready, u + 1)
                nc.scalar.activation(hn_hi[:, k, halves(n)], hn_f32[u % 4], ACT.Copy).then_inc(s_hn_hi_ready, 1)
                act.wait_ge(s_hn_hi_ready, after(s_hn_hi_ready))
            act.wait_ge(s_lam_abs, 1)
            nc.scalar.activation(sc2, sc1, ACT.Exp, scale=-1.0).then_inc(s_lam_exp, 1)
            act.wait_ge(s_lam_exp, after(s_lam_exp))
            act.wait_ge(s_lb_shifted, 1)
            nc.scalar.activation(lball, sc4, ACT.Exp).then_inc(s_lb_exp, 1)
            act.wait_ge(s_lb_exp, after(s_lb_exp))

            state = {"bi": 0, "merge": 0}

            def evac(count):
                for _ in range(count):
                    bi = state["bi"]
                    ct = BULK[bi]
                    banks = (0, 1) if bi % 2 == 0 else (2, 3)
                    for n in range(2):
                        act.wait_ge(s_proj_done, 2 * bi + n + 1)
                        src = bank[banks[n]][:, :]
                        if ct in (BF, BF + 1):
                            nc.scalar.activation(b_f_raw[ct - BF][:, halves(n)], src, ACT.Copy).then_inc(s_evac, 1)
                            act.wait_ge(s_evac, after(s_evac))
                        else:
                            nc.scalar.activation(slot(PROJ[ct])[:, halves(n)], src,
                                                 ACT.Silu if ct in GATED else ACT.Copy).then_inc(s_evac, 1)
                            act.wait_ge(s_evac, after(s_evac))
                    state["bi"] += 1

            def evac_turned(ct, turned):
                bi = BULK_AT[ct]
                s0, j = TIME_MAJOR[ct]
                dst = pair(s0).rearrange("p a t -> p (a t)").rearrange("p (i c) -> p i c", i=NT)
                for n in range(2):
                    act.wait_ge(s_tm_turned, 2 * turned + n + 1)
                    nc.scalar.activation(dst[:, 4 * n:4 * n + 4, j * P:(j + 1) * P],
                                         bank[(0 if bi % 2 == 0 else 2) + n][:, :].rearrange("p (i c) -> p i c", c=P),
                                         ACT.Copy).then_inc(s_tm_ready, 1)
                    act.wait_ge(s_tm_ready, after(s_tm_ready))

            def merge_gate():
                bi, mi = state["bi"], state["merge"]
                for n in range(2):
                    act.wait_ge(s_proj_done, 2 * bi + n + 1)
                    if mi:
                        act.wait_ge(s_merged, 2 * (mi - 1) + n + 1)
                    nc.scalar.activation(sig[n], bank[n][:, :], ACT.Sigmoid).then_inc(s_evac, 1)
                    act.wait_ge(s_evac, after(s_evac))
                state["bi"] += 1
                state["merge"] += 1

            act.wait_ge(s_mod_read, 2)
            evac(4)
            for j in range(2):
                for g, bias in enumerate(("ba", "bx")):
                    for n in range(2):
                        act.wait_ge(s_gates_done, 4 * j + 2 * g + n + 1)
                        dst = slot(j) if g == 0 else slot(14 + j)
                        nc.scalar.activation(dst[:, halves(n)], bank[4 + 2 * g + n][:, :], ACT.Sigmoid,
                                             bias=pc(bias, j)).then_inc(s_gates_ready, 1)
                        act.wait_ge(s_gates_ready, after(s_gates_ready))
            for j in range(2):
                act.wait_ge(s_lru_y8_ready, j + 1)
                nc.scalar.activation(slot(6 + j), slot(j), ACT.Tanh).then_inc(s_lru_t, 1)
                act.wait_ge(s_lru_t, after(s_lru_t))
                nc.scalar.activation(slot(j), slot(j), ACT.Exp, scale=-1.0).then_inc(s_lru_a, 1)
                act.wait_ge(s_lru_a, after(s_lru_a))
            for j in range(2):
                act.wait_ge(s_lru_q_ready, j + 1)
                nc.scalar.activation(slot(6 + j), slot(6 + j), ACT.Sqrt, scale=2.0).then_inc(s_lru_mult, 1)
                act.wait_ge(s_lru_mult, after(s_lru_mult))
            evac(7)
            act.wait_ge(s_a_mixed, 7)
            nc.scalar.activation(slot(16)[0:64, :], slot(16)[0:64, :], ACT.Tanh).then_inc(s_a_tanh, 1)
            act.wait_ge(s_a_tanh, after(s_a_tanh))
            evac(1)
            act.wait_ge(s_y_ready[3], 2)
            for j in range(2):
                for g, bias in enumerate(("w0", "a0")):
                    for n in range(2):
                        act.wait_ge(s_gates_done, 8 + 4 * j + 2 * g + n + 1)
                        dst = slot(j) if g == 0 else slot(14 + j)
                        nc.scalar.activation(dst[:, halves(n)], bank[4 + 2 * g + n][:, :], ACT.Sigmoid,
                                             bias=pc(bias, j)).then_inc(s_gates_ready, 1)
                        act.wait_ge(s_gates_ready, after(s_gates_ready))
            for j in range(2):
                act.wait_ge(s_a_kk_ready, j + 1)
                nc.scalar.activation(slot(18 + j), slot(4 + j), ACT.Square).then_inc(s_squares, 1)
                act.wait_ge(s_squares, after(s_squares))
            act.dma_start(slot(16), ins["cos"]).then_inc(s_cos_landed, 16)
            act.dma_start(slot(17), ins["sin"]).then_inc(s_sin_landed, 16)
            evac(1)
            for j in range(2):
                for n in range(2):
                    act.wait_ge(s_head_sums, 2 * j + n + 1)
                    nc.scalar.activation(slot(18 + j)[:, halves(n)], bank[4 + 2 * j + n][:, :], ACT.Sqrt)\
                        .then_inc(s_roots, 1)
                    act.wait_ge(s_roots, after(s_roots))
            evac(2)
            act.wait_ge(s_a_b_ready, 2)
            evac_turned(CV, 0)
            for n in range(2):
                act.wait_ge(s_kz_turned, n + 1)
                nc.scalar.activation(kz_tm[:, 4 * n:4 * n + 4, :],
                                     bank[4 + n][:, :].rearrange("p (i c) -> p i c", c=P), ACT.Copy)\
                    .then_inc(s_kz_tm_ready, 1)
                act.wait_ge(s_kz_tm_ready, after(s_kz_tm_ready))
            evac_turned(CV + 1, 1)
            for i in range(NT):
                act.wait_ge(s_ret_o_done, i + 1)
                nc.scalar.activation(pair(18)[:, :, i * P:(i + 1) * P],
                                     bank[7][:, 0:256].rearrange("p (j t) -> p j t", j=2), ACT.Copy)\
                    .then_inc(s_ret_o_ready, 1)
                act.wait_ge(s_ret_o_ready, after(s_ret_o_ready))
                if i % 4 == 3:
                    evac(1)

            def squares(src, tmp):
                for j in range(2):
                    nc.scalar.activation(slot(tmp + j), slot(src + j), ACT.Square).then_inc(s_squares, 1)
                    act.wait_ge(s_squares, after(s_squares))

            def roots(tmp, turn, scale, eps):
                for j in range(2):
                    act.wait_ge(s_head_sums, 4 * turn + 2 * j + 2)
                    for n in range(2):
                        nc.scalar.activation(slot(tmp + j)[:, halves(n)], bank[4 + 2 * j + n][:, :],
                                             ACT.Sqrt, scale=scale, bias=pc(eps)).then_inc(s_roots, 1)
                        act.wait_ge(s_roots, after(s_roots))

            def decays(i):
                ts = slice(i * P, (i + 1) * P)
                b4 = pair(0)[:, :, ts].rearrange("p j (c t) -> p j c t", t=C)
                if i:
                    act.wait_ge(s_a_g_ready, 4 * i)
                else:
                    act.wait_ge(s_a_starts_ready, 1)
                nc.scalar.activation(Ep.rearrange("p (j c) t -> p j c t", c=2)[:, :, :, 1:65], b4, ACT.Exp)\
                    .then_inc(s_a_e_ready, 1)
                act.wait_ge(s_a_e_ready, after(s_a_e_ready))
                if i:
                    act.wait_ge(s_a_y_done, 4 * i)
                nc.scalar.activation(Em.rearrange("p (j c) t -> p j c t", c=2), b4, ACT.Exp, scale=-1.0)\
                    .then_inc(s_a_e_ready, 1)
                act.wait_ge(s_a_e_ready, after(s_a_e_ready))

            squares(18, 16)
            decays(0)
            roots(16, 1, 1.0 / 64, "eps")

            for i in range(NT):
                act.wait_ge(s_a_tm1_done, i + 1)
                nc.scalar.activation(tm1, bank[4][:, :], ACT.Copy).then_inc(s_a_tm_ready, 1)
                act.wait_ge(s_a_tm_ready, after(s_a_tm_ready))
                act.wait_ge(s_a_tm2_done, i + 1)
                nc.scalar.activation(tm2, bank[5][:, :], ACT.Copy).then_inc(s_a_tm_ready, 1)
                act.wait_ge(s_a_tm_ready, after(s_a_tm_ready))
                merge_gate()
                act.wait_ge(s_a_p_done, i + 1)
                nc.scalar.activation(p_sb, bank[4][:, 0:256], ACT.Copy).then_inc(s_a_p_ready, 1)
                act.wait_ge(s_a_p_ready, after(s_a_p_ready))
                act.wait_ge(s_a_w_done, i + 1)
                for c in range(2):
                    nc.scalar.activation(w_t[:, c * P:(c + 1) * P], bank[6 + c][:, 0:P], ACT.Copy)\
                        .then_inc(s_a_w_ready, 1)
                    act.wait_ge(s_a_w_ready, after(s_a_w_ready))
                act.wait_ge(s_a_u_done, i + 1)
                nc.scalar.activation(u_sb, bank[5][:, 0:256], ACT.Copy).then_inc(s_a_u_ready, 1)
                act.wait_ge(s_a_u_ready, after(s_a_u_ready))
                for c in range(2):
                    act.wait_ge(s_a_y_done, 4 * i + 2 * c + 1)
                    nc.scalar.activation(pair(4)[:, :, i * P + c * C:i * P + (c + 1) * C],
                                         bank[4][:, 0:P].rearrange("p (j t) -> p j t", j=2), ACT.Copy)\
                        .then_inc(s_a_y_part, 1)
                    act.wait_ge(s_a_y_part, after(s_a_y_part))
                if i + 1 < NT:
                    decays(i + 1)
                merge_gate()
            act.wait_ge(s_a_y_ready, 16)
            act.wait_ge(s_a_g_ready, 32)
            evac(2)
            for j in range(2):
                nc.scalar.activation(b_f[j], b_f_raw[j], ACT.Sigmoid).then_inc(s_b_f_sig, 1)
                act.wait_ge(s_b_f_sig, after(s_b_f_sig))
            act.wait_ge(s_merged, 32)
            act.dma_start(b_reset, ins["reset128"]).then_inc(s_reset128_landed, 16)
            for j in range(2):
                act.wait_ge(s_b_f_ready, j + 1)
                nc.scalar.activation(b_f[j], b_f[j], ACT.Ln).then_inc(s_b_lnf, 1)
                act.wait_ge(s_b_lnf, after(s_b_lnf))
            evac(2)
            act.wait_ge(s_a_centred, 4)
            squares(4, 6)
            act.wait_ge(s_a_rk_ready, 2)
            evac(1)
            roots(6, 2, 1.0 / 64, "ln_eps")
            act.wait_ge(s_b_d_ready, 1)
            nc.scalar.activation(dz[:, :, :, :], dz[:, :, :, :], ACT.Exp).then_inc(s_b_e_ready, 1)
            act.wait_ge(s_b_e_ready, after(s_b_e_ready))
            evac(1)
            act.wait_ge(s_a_bonus_done, 4)
            evac_turned(BI, 2)
            evac_turned(BI + 1, 3)
            evac(2)
            for j in range(2):
                act.wait_ge(s_a_bonus_read, 2 * j + 2)
                nc.scalar.activation(slot(12 + j), b_f_raw[j], ACT.Sigmoid, scale=-1.0).then_inc(s_b_k_sig, 1)
                act.wait_ge(s_b_k_sig, after(s_b_k_sig))
            evac(2)
            for i in range(NT):
                act.wait_ge(s_b_scores_done, 2 * i + 1)
                nc.scalar.activation(ke_tm, bank[6][:, 0:256], ACT.Copy).then_inc(s_b_ke_ready, 1)
                act.wait_ge(s_b_ke_ready, after(s_b_ke_ready))
                act.wait_ge(s_b_o_done, i + 1)
                nc.scalar.activation(pair(6)[:, :, i * P:(i + 1) * P],
                                     bank[7][:, 0:256].rearrange("p (j t) -> p j t", j=2), ACT.Copy)\
                    .then_inc(s_b_o_ready, 1)
                act.wait_ge(s_b_o_ready, after(s_b_o_ready))
                if i + 1 < NT:
                    act.wait_ge(s_b_d_ready, i + 2)
                    nc.scalar.activation(dz[:, :, :, :], dz[:, :, :, :], ACT.Exp).then_inc(s_b_e_ready, 1)
                    act.wait_ge(s_b_e_ready, after(s_b_e_ready))
                    merge_gate()
            for n in range(2):
                for j in range(2):
                    nc.scalar.activation(slot(12 + j)[:, halves(n)], slot(6 + j)[:, halves(n)], ACT.Square)\
                        .then_inc(s_squares, 1)
                    act.wait_ge(s_squares, after(s_squares))
            for n in range(2):
                for j in range(2):
                    act.wait_ge(s_head_sums, 12 + 2 * n + j + 1)
                    nc.scalar.activation(slot(12 + j)[:, halves(n)], bank[4 + 2 * j + n][:, :], ACT.Sqrt,
                                         scale=1.0 / 64, bias=pc("eps")).then_inc(s_roots, 1)
                    act.wait_ge(s_roots, after(s_roots))
            merge_gate()
            act.wait_ge(s_y_ready[1], 4)
            for k in range(KT):
                if k >= 4:
                    act.wait_ge(s_gate_acc, k - 3)
                    merge_gate()
                act.dma_start(gate_w[k % 4], w_mod_d[0, k * P:(k + 1) * P, 2 * D:3 * D]).then_inc(
                    s_w_mod_landed[k % 4], 16)
                act.dma_start(out_w_raw[k], w_out_d[0, k * P:(k + 1) * P, :]).then_inc(s_x_landed[k], 16)
            act.dma_start(slot(2), ins["b_gate"].partition_broadcast(P)).then_inc(s_b_gate_landed, 16)
            for _ in range(4):
                merge_gate()
            act.dma_start(xr[0], x_d[0, 0:P, :]).then_inc(s_xr_landed[0], 16)
            act.dma_start(final_g, ins["final_g"].partition_broadcast(P)).then_inc(s_final_g_landed, 16)

            def split_merged(tt):
                if tt >= 2:
                    act.wait_ge(s_out_done, 2 * (tt - 1))
                nc.scalar.activation(merged_hi[tt % 2].rearrange("p (k t) -> p k t", t=P),
                                     slots[:, MERGED:MERGED + KT, tt * P:(tt + 1) * P], ACT.Copy)\
                    .then_inc(s_merged_hi_ready, 1)
                act.wait_ge(s_merged_hi_ready, after(s_merged_hi_ready))

            act.wait_ge(s_merged, 64)
            split_merged(0)
            split_merged(1)
            for i in range(1, 4):
                act.dma_start(xr[i], x_d[0, i * P:(i + 1) * P, :]).then_inc(s_xr_landed[i], 16)
            for tt in range(NT):
                if tt + 2 < NT:
                    split_merged(tt + 2)
                act.wait_ge(s_h_ready, 2 * tt + 2)
                nc.scalar.activation(fin_squares, xr[tt % 4], ACT.Square, accum_out=ssq2[:, tt:tt + 1])\
                    .then_inc(s_h_squares, 1)
                act.wait_ge(s_h_squares, after(s_h_squares))
                nc.scalar.activation(rs2[:, tt:tt + 1], ssq2[:, tt:tt + 1], ACT.Sqrt, scale=1.0 / D, bias=pc("eps"))\
                    .then_inc(s_h_rms, 1)
                act.wait_ge(s_h_rms, after(s_h_rms))
                act.wait_ge(s_out_ready, tt + 1)
                act.dma_start(out_d[0, tt * P:(tt + 1) * P, :], xr[tt % 4]).then_inc(s_stored[tt % 4], 16)
                if tt + 4 < NT:
                    act.wait_ge(s_stored[tt % 4], 16)
                    act.dma_start(xr[tt % 4], x_d[0, (tt + 4) * P:(tt + 5) * P, :]).then_inc(
                        s_xr_landed[tt % 4], 16)
            for i in range(4):
                act.wait_ge(s_stored[i], 32)

        @block.vector
        def _(dve):





            def halves(n):
                return slice(n * HALF, (n + 1) * HALF)

            MUL, ADD, SUB, MAX = ALU.mult, ALU.add, ALU.subtract, ALU.max
            nc.vector.memset(ones, 1.0).then_inc(s_ones_ready, 1)
            dve.wait_ge(s_ones_ready, after(s_ones_ready))
            dve.wait_ge(s_params_landed, 16)
            lam = pcs("lam")
            nc.vector.tensor_scalar(sc3, lam, -1.0, None, MUL).then_inc(s_vector_step, 1)
            dve.wait_ge(s_vector_step, after(s_vector_step))
            nc.vector.tensor_tensor(sc1, lam, sc3, MAX).then_inc(s_lam_abs, 1)
            dve.wait_ge(s_lam_abs, after(s_lam_abs))
            lb = pcs("lb")
            nc.vector.tensor_tensor(sc4, lb, lb, SUB).then_inc(s_lb_shifted, 1)
            dve.wait_ge(s_lb_shifted, after(s_lb_shifted))
            dve.wait_ge(s_x_rms, 1)
            nc.vector.reciprocal(rs[:, 0:4], rs[:, 0:4]).then_inc(s_rs_ready, 1)
            dve.wait_ge(s_rs_ready, after(s_rs_ready))
            dve.wait_ge(s_cond_ready, 1)
            for k in range(KT):
                dve.wait_ge(s_w_mod_landed[k % 4], 16 * (k // 4 + 1))
                if k == 0:
                    nc.vector.tensor_scalar(acc, w_mod[0], cond[:, 0:1], None, MUL).then_inc(s_mod_acc, 1)
                    dve.wait_ge(s_mod_acc, after(s_mod_acc))
                elif k == KT - 1:
                    for half in (slice(0, D), slice(D, 2 * D)):
                        nc.vector.scalar_tensor_tensor(out=acc[:, half], in0=w_mod[k % 4][:, half],
                                                       scalar=cond[:, k:k + 1], in1=acc[:, half], op0=MUL,
                                                       op1=ADD).then_inc(s_mod_acc, 1)
                        dve.wait_ge(s_mod_acc, after(s_mod_acc))
                else:
                    nc.vector.scalar_tensor_tensor(out=acc, in0=w_mod[k % 4], scalar=cond[:, k:k + 1],
                                                   in1=acc, op0=MUL, op1=ADD).then_inc(s_mod_acc, 1)
                    dve.wait_ge(s_mod_acc, after(s_mod_acc))
            dve.wait_ge(s_x_rms, 2)
            nc.vector.reciprocal(rs[:, 4:8], rs[:, 4:8]).then_inc(s_rs_ready, 1)
            dve.wait_ge(s_rs_ready, after(s_rs_ready))
            dve.wait_ge(s_mod_done, 1)
            b_mod = pcs("b_mod")
            nc.vector.tensor_tensor(sh, bank[0][:, 0:8], b_mod[:, 0:8], ADD).then_inc(s_mod_read, 1)
            dve.wait_ge(s_mod_read, after(s_mod_read))
            nc.vector.scalar_tensor_tensor(out=gs, in0=bank[0][:, 8:16], scalar=1.0, in1=b_mod[:, 8:16],
                                           op0=ADD, op1=ADD).then_inc(s_mod_read, 1)
            dve.wait_ge(s_mod_read, after(s_mod_read))
            nc.vector.tensor_tensor(gs, gs, pcs("norm_g"), MUL).then_inc(s_vector_step, 1)
            dve.wait_ge(s_vector_step, after(s_vector_step))
            for u in range(17):
                if u < 16:

                    dve.wait_ge(s_xn_turned, u + 1)
                    if u >= 4 and u % 2 == 0:
                        dve.wait_ge(s_hn_even_ready, (u - 4) // 2 + 1)
                    elif u >= 4:
                        dve.wait_ge(s_hn_odd_ready, (u - 4) // 2 + 1)
                    nc.vector.tensor_scalar(hn_f32[u % 4], bank[4 + u % 4][:, :], gs[:, u % 8:u % 8 + 1],
                                            sh[:, u % 8:u % 8 + 1], MUL, ADD).then_inc(s_hn_f32_ready, 1)
                    dve.wait_ge(s_hn_f32_ready, after(s_hn_f32_ready))
                if u % 2 == 1:
                    v = u - 1
                    dve.wait_ge(s_hn_hi_ready, v + 1)
                    o = (slice(None), v % 8, halves(v // 8))
                    nc.vector.tensor_tensor(hn_lo[o], hn_f32[v % 4], hn_hi[o].bitcast(F32), SUB)\
                        .then_inc(s_hn_even_ready, 1)
                    dve.wait_ge(s_hn_even_ready, after(s_hn_even_ready))
            dve.wait_ge(s_lam_exp, 1)
            nc.vector.tensor_scalar(sc1, sc2, 2.0, None, ADD).then_inc(s_vector_step, 1)
            dve.wait_ge(s_vector_step, after(s_vector_step))
            nc.vector.reciprocal(sc1, sc1).then_inc(s_vector_step, 1)
            dve.wait_ge(s_vector_step, after(s_vector_step))
            nc.vector.tensor_tensor(sc1, sc1, sc2, MUL).then_inc(s_vector_step, 1)
            dve.wait_ge(s_vector_step, after(s_vector_step))
            nc.vector.tensor_tensor(sc2, sc1, sc1, MUL).then_inc(s_vector_step, 1)
            dve.wait_ge(s_vector_step, after(s_vector_step))
            dve.wait_ge(s_lb_exp, 1)
            nc.vector.tensor_scalar(sp8, sc2, 1.0 / 17, 1.0 / 15, MUL, ADD).then_inc(s_vector_step, 1)
            dve.wait_ge(s_vector_step, after(s_vector_step))
            for q in (13, 11, 9, 7, 5, 3, 1):
                nc.vector.tensor_tensor(sp8, sp8, sc2, MUL).then_inc(s_vector_step, 1)
                dve.wait_ge(s_vector_step, after(s_vector_step))
                nc.vector.tensor_scalar(sp8, sp8, 1.0 / q, None, ADD).then_inc(s_vector_step, 1)
                dve.wait_ge(s_vector_step, after(s_vector_step))
            nc.vector.tensor_tensor(sp8, sp8, sc1, MUL).then_inc(s_vector_step, 1)
            dve.wait_ge(s_vector_step, after(s_vector_step))
            nc.vector.tensor_scalar(sc3, sc3, 0.0, None, MAX).then_inc(s_vector_step, 1)
            dve.wait_ge(s_vector_step, after(s_vector_step))
            nc.vector.scalar_tensor_tensor(out=sp8, in0=sp8, scalar=2.0, in1=sc3, op0=MUL, op1=ADD)\
                .then_inc(s_vector_step, 1)
            dve.wait_ge(s_vector_step, after(s_vector_step))
            nc.vector.tensor_scalar(sp8, sp8, 8.0, None, MUL).then_inc(s_vector_step, 1)
            dve.wait_ge(s_vector_step, after(s_vector_step))
            nc.vector.reciprocal(sc4, lball).then_inc(s_vector_step, 1)
            dve.wait_ge(s_vector_step, after(s_vector_step))
            nc.vector.tensor_tensor(lball, lball, sc4, MUL).then_inc(s_vector_step, 1)
            dve.wait_ge(s_vector_step, after(s_vector_step))
            nc.vector.tensor_tensor(lball, lball, lball, SUB).then_inc(s_vector_step, 1)
            dve.wait_ge(s_vector_step, after(s_vector_step))
            nc.vector.tensor_scalar(omlb, lball, -1.0, 1.0, MUL, ADD).then_inc(s_lb_ready, 1)
            dve.wait_ge(s_lb_ready, after(s_lb_ready))

            for j in range(2):
                dve.wait_ge(s_evac, 2 * (j + 1))
                x, y = slot(j), slot(4 + j)
                if j == 0:
                    dve.wait_ge(s_mod_done, 1)
                nc.vector.tensor_scalar(y, x, pc("conv_w", 6 + j), pc("conv_b", j), MUL, ADD).then_inc(s_vector_step, 1)
                dve.wait_ge(s_vector_step, after(s_vector_step))
                for lag in (1, 2, 3):
                    nc.vector.scalar_tensor_tensor(out=y[:, lag:], in0=x[:, :T - lag],
                                                   scalar=pc("conv_w", 2 * (3 - lag) + j), in1=y[:, lag:],
                                                   op0=MUL, op1=ADD)\
                        .then_inc(s_vector_step if lag < 3 else s_conv_ready, 1)
                    dve.wait_ge(s_vector_step if lag < 3 else s_conv_ready, after(s_vector_step if lag < 3 else s_conv_ready))
            for j in range(2):
                dve.wait_ge(s_gates_ready, 4 * j + 4)
                nc.vector.tensor_scalar(slot(j), slot(j), sp8[:, j:j + 1], None, MUL).then_inc(s_lru_y8_ready, 1)
                dve.wait_ge(s_lru_y8_ready, after(s_lru_y8_ready))
                nc.vector.tensor_tensor(slot(4 + j), slot(14 + j), slot(4 + j), MUL).then_inc(s_vector_step, 1)
                dve.wait_ge(s_vector_step, after(s_vector_step))
            for j in range(2):
                dve.wait_ge(s_lru_t, j + 1)
                nc.vector.tensor_scalar(slot(14 + j), slot(6 + j), 1.0, None, ADD).then_inc(s_vector_step, 1)
                dve.wait_ge(s_vector_step, after(s_vector_step))
                nc.vector.reciprocal(slot(14 + j), slot(14 + j)).then_inc(s_vector_step, 1)
                dve.wait_ge(s_vector_step, after(s_vector_step))
                nc.vector.tensor_tensor(slot(6 + j), slot(6 + j), slot(14 + j), MUL).then_inc(s_lru_q_ready, 1)
                dve.wait_ge(s_lru_q_ready, after(s_lru_q_ready))
            for j in range(2):
                dve.wait_ge(s_lru_mult, j + 1)
                nc.vector.memset(slot(6 + j)[:, 0:1], 1.0).then_inc(s_vector_step, 1)
                dve.wait_ge(s_vector_step, after(s_vector_step))
                nc.vector.tensor_tensor(slot(4 + j), slot(4 + j), slot(6 + j), MUL).then_inc(s_vector_step, 1)
                dve.wait_ge(s_vector_step, after(s_vector_step))
                dve.wait_ge(s_lru_a, j + 1)
                nc.vector.tensor_tensor_scan(slot(6 + j), slot(j), slot(4 + j), 0.0, MUL, ADD)\
                    .then_inc(s_vector_step, 1)
                dve.wait_ge(s_vector_step, after(s_vector_step))
                dve.wait_ge(s_evac, 2 * (BULK_AT[DG] + j + 1))
                nc.vector.tensor_tensor(slot(2 + j), slot(6 + j), slot(2 + j), MUL).then_inc(s_y_ready[3], 1)
                dve.wait_ge(s_y_ready[3], after(s_y_ready[3]))

            for q, s in enumerate((8, 9, 10, 11, 12, 13, 16)):
                dve.wait_ge(s_evac, 2 * (BULK_AT[AR] + q + 1))
                u, d = slot(s), slot(18 + q % 2)
                nc.vector.tensor_scalar(d[:, 0:1], u[:, 0:1], -1.0, None, MUL).then_inc(s_vector_step, 1)
                dve.wait_ge(s_vector_step, after(s_vector_step))
                nc.vector.tensor_tensor(d[:, 1:], u[:, :T - 1], u[:, 1:], SUB).then_inc(s_vector_step, 1)
                dve.wait_ge(s_vector_step, after(s_vector_step))
                nc.vector.scalar_tensor_tensor(out=u, in0=d, scalar=pc("mu", q), in1=u, op0=MUL, op1=ADD)\
                    .then_inc(s_a_mixed, 1)
                dve.wait_ge(s_a_mixed, after(s_a_mixed))
            for j in range(2):
                nc.vector.tensor_scalar(slot(4 + j), slot(10 + j), pc("kk", j), None, MUL).then_inc(s_a_kk_ready, 1)
                dve.wait_ge(s_a_kk_ready, after(s_a_kk_ready))
            for j in range(2):
                dve.wait_ge(s_gates_ready, 8 + 4 * (j + 1))
                a, k, ld = slot(14 + j), slot(10 + j), slot(j)
                nc.vector.tensor_scalar(slot(22 + j), a, 1.0, pc("ka", j), SUB, MUL).then_inc(s_vector_step, 1)
                dve.wait_ge(s_vector_step, after(s_vector_step))
                nc.vector.scalar_tensor_tensor(out=k, in0=slot(22 + j), scalar=1.0, in1=k, op0=ADD, op1=MUL)\
                    .then_inc(s_vector_step, 1)
                dve.wait_ge(s_vector_step, after(s_vector_step))
                nc.vector.tensor_scalar(ld, ld, float(-np.exp(-0.5)), None, MUL).then_inc(s_vector_step, 1)
                dve.wait_ge(s_vector_step, after(s_vector_step))
                dve.wait_ge(s_tables_landed, TAB_DMAS)
                nc.vector.tensor_tensor_scan(slot(22 + j), reset, ld, 0.0, MUL, ADD).then_inc(s_vector_step, 1)
                dve.wait_ge(s_vector_step, after(s_vector_step))
                nc.vector.tensor_copy(ld, slot(22 + j)).then_inc(s_a_b_ready, 1)
                dve.wait_ge(s_a_b_ready, after(s_a_b_ready))
            for j in range(2):
                dve.wait_ge(s_roots, 2 * j + 2)
                n, kk = slot(18 + j), slot(4 + j)
                nc.vector.tensor_scalar(n, n, 1e-12, None, MAX).then_inc(s_vector_step, 1)
                dve.wait_ge(s_vector_step, after(s_vector_step))
                nc.vector.reciprocal(n, n).then_inc(s_vector_step, 1)
                dve.wait_ge(s_vector_step, after(s_vector_step))
                nc.vector.scalar_tensor_tensor(out=kk, in0=kk, scalar=-1.0, in1=n, op0=MUL, op1=MUL)\
                    .then_inc(s_a_norms_used, 1)
                dve.wait_ge(s_a_norms_used, after(s_a_norms_used))

            dve.wait_ge(s_cos_landed, 16)
            dve.wait_ge(s_sin_landed, 16)
            for q in range(2):
                for n in range(2):
                    dve.wait_ge(s_rot_done, 2 * q + n + 1)
                    s = slot(20 + q)[:, halves(n)]
                    nc.vector.tensor_tensor(rope_tmp[n], bank[4 + 2 * q + n][:, :], slot(17)[:, halves(n)], MUL)\
                        .then_inc(s_vector_step, 1)
                    dve.wait_ge(s_vector_step, after(s_vector_step))
                    nc.vector.tensor_tensor(s, s, slot(16)[:, halves(n)], MUL).then_inc(s_vector_step, 1)
                    dve.wait_ge(s_vector_step, after(s_vector_step))
                    nc.vector.tensor_tensor(s, s, rope_tmp[n], ADD).then_inc(s_vector_step, 1)
                    dve.wait_ge(s_vector_step, after(s_vector_step))

            def by_chunk(ap):
                return ap.rearrange("p (i t) -> p i t", t=P)

            def over_chunks(name):
                return tb(name).unsqueeze(1).to_broadcast([P, NT, P])

            nc.vector.tensor_tensor(by_chunk(slot(17)), by_chunk(slot(21)), over_chunks("zeta"), MUL)\
                .then_inc(s_kz_ready, 1)
            dve.wait_ge(s_kz_ready, after(s_kz_ready))
            nc.vector.tensor_tensor(by_chunk(slot(16)), by_chunk(slot(20)), over_chunks("xi"), MUL)\
                .then_inc(s_vector_step, 1)
            dve.wait_ge(s_vector_step, after(s_vector_step))
            nc.vector.memset(ret_r, 0.0).then_inc(s_ret_r_ready, 1)
            dve.wait_ge(s_ret_r_ready, after(s_ret_r_ready))
            heads = tb("ret_head").unsqueeze(2)

            def ret_mask_q(i):
                q_all = slot(20)[:, i * P:(i + 1) * P].unsqueeze(1).to_broadcast([P, 4, P])
                if i >= 2:
                    dve.wait_ge(s_ret_s_done, i - 1)
                nc.vector.tensor_tensor(ret_q[i % 2], q_all, heads.to_broadcast([P, 4, P]), MUL)\
                    .then_inc(s_ret_q_ready, 1)
                dve.wait_ge(s_ret_q_ready, after(s_ret_q_ready))

            ret_mask_q(0)
            ret_mask_q(1)
            for i in range(NT):
                dve.wait_ge(s_ret_kv_done, i + 1)
                nc.vector.tensor_tensor(ret_kv.rearrange("p (h v) -> p h v", h=4),
                                        bank[4][:, 0:256].rearrange("p (h v) -> p h v", h=4),
                                        heads.to_broadcast([P, 4, C]), MUL).then_inc(s_vector_step, 1)
                dve.wait_ge(s_vector_step, after(s_vector_step))
                if i >= 2:
                    dve.wait_ge(s_ret_o_done, i - 1)
                dve.wait_ge(s_ret_s_done, i + 1)
                nc.vector.tensor_tensor(ret_p[i % 2].rearrange("p h t -> p (h t)"), bank[5 + i % 2][:, :],
                                        tb("decay"), MUL).then_inc(s_ret_p_ready, 1)
                dve.wait_ge(s_ret_p_ready, after(s_ret_p_ready))
                if i + 2 < NT:
                    ret_mask_q(i + 2)
                dve.wait_ge(s_ret_o_done, i + 1)
                nc.vector.scalar_tensor_tensor(out=ret_r, in0=ret_r, scalar=pc("gamma_c"), in1=ret_kv,
                                               op0=MUL, op1=ADD).then_inc(s_ret_r_ready, 1)
                dve.wait_ge(s_ret_r_ready, after(s_ret_r_ready))
                if i < 2:
                    nc.vector.scalar_tensor_tensor(out=slot(14 + i), in0=slot(4 + i), scalar=-1.0,
                                                   in1=slot(14 + i), op0=MUL, op1=MUL).then_inc(s_vector_step, 1)
                    dve.wait_ge(s_vector_step, after(s_vector_step))

            def normed(o, tmp, turn, gain, g, final):
                for j in range(2):
                    dve.wait_ge(s_roots, 4 * turn + 2 * j + 2)
                    nc.vector.reciprocal(slot(tmp + j), slot(tmp + j)).then_inc(s_vector_step, 1)
                    dve.wait_ge(s_vector_step, after(s_vector_step))
                    nc.vector.tensor_tensor(slot(o + j), slot(o + j), slot(tmp + j), MUL).then_inc(s_vector_step, 1)
                    dve.wait_ge(s_vector_step, after(s_vector_step))
                    nc.vector.scalar_tensor_tensor(out=slot(g + j), in0=slot(o + j), scalar=pc(gain, j),
                                                   in1=slot(g + j), op0=MUL, op1=MUL).then_inc(final, 1)
                    dve.wait_ge(final, after(final))

            nc.vector.memset(Ep[:, :, 0:1], 1.0).then_inc(s_a_starts_ready, 1)
            dve.wait_ge(s_a_starts_ready, after(s_a_starts_ready))

            state = {"merge": 0}

            def merge():
                mi = state["merge"]
                b, m = MERGE_TILES[mi]
                bi = BULK_AT[MG + 8 * b + m]
                for n in range(2):
                    dve.wait_ge(s_evac, 2 * bi + n + 1)
                    dve.wait_ge(s_br_done, 2 * mi + n + 1)
                    o = slot(MERGED + m)[:, halves(n)]
                    if mi == 4 and n == 0:
                        dve.wait_ge(s_y_ready[2], 2)
                    if mi < 8:
                        nc.vector.tensor_tensor(o, sig[n], bank[2 + n][:, :], MUL).then_inc(s_merged, 1)
                        dve.wait_ge(s_merged, after(s_merged))
                    else:
                        nc.vector.tensor_tensor(sig[n], sig[n], bank[2 + n][:, :], MUL).then_inc(s_vector_step, 1)
                        dve.wait_ge(s_vector_step, after(s_vector_step))
                        nc.vector.tensor_tensor(o, o, sig[n], ADD).then_inc(s_merged, 1)
                        dve.wait_ge(s_merged, after(s_merged))
                state["merge"] += 1

            nc.vector.memset(G, 0.0).then_inc(s_a_g_zero, 1)
            dve.wait_ge(s_a_g_zero, after(s_a_g_zero))
            def prep(i):
                tsl = slice(i * P, (i + 1) * P)

                def four(s):
                    return pair(s)[:, :, tsl].rearrange("p j (c t) -> p j c t", t=C)

                def jc(ap):
                    return ap.rearrange("p (j c) t -> p j c t", c=2)

                ar = a_r.rearrange("p (j c) a t -> p j c a t", c=2)
                ep = jc(Ep)
                dve.wait_ge(s_a_e_ready, 2 * i + 2)
                if i:
                    dve.wait_ge(s_a_gnew_done, 2 * i)
                nc.vector.tensor_tensor(ar[:, :, :, 0, :], four(4), ep[:, :, :, 0:64], MUL).then_inc(s_vector_step, 1)
                dve.wait_ge(s_vector_step, after(s_vector_step))
                nc.vector.tensor_tensor(ar[:, :, :, 1, :], four(8), ep[:, :, :, 1:65], MUL).then_inc(s_vector_step, 1)
                dve.wait_ge(s_vector_step, after(s_vector_step))
                nc.vector.tensor_tensor(jc(b_hat), four(14), jc(Em), MUL).then_inc(s_vector_step, 1)
                dve.wait_ge(s_vector_step, after(s_vector_step))
                nc.vector.tensor_tensor(jc(k_hat), four(10), jc(Em), MUL).then_inc(s_vector_step, 1)
                dve.wait_ge(s_vector_step, after(s_vector_step))
                e_end = Ep[:, :, 64:65].to_broadcast([P, 4, C])
                nc.vector.tensor_tensor(b_end, b_hat, e_end, MUL).then_inc(s_vector_step, 1)
                dve.wait_ge(s_vector_step, after(s_vector_step))
                nc.vector.tensor_tensor(k_end, k_hat, e_end, MUL).then_inc(s_a_ends_ready, 1)
                dve.wait_ge(s_a_ends_ready, after(s_a_ends_ready))

            prep(0)

            for i in range(NT):
                m_b = tb("m_rwkv").unsqueeze(1).to_broadcast([P, 4, P])
                for par in range(2):
                    dve.wait_ge(s_a_m_done, 2 * i + par + 1)
                    nc.vector.tensor_tensor(m_all[:, par].rearrange("p a j t -> p (a j) t"),
                                            bank[6 + par][:, :].rearrange("p (h t) -> p h t", h=4), m_b,
                                            MUL).then_inc(s_vector_step, 1)
                    dve.wait_ge(s_vector_step, after(s_vector_step))

                def heads_of(a, par):
                    return xx[:, a, :, :].rearrange("p (j o) t -> p j o t", o=2)[:, :, par, :]

                eye = tb("eye64").unsqueeze(1).to_broadcast([P, 4, C])
                for par in range(2):
                    nc.vector.tensor_tensor(heads_of(1, par), m_all[:, par, 0, :, 0:C],
                                            tb("up1").unsqueeze(1).to_broadcast([P, 2, C]), MUL)\
                        .then_inc(s_vector_step, 1)
                    dve.wait_ge(s_vector_step, after(s_vector_step))
                nc.vector.tensor_tensor(xx[:, 1, :, :], xx[:, 1, :, :], eye, ADD).then_inc(s_vector_step, 1)
                dve.wait_ge(s_vector_step, after(s_vector_step))

                def lev(l):
                    return tb("lev")[:, l * C:(l + 1) * C].unsqueeze(1).to_broadcast([P, 4, C])

                for par in range(2):
                    dve.wait_ge(s_a_a_done, 2 * i + par + 1)
                    nc.vector.tensor_tensor(heads_of(0, par),
                                            bank[4 + par][:, 0:128].rearrange("p (j t) -> p j t", j=2),
                                            tb("lev")[:, 0:C].unsqueeze(1).to_broadcast([P, 2, C]), MUL)\
                        .then_inc(s_vector_step, 1)
                    dve.wait_ge(s_vector_step, after(s_vector_step))
                nc.vector.tensor_tensor(xx[:, 0, :, :], xx[:, 0, :, :], eye, ADD).then_inc(s_a_x_ready, 1)
                dve.wait_ge(s_a_x_ready, after(s_a_x_ready))
                for l in range(1, 6):
                    dve.wait_ge(s_a_v_done, 5 * i + l)
                    nc.vector.tensor_tensor(v_lev, bank[5][:, 0:256].rearrange("p (h t) -> p h t", h=4), lev(l), MUL)\
                        .then_inc(s_a_v_ready, 1)
                    dve.wait_ge(s_a_v_ready, after(s_a_v_ready))
                    dve.wait_ge(s_a_dx_done, 5 * i + l)
                    xf = xx.rearrange("p a h t -> p (a h t)")
                    c0 = 0 if l < 5 else 256
                    nc.vector.tensor_tensor(xf[:, c0:512], xf[:, c0:512], bank[6][:, c0:512], ADD)\
                        .then_inc(s_a_x_ready, 1)
                    dve.wait_ge(s_a_x_ready, after(s_a_x_ready))
                    if i == 0 and l < 5:
                        j, n = (l - 1) // 2, (l - 1) % 2
                        dve.wait_ge(s_roots, 4 + l)
                        q = slot(16 + j)[:, halves(n)]
                        nc.vector.reciprocal(q, q).then_inc(s_ret_norm_ready, 1)
                        dve.wait_ge(s_ret_norm_ready, after(s_ret_norm_ready))
                merge()
                for c in range(2):
                    n = 2 * i + c
                    rc = slice(64 * c, 64 * c + 64)
                    dve.wait_ge(s_a_wg_done, n + 1)
                    u4 = u_sb.rearrange("p (j o v) -> p j o v", j=2, o=2)
                    dve.wait_ge(s_a_u_ready, i + 1)
                    for par in range(2):
                        nc.vector.tensor_tensor(u4[rc, :, par, :], u4[rc, :, par, :],
                                                bank[6 + par][rc, 0:128].rearrange("p (j v) -> p j v", j=2),
                                                ADD).then_inc(s_a_sa_ready, 1)
                        dve.wait_ge(s_a_sa_ready, after(s_a_sa_ready))
                    dve.wait_ge(s_a_y_done, 2 * n + 2)
                    dve.wait_ge(s_a_y_part, n + 1)
                    y = pair(4)[:, :, i * P + c * C:i * P + (c + 1) * C]
                    nc.vector.tensor_tensor(y, y, bank[6][:, 256:384].rearrange("p (j t) -> p j t", j=2), ADD)\
                        .then_inc(s_a_y_ready, 1)
                    dve.wait_ge(s_a_y_ready, after(s_a_y_ready))
                    dve.wait_ge(s_a_gnew_done, n + 1)
                    for j in range(2):
                        nc.vector.scalar_tensor_tensor(out=G[:, j * C:(j + 1) * C],
                                                       in0=G[:, j * C:(j + 1) * C],
                                                       scalar=Ep[:, 2 * j + c, 64:65],
                                                       in1=bank[5][:, j * C:(j + 1) * C], op0=MUL, op1=ADD)\
                            .then_inc(s_a_g_ready, 1)
                        dve.wait_ge(s_a_g_ready, after(s_a_g_ready))
                if i + 1 < NT:
                    prep(i + 1)
                merge()

            for j in range(2):
                dve.wait_ge(s_b_f_sig, j + 1)
                nc.vector.tensor_scalar(b_f[j], b_f[j], omlb[:, j:j + 1], lball[:, j:j + 1], MUL, ADD)\
                    .then_inc(s_vector_step, 1)
                dve.wait_ge(s_vector_step, after(s_vector_step))
                nc.vector.tensor_scalar(b_f[j], b_f[j], 1e-19, None, MAX).then_inc(s_b_f_ready, 1)
                dve.wait_ge(s_b_f_ready, after(s_b_f_ready))
            for j in range(2):
                for n in range(2):
                    dve.wait_ge(s_a_mean_done, 2 * j + n + 1)
                    y = slot(4 + j)[:, halves(n)]
                    nc.vector.scalar_tensor_tensor(out=y, in0=bank[4 + 2 * j + n][:, :], scalar=-1.0 / 64,
                                                   in1=y, op0=MUL, op1=ADD).then_inc(s_a_centred, 1)
                    dve.wait_ge(s_a_centred, after(s_a_centred))
            for j in range(2):
                nc.vector.scalar_tensor_tensor(out=slot(8 + j), in0=slot(8 + j), scalar=pc("rk", j),
                                               in1=slot(10 + j), op0=MUL, op1=MUL).then_inc(s_a_rk_ready, 1)
                dve.wait_ge(s_a_rk_ready, after(s_a_rk_ready))
            dve.wait_ge(s_reset128_landed, 16)
            for j in range(2):
                dve.wait_ge(s_b_lnf, j + 1)
                nc.vector.tensor_tensor_scan(slot(14 + j), b_reset, b_f[j], 0.0, MUL, ADD).then_inc(s_b_scanned, 1)
                dve.wait_ge(s_b_scanned, after(s_b_scanned))

            def exponents(i):
                b = pair(14)[:, :, i * P:(i + 1) * P]
                for li, hl in enumerate(LEVELS):
                    nb = 64 // hl
                    bb = b.rearrange("p j (n s) -> p j n s", s=2 * hl)
                    zz = dz[:, li, :, :].rearrange("p j (n s) -> p j n s", s=2 * hl)
                    mid = bb[:, :, :, hl - 1:hl].to_broadcast([P, 2, nb, hl])
                    nc.vector.tensor_tensor(zz[:, :, :, 0:hl], mid, bb[:, :, :, 0:hl], SUB).then_inc(s_vector_step, 1)
                    dve.wait_ge(s_vector_step, after(s_vector_step))
                    nc.vector.tensor_tensor(zz[:, :, :, hl:2 * hl], bb[:, :, :, hl:2 * hl], mid, SUB)\
                        .then_inc(s_vector_step, 1)
                    dve.wait_ge(s_vector_step, after(s_vector_step))
                nc.vector.tensor_copy(dz[:, 7, :, :], b).then_inc(s_vector_step, 1)
                dve.wait_ge(s_vector_step, after(s_vector_step))
                nc.vector.tensor_tensor(dz[:, 8, :, :], b[:, :, P - 1:P].to_broadcast([P, 2, P]), b, SUB)\
                    .then_inc(s_b_d_ready, 1)
                dve.wait_ge(s_b_d_ready, after(s_b_d_ready))

            exponents(0)
            for j in range(2):
                dve.wait_ge(s_roots, 8 + 2 * j + 2)
                y, q = slot(4 + j), slot(6 + j)
                nc.vector.reciprocal(q, q).then_inc(s_vector_step, 1)
                dve.wait_ge(s_vector_step, after(s_vector_step))
                nc.vector.tensor_tensor(y, y, q, MUL).then_inc(s_vector_step, 1)
                dve.wait_ge(s_vector_step, after(s_vector_step))
                nc.vector.tensor_scalar(y, y, pc("ln_g", j), pc("ln_b", j), MUL, ADD).then_inc(s_vector_step, 1)
                dve.wait_ge(s_vector_step, after(s_vector_step))
                for n in range(2):
                    dve.wait_ge(s_a_bonus_done, 2 * j + n + 1)
                    nc.vector.tensor_tensor(q[:, halves(n)], slot(12 + j)[:, halves(n)],
                                            bank[4 + 2 * j + n][:, :], MUL).then_inc(s_a_bonus_read, 1)
                    dve.wait_ge(s_a_bonus_read, after(s_a_bonus_read))
                nc.vector.tensor_tensor(y, y, q, ADD).then_inc(s_vector_step, 1)
                dve.wait_ge(s_vector_step, after(s_vector_step))
                dve.wait_ge(s_evac, 2 * (BULK_AT[AG] + j + 1))
                nc.vector.tensor_tensor(slot(2 + j), y, slot(2 + j), MUL).then_inc(s_y_ready[0], 1)
                dve.wait_ge(s_y_ready[0], after(s_y_ready[0]))
            for j in range(2):
                dve.wait_ge(s_b_k_sig, j + 1)
                nc.vector.tensor_scalar(slot(12 + j), slot(12 + j), omlb[:, j:j + 1], None, MUL)\
                    .then_inc(s_vector_step, 1)
                dve.wait_ge(s_vector_step, after(s_vector_step))
            nc.vector.memset(h_p, 0.0).then_inc(s_vector_step, 1)
            dve.wait_ge(s_vector_step, after(s_vector_step))
            nc.vector.memset(h_s, 0.0).then_inc(s_b_s_ready, 1)
            dve.wait_ge(s_b_s_ready, after(s_b_s_ready))
            def decayed(i):
                tsl = slice(i * P, (i + 1) * P)
                dve.wait_ge(s_b_e_ready, i + 1)

                q, k = pair(0)[:, :, tsl], pair(12)[:, :, tsl]
                for li, hl in enumerate(LEVELS):
                    zz = dz[:, li, :, :].rearrange("p j (n s) -> p j n s", s=2 * hl)
                    kk = k.rearrange("p j (n s) -> p j n s", s=2 * hl)
                    qq = q.rearrange("p j (n s) -> p j n s", s=2 * hl)
                    nc.vector.tensor_tensor(zz[:, :, :, 0:hl], zz[:, :, :, 0:hl], kk[:, :, :, 0:hl], MUL)\
                        .then_inc(s_vector_step, 1)
                    dve.wait_ge(s_vector_step, after(s_vector_step))
                    nc.vector.tensor_tensor(zz[:, :, :, hl:2 * hl], zz[:, :, :, hl:2 * hl],
                                            qq[:, :, :, hl:2 * hl], MUL).then_inc(s_vector_step, 1)
                    dve.wait_ge(s_vector_step, after(s_vector_step))
                nc.vector.tensor_copy(e_last, dz[:, 7, :, P - 1:P].rearrange("p j t -> p (j t)"))\
                    .then_inc(s_vector_step, 1)
                dve.wait_ge(s_vector_step, after(s_vector_step))
                nc.vector.tensor_tensor(h_qe, dz[:, 7, :, :], q, MUL).then_inc(s_vector_step, 1)
                dve.wait_ge(s_vector_step, after(s_vector_step))
                nc.vector.tensor_tensor(dz[:, 8, :, :], dz[:, 8, :, :], k, MUL).then_inc(s_b_z_ready, 1)
                dve.wait_ge(s_b_z_ready, after(s_b_z_ready))

            decayed(0)
            for i in range(NT):
                low = tb("low").rearrange("p (l t) -> p l t", l=NLOW)
                hd4 = h_diag.rearrange("p (j o) t -> p j o t", o=2)
                hp4 = h_p.rearrange("p (j o) t -> p j o t", o=2)
                for hh in range(2):
                    dve.wait_ge(s_b_scores_done, 2 * i + hh + 1)
                    for j in range(2):
                        nc.vector.tensor_tensor(h_prod[:, j],
                                                bank[4 + hh][:, j * 192:(j + 1) * 192].rearrange( "p (l t) -> p l t", l=NLOW),
                                                low, MUL).then_inc(s_vector_step, 1)
                        dve.wait_ge(s_vector_step, after(s_vector_step))
                    nc.vector.tensor_reduce(hd4[:, :, hh, :], h_prod.rearrange("p j l t -> p j t l"),
                                            mybir.AxisListType.X, ADD).then_inc(s_vector_step, 1)
                    dve.wait_ge(s_vector_step, after(s_vector_step))
                    nc.vector.tensor_copy(hp4[0:64, :, hh, 64:128],
                                          bank[4 + hh][0:64, 384:512].rearrange("p (j t) -> p j t", j=2))\
                        .then_inc(s_vector_step, 1)
                    dve.wait_ge(s_vector_step, after(s_vector_step))
                    dve.wait_ge(s_b_ke_ready, i + 1)
                    for nb in (0, 2):
                        r = slice(32 * nb, 32 * nb + 32)
                        nc.vector.tensor_copy(hp4[r, :, hh, 32 * nb + 32:32 * nb + 64],
                                              bank[6 + hh][r, 256:320].rearrange("p (j t) -> p j t", j=2))\
                            .then_inc(s_vector_step, 1)
                        dve.wait_ge(s_vector_step, after(s_vector_step))
                for nb in range(4):
                    r = slice(32 * nb, 32 * nb + 32)
                    nc.vector.tensor_copy(h_p[r, :, 32 * nb:32 * nb + 32], h_diag[r, :, :])\
                        .then_inc(s_vector_step if nb < 3 else s_b_p_ready, 1)
                    dve.wait_ge(s_vector_step if nb < 3 else s_b_p_ready, after(s_vector_step if nb < 3 else s_b_p_ready))
                if i + 1 < NT:
                    exponents(i + 1)
                dve.wait_ge(s_b_snew_done, i + 1)
                for j in range(2):
                    nc.vector.scalar_tensor_tensor(out=h_s[:, j * 64:(j + 1) * 64],
                                                   in0=h_s[:, j * 64:(j + 1) * 64],
                                                   scalar=e_last[:, j:j + 1],
                                                   in1=bank[6][:, 384 + j * 64:448 + j * 64], op0=MUL,
                                                   op1=ADD).then_inc(s_b_s_ready, 1)
                    dve.wait_ge(s_b_s_ready, after(s_b_s_ready))
                if i + 1 < NT:
                    decayed(i + 1)
                    merge()
            dve.wait_ge(s_b_o_ready, NT)
            for j in range(2):
                nc.vector.scalar_tensor_tensor(out=slot(10 + j), in0=slot(6 + j), scalar=pc("hgrn_g", j),
                                               in1=slot(10 + j), op0=MUL, op1=MUL).then_inc(s_vector_step, 1)
                dve.wait_ge(s_vector_step, after(s_vector_step))
            for n in range(2):
                for j in range(2):
                    dve.wait_ge(s_roots, 12 + 2 * n + j + 1)
                    q, y = slot(12 + j)[:, halves(n)], slot(10 + j)[:, halves(n)]
                    nc.vector.reciprocal(q, q).then_inc(s_vector_step, 1)
                    dve.wait_ge(s_vector_step, after(s_vector_step))
                    nc.vector.tensor_tensor(y, y, q, MUL).then_inc(s_y_ready[1], 1)
                    dve.wait_ge(s_y_ready[1], after(s_y_ready[1]))
            merge()
            nc.vector.memset(ones2, 1.0).then_inc(s_ones2_ready, 1)
            dve.wait_ge(s_ones2_ready, after(s_ones2_ready))
            for k in range(KT):
                if k >= 4:
                    merge()
                dve.wait_ge(s_w_mod_landed[k % 4], 32 + 16 * (k // 4 + 1))
                if k == 0:
                    nc.vector.tensor_scalar(slot(3), gate_w[0], cond[:, 0:1], None, MUL).then_inc(s_gate_acc, 1)
                    dve.wait_ge(s_gate_acc, after(s_gate_acc))
                else:
                    nc.vector.scalar_tensor_tensor(out=slot(3), in0=gate_w[k % 4],
                                                   scalar=cond[:, k:k + 1], in1=slot(3), op0=MUL, op1=ADD)\
                        .then_inc(s_gate_acc, 1)
                    dve.wait_ge(s_gate_acc, after(s_gate_acc))
            for _ in range(4):
                merge()
            dve.wait_ge(s_b_gate_landed, 16)
            for n in range(2):
                dve.wait_ge(s_gate_done, n + 1)
                nc.vector.tensor_tensor(slot(2)[:, halves(n)], slot(2)[:, halves(n)], bank[4 + n][:, :], ADD)\
                    .then_inc(s_gate_read, 1)
                dve.wait_ge(s_gate_read, after(s_gate_read))
            def split_merged(tt):
                dve.wait_ge(s_merged_hi_ready, tt + 1)
                tt_hi = merged_hi[tt % 2].rearrange("p (k t) -> p k t", t=P)
                nc.vector.tensor_tensor(merged_lo[tt % 2].rearrange("p (k t) -> p k t", t=P),
                                        slots[:, MERGED:MERGED + KT, tt * P:(tt + 1) * P],
                                        tt_hi.bitcast(F32), SUB).then_inc(s_merged_lo_ready, 1)
                dve.wait_ge(s_merged_lo_ready, after(s_merged_lo_ready))

            split_merged(0)
            split_merged(1)
            dve.wait_ge(s_final_g_landed, 16)
            for i in range(NT):
                dve.wait_ge(s_xr_landed[i % 4], 16 * (i // 4 + 1))
                for n in range(2):
                    dve.wait_ge(s_out_done, 2 * i + n + 1)
                    tmp = fin_tmp[:, halves(n)]
                    nc.vector.tensor_tensor(tmp, bank[(2 * i + n) % 8][:, :], slot(2)[:, halves(n)], MUL)\
                        .then_inc(s_out_read, 1)
                    dve.wait_ge(s_out_read, after(s_out_read))
                    nc.vector.tensor_tensor(xr[i % 4][:, halves(n)], xr[i % 4][:, halves(n)], tmp, ADD)\
                        .then_inc(s_h_ready, 1)
                    dve.wait_ge(s_h_ready, after(s_h_ready))
                if i + 2 < NT:
                    split_merged(i + 2)
                dve.wait_ge(s_h_rms, i + 1)
                nc.vector.reciprocal(rs2[:, i:i + 1], rs2[:, i:i + 1]).then_inc(s_vector_step, 1)
                dve.wait_ge(s_vector_step, after(s_vector_step))
                nc.vector.scalar_tensor_tensor(out=xr[i % 4], in0=xr[i % 4], scalar=rs2[:, i:i + 1],
                                               in1=final_g, op0=MUL, op1=MUL).then_inc(s_out_ready, 1)
                dve.wait_ge(s_out_ready, after(s_out_ready))


TAB_DMAS = 48


def shape_tables():
    f = np.float32
    p = np.arange(P)
    t = {}
    t["ident"] = np.eye(P)
    t["blockones"] = (p[:, None] // 64 == p[None, :] // 64)
    perm = np.zeros((P, P))
    for m in range(P):
        if m % 32 < 16:
            perm[m + 16, m] = -1
        else:
            perm[m - 16, m] = 1
    t["perm"] = perm
    lg = np.log1p(-np.exp2(-5.0 - np.arange(4)))
    head = p // 32
    i = np.arange(P)
    t["xi"] = np.exp(lg[head][:, None] * (i[None] + 1.0))
    t["zeta"] = np.exp(lg[head][:, None] * (P - 1 - i[None])) * RET_SCALE
    rel = i[None, :] - i[:, None]
    t["decay"] = np.concatenate([np.where(rel >= 0, np.exp(lg[h] * np.maximum(rel, 0)), 0) * RET_SCALE
                                 for h in range(4)], 1)
    ks, qs = p[:, None] % 32, np.arange(32)[None]
    low = [(ks // (2 * l) == qs // (2 * l)) & (ks % (2 * l) < l) & (qs % (2 * l) >= l) for l in LEVELS[2:]]
    t["low"] = np.concatenate(low + [ks == qs], 1)
    s, q = p[:, None] % 64, np.arange(64)[None]
    t["m_rwkv"] = np.concatenate([s < q, s <= q], 1)
    t["lev"] = np.concatenate([(s // (2 * l) == q // (2 * l)) & (s % (2 * l) >= l) & (q % (2 * l) < l)
                               for l in (1, 2, 4, 8, 16, 32)], 1)
    t["up1"] = (s // 2 == q // 2) & (s < q)
    t["eye64"] = s == q
    t["ret_head"] = head[:, None] == np.arange(4)[None]
    tables = np.concatenate([np.asarray(t[n], f) for n, _ in TABLES], 1)
    inv = (f(1.0) / (f(10000.0) ** np.linspace(0.0, 1.0, 16, dtype=f))).astype(f)
    ang = (inv[p % 32 % 16][:, None] * np.arange(T, dtype=f)[None]).astype(f)
    starts = {n: np.broadcast_to((np.arange(T) % n != 0).astype(f), (P, T)) for n in (64, 128)}
    return {"tables": tables, "cos": np.cos(ang).astype(f), "sin": np.sin(ang).astype(f),
            "reset64": starts[64], "reset128": starts[128], "gamma_c": np.exp(lg[head] * P).astype(f)[:, None]}


def kernel(**inputs):
    import concourse.bacc as _bacc
    from concourse.bass_utils import run_bass_kernel_spmd as _run

    a = {k: np.ascontiguousarray(v) for k, v in inputs.items()}
    consts = shape_tables()

    def cols(v):
        return v.reshape(-1, P).T

    fields = {
        "c": cols(a["c"]), "norm_g": cols(a["norm_g"]), "b_mod": cols(a["b_mod"][0, :2 * D]), "mu": cols(a["rwkv_mu"]),
        "w0": cols(a["rwkv_w0"]), "a0": cols(a["rwkv_a0"]), "kk": cols(a["rwkv_kk"]), "ka": cols(a["rwkv_ka"]),
        "rk": cols(a["rwkv_rk"]), "ln_g": cols(a["rwkv_ln_g"]), "ln_b": cols(a["rwkv_ln_b"]), "lb": cols(a["hgrn_lb"]),
        "hgrn_g": cols(a["hgrn_norm_g"]), "ret_g": cols(a["ret_norm_g"]), "conv_w": cols(a["lru_conv_w"]),
        "conv_b": cols(a["lru_conv_b"]), "ba": cols(a["lru_ba"]), "bx": cols(a["lru_bx"]), "lam": cols(a["lru_lam"]),
        "eps": np.full((P, 1), EPS, np.float32), "ln_eps": np.full((P, 1), RWKV_LN_EPS, np.float32),
        "gamma_c": consts["gamma_c"],
    }
    arrays = {
        "x": a["x"], "w_mod": a["w_mod"], "w_in": a["w_in"], "w_branch": a["w_branch"], "w_out": a["w_out"],
        "params": np.concatenate([fields[n] for n, _ in PARAMS], 1), "wa2": np.concatenate([a["rwkv_w2"][0], a["rwkv_a2"][0]], 0),
        "lru_wa": a["lru_wa"], "lru_wx": a["lru_wx"], "b_gate": a["b_mod"][0, 2 * D:], "final_g": a["final_g"],
        "tables": consts["tables"], "cos": consts["cos"], "sin": consts["sin"],
        "reset64": consts["reset64"], "reset128": consts["reset128"],
    }
    arrays = {f"in_{n}": np.ascontiguousarray(v) for n, v in arrays.items()}
    nc = _bacc.Bacc("TRN2", target_bir_lowering=False, num_devices=1)
    ins = {n[3:]: nc.dram_tensor(n, v.shape, F32, kind="ExternalInput").ap() for n, v in arrays.items()}
    out = nc.dram_tensor("out", (1, T, D), F32, kind="ExternalOutput").ap()
    build(nc, ins, out)
    r = _run(nc, [arrays], core_ids=[0])
    return r.results[0]["out"]
```
